# Optimizing a Trainium2 kernel written in Bass

```python
import jax, jax.numpy as jnp
from jax import lax
import numpy as np

D_MODEL = 1024
BATCH = 1
SEQ = 256
DEPTH = 2
DEC_BATCH = 8
DEC_SEQ = 4
PAST_LEN = 2048
PAGE_SIZE = 128

N_BRANCH = 4
BRANCH_WIDTH = D_MODEL // N_BRANCH
EPS = 1e-6

GLA_HEADS = 4
GLA_HEAD_K = BRANCH_WIDTH // GLA_HEADS // 2
GLA_HEAD_V = BRANCH_WIDTH // GLA_HEADS
GLA_GATE_RANK = 16
GLA_GATE_TAU = 16.0
GLA_CHUNK = 32

MLA_HEADS = 4
MLA_NOPE_DIM = 64
MLA_ROPE_DIM = 32
MLA_V_DIM = BRANCH_WIDTH // MLA_HEADS
MLA_Q_LORA = 256
MLA_KV_LORA = 128
ROPE_THETA = 10000.0
Q_BLOCK = 128

RWKV_HEADS = 4
RWKV_HEAD = BRANCH_WIDTH // RWKV_HEADS
RWKV_DECAY_LORA = 64
RWKV_A_LORA = 64
RWKV_GATE_LORA = 128
RWKV_LN_EPS = 64e-5

MLSTM_HEADS = 4
MLSTM_HEAD_QK = BRANCH_WIDTH // MLSTM_HEADS
MLSTM_HEAD_V = BRANCH_WIDTH // MLSTM_HEADS
MLSTM_CHUNK = 64

MEM_LEN = 256
CA_HEADS = 4
CA_HEAD_DIM = D_MODEL // CA_HEADS

D_FF = 2816
CONV_W = 3

GLA_SIZES = (GLA_HEADS * GLA_HEAD_K, GLA_HEADS * GLA_HEAD_K, GLA_HEADS * GLA_HEAD_V, GLA_GATE_RANK, GLA_HEADS * GLA_HEAD_V)
MLA_SIZES = (MLA_Q_LORA, MLA_KV_LORA, MLA_ROPE_DIM)
RWKV_SIZES = (BRANCH_WIDTH, BRANCH_WIDTH, BRANCH_WIDTH, RWKV_DECAY_LORA, RWKV_A_LORA, RWKV_GATE_LORA)
MLSTM_SIZES = (MLSTM_HEADS * MLSTM_HEAD_QK, MLSTM_HEADS * MLSTM_HEAD_QK, MLSTM_HEADS * MLSTM_HEAD_V, MLSTM_HEADS, MLSTM_HEADS, MLSTM_HEADS * MLSTM_HEAD_V)
RWKV_PROJ = sum(RWKV_SIZES)
PROJ_SIZES = (sum(GLA_SIZES), sum(MLA_SIZES), RWKV_PROJ, sum(MLSTM_SIZES), N_BRANCH * D_MODEL)
PROJ_TOTAL = sum(PROJ_SIZES)

kernel_name = 'hybrid_gated_branch_decoder_step'

def _rms_norm(x, g):
    xf = x.astype(jnp.float32)
    y = xf * lax.rsqrt(jnp.mean(xf * xf, axis=-1, keepdims=True) + EPS)
    return (y * g.astype(jnp.float32)).astype(x.dtype)

def _head_rms_norm(x, g):
    return x * lax.rsqrt(jnp.mean(x * x, axis=-1, keepdims=True) + EPS) * g

def _head_layer_norm(x, w, b, eps):
    xc = x - jnp.mean(x, axis=-1, keepdims=True)
    y = xc * lax.rsqrt(jnp.mean(xc * xc, axis=-1, keepdims=True) + eps) * w
    return y if b is None else y + b

def _split_cols(x, sizes):
    return jnp.split(x, np.cumsum(sizes)[:-1].tolist(), axis=-1)

def _heads(t, n):
    return t.reshape(t.shape[:-1] + (t.shape[-1] // n, n))

def _rope(x, pos):
    half = MLA_ROPE_DIM // 2
    inv_freq = ROPE_THETA ** (-jnp.arange(half, dtype=jnp.float32) / half)
    ang = pos[:, None] * inv_freq[None, :]
    shape = (1, x.shape[1]) + (1,) * (x.ndim - 3) + (half,)
    cos, sin = jnp.cos(ang).reshape(shape), jnp.sin(ang).reshape(shape)
    xf = x.astype(jnp.float32)
    x1, x2 = xf[..., :half], xf[..., half:]
    return jnp.concatenate([x1 * cos - x2 * sin, x1 * sin + x2 * cos], axis=-1).astype(x.dtype)

def _to_blocks(t, n, L):
    B, T, H, d = t.shape
    return t.reshape(B, n, L, H, d).transpose(1, 0, 3, 2, 4)

def _from_blocks(t):
    n, B, H, L, d = t.shape
    return t.transpose(1, 0, 3, 2, 4).reshape(B, n * L, H, d)

def _gla_chunked(q, k, v, log_a, s0):
    T = q.shape[1]
    L = GLA_CHUNK if T % GLA_CHUNK == 0 else T
    n = T // L
    causal = jnp.tril(jnp.ones((L, L), dtype=bool))

    def step(S, blk):
        qb, kb, vb, gb = blk
        b = jnp.cumsum(gb, axis=-2)
        q_dec = qb * jnp.exp(b)
        k_inv = kb * jnp.exp(-b)
        k_end = kb * jnp.exp(b[:, :, -1:, :] - b)
        att = jnp.where(causal, jnp.einsum('bhlk,bhsk->bhls', q_dec, k_inv), 0.0)
        out = jnp.einsum('bhlk,bhkv->bhlv', q_dec, S) + jnp.einsum('bhls,bhsv->bhlv', att, vb)
        S = S * jnp.exp(b[:, :, -1, :])[..., None] + jnp.einsum('bhlk,bhlv->bhkv', k_end, vb)
        return S, out

    S, out = lax.scan(step, s0, tuple(_to_blocks(t, n, L) for t in (q, k, v, log_a)))
    return _from_blocks(out), S

def _mlstm_chunked(q, k, v, i_pre, log_f, c0, n0, m0):
    B, T, H, _ = q.shape
    L = MLSTM_CHUNK if T % MLSTM_CHUNK == 0 else T
    n = T // L
    causal = jnp.tril(jnp.ones((L, L), dtype=bool))
    gate_blocks = lambda g: g.reshape(B, n, L, H).transpose(1, 0, 3, 2)

    def step(carry, blk):
        C, nv, m = carry
        qb, kb, vb, ib, fb = blk
        b = jnp.cumsum(fb, axis=-1)
        d = jnp.where(causal, b[..., :, None] - b[..., None, :] + ib[..., None, :], -jnp.inf)
        inter = b + m[..., None]
        m_t = jnp.maximum(inter, jnp.max(d, axis=-1))
        w_inter = jnp.exp(inter - m_t)
        w_intra = jnp.exp(d - m_t[..., None]) * jnp.einsum('bhlk,bhsk->bhls', qb, kb)
        num = w_inter[..., None] * jnp.einsum('bhlk,bhkv->bhlv', qb, C) + jnp.einsum('bhls,bhsv->bhlv', w_intra, vb)
        den = w_inter * jnp.einsum('bhlk,bhk->bhl', qb, nv) + jnp.sum(w_intra, axis=-1)
        h = num / jnp.maximum(jnp.abs(den), jnp.exp(-m_t))[..., None]
        m_new = m_t[..., -1]
        scale_old = jnp.exp(b[..., -1] + m - m_new)
        w_end = jnp.exp(b[..., -1:] - b + ib - m_new[..., None])
        C = scale_old[..., None, None] * C + jnp.einsum('bhl,bhlk,bhlv->bhkv', w_end, kb, vb)
        nv = scale_old[..., None] * nv + jnp.einsum('bhl,bhlk->bhk', w_end, kb)
        return (C, nv, m_new), h

    blks = (_to_blocks(q, n, L), _to_blocks(k, n, L), _to_blocks(v, n, L), gate_blocks(i_pre), gate_blocks(log_f))
    (C, nv, m), h = lax.scan(step, (c0, n0, m0), blks)
    return _from_blocks(h), C, nv, m

def _rwkv7_scan(r, decay, k, v, kk, a, s0):
    def step(S, inp):
        r_t, w_t, k_t, v_t, kk_t, a_t = inp
        S = (S * w_t[:, :, None, :]
             - jnp.einsum('bhvk,bhk->bhv', S, kk_t)[..., None] * (kk_t * a_t)[:, :, None, :]
             + v_t[..., None] * k_t[:, :, None, :])
        return S, jnp.einsum('bhvk,bhk->bhv', S, r_t)

    S, y = lax.scan(step, s0, tuple(jnp.swapaxes(t, 0, 1) for t in (r, decay, k, v, kk, a)))
    return jnp.swapaxes(y, 0, 1), S

def _latent_attend(q_lat, q_pe, key_sets):
    scale = (MLA_NOPE_DIM + MLA_ROPE_DIM) ** -0.5
    scores = []
    for ckv, kpe, mask in key_sets:
        s = (jnp.einsum('bthc,bsc->bhts', q_lat, ckv) + jnp.einsum('bthr,bsr->bhts', q_pe, kpe)).astype(jnp.float32) * scale
        if mask is not None:
            s = jnp.where(mask, s, -jnp.inf)
        scores.append(s)
    probs = jax.nn.softmax(jnp.concatenate(scores, axis=-1), axis=-1)
    out, start = None, 0
    for ckv, _, _ in key_sets:
        stop = start + ckv.shape[1]
        part = jnp.einsum('bhts,bsc->bthc', probs[..., start:stop].astype(ckv.dtype), ckv)
        out = part if out is None else out + part
        start = stop
    return out

def _mla_prompt(q_lat, q_pe, ckv, kpe):
    T = q_lat.shape[1]
    outs = []
    for start in range(0, T, Q_BLOCK):
        stop = min(start + Q_BLOCK, T)
        mask = jnp.arange(stop)[None, :] <= jnp.arange(start, stop)[:, None]
        outs.append(_latent_attend(q_lat[:, start:stop], q_pe[:, start:stop], ((ckv[:, :stop], kpe[:, :stop], mask),)))
    return jnp.concatenate(outs, axis=1)

def _layer(x, lp, st, pos0, mla_past, mem_k, mem_v):
    bsz, T, _ = x.shape
    dt = x.dtype
    f32 = jnp.float32
    gla_s, rwkv_s, shift_s, mc_s, mn_s, mm_s, conv_s = st
    pos = pos0 + jnp.arange(T, dtype=f32)

    h = _rms_norm(x, lp['norm_pre_mix'])
    proj = h @ lp['w_in']
    p_gla, p_mla, p_rwkv, p_mlstm, p_gate = _split_cols(proj, PROJ_SIZES)

    gq, gk, gv, glo, gr = _split_cols(p_gla.astype(f32), GLA_SIZES)
    log_a = jax.nn.log_sigmoid(glo @ lp['gla_w_gate2'] + lp['gla_b_gate']) / GLA_GATE_TAU
    o_gla, gla_new = _gla_chunked(_heads(gq, GLA_HEAD_K) * GLA_HEAD_K ** -0.5, _heads(gk, GLA_HEAD_K),
                                  _heads(gv, GLA_HEAD_V), _heads(log_a, GLA_HEAD_K), gla_s.astype(f32))
    o_gla = (_head_rms_norm(o_gla, lp['gla_norm']) * jax.nn.silu(_heads(gr, GLA_HEAD_V))).reshape(bsz, T, BRANCH_WIDTH)

    cq, ckv_raw, kr = _split_cols(p_mla, MLA_SIZES)
    q = (_rms_norm(cq, lp['mla_norm_q']) @ lp['mla_w_uq']).reshape(bsz, T, MLA_HEADS, MLA_NOPE_DIM + MLA_ROPE_DIM)
    q_pe = _rope(q[..., MLA_NOPE_DIM:], pos)
    q_lat = jnp.einsum('bthd,hcd->bthc', q[..., :MLA_NOPE_DIM], lp['mla_w_uk'])
    ckv = _rms_norm(ckv_raw, lp['mla_norm_kv'])
    kpe = _rope(kr, pos)
    if mla_past is None:
        o_lat = _mla_prompt(q_lat, q_pe, ckv, kpe)
    else:
        causal = jnp.tril(jnp.ones((T, T), dtype=bool))
        o_lat = _latent_attend(q_lat, q_pe, ((mla_past[0], mla_past[1], None), (ckv, kpe, causal)))
    o_mla = jnp.einsum('bthc,hcd->bthd', o_lat, lp['mla_w_uv']).reshape(bsz, T, BRANCH_WIDTH)

    shifted = jnp.concatenate([shift_s[:, None, :].astype(dt), p_rwkv[:, :-1]], axis=1)
    pm = (p_rwkv + (shifted - p_rwkv) * lp['rwkv_mu']).astype(f32)
    rr, rk, rv, wlo, alo, rglo = _split_cols(pm, RWKV_SIZES)
    decay = jnp.exp(-jnp.exp(-jax.nn.softplus(-(lp['rwkv_w0'] + jnp.tanh(wlo) @ lp['rwkv_w2'])) - 0.5))
    a = jax.nn.sigmoid(lp['rwkv_a0'] + alo @ lp['rwkv_a2'])
    g = jax.nn.sigmoid(rglo) @ lp['rwkv_g2']
    kk = _heads(rk * lp['rwkv_k_k'], RWKV_HEAD)
    kk = kk / jnp.maximum(jnp.sqrt(jnp.sum(kk * kk, axis=-1, keepdims=True)), 1e-12)
    rk = rk * (1.0 + (a - 1.0) * lp['rwkv_k_a'])
    r_h, k_h, v_h = _heads(rr, RWKV_HEAD), _heads(rk, RWKV_HEAD), _heads(rv, RWKV_HEAD)
    y, rwkv_new = _rwkv7_scan(r_h, _heads(decay, RWKV_HEAD), k_h, v_h, kk, _heads(a, RWKV_HEAD), rwkv_s.astype(f32))
    y = _head_layer_norm(y, _heads(lp['rwkv_ln_w'], RWKV_HEAD), _heads(lp['rwkv_ln_b'], RWKV_HEAD), RWKV_LN_EPS)
    y = y + jnp.sum(r_h * k_h * lp['rwkv_r_k'], axis=-1, keepdims=True) * v_h
    o_rwkv = y.reshape(bsz, T, BRANCH_WIDTH) * g
    shift_new = p_rwkv[:, -1]

    mlq, mlk, mlv, mli, mlf, mlo = _split_cols(p_mlstm.astype(f32), MLSTM_SIZES)
    h_m, mc_new, mn_new, mm_new = _mlstm_chunked(
        _heads(mlq, MLSTM_HEAD_QK) * MLSTM_HEAD_QK ** -0.5, _heads(mlk, MLSTM_HEAD_QK), _heads(mlv, MLSTM_HEAD_V),
        mli + lp['mlstm_i_bias'], jax.nn.log_sigmoid(mlf + lp['mlstm_f_bias']),
        mc_s.astype(f32), mn_s.astype(f32), mm_s.astype(f32))
    h_m = _head_layer_norm(h_m, _heads(lp['mlstm_norm'], MLSTM_HEAD_V), None, EPS)
    o_mlstm = h_m.reshape(bsz, T, BRANCH_WIDTH) * jax.nn.sigmoid(mlo)

    branches = jnp.stack([o_gla, o_mla.astype(f32), o_rwkv, o_mlstm], axis=2).astype(dt)
    up = jnp.einsum('btnc,ncd->btnd', branches, lp['w_branch'])
    gates = jax.nn.sigmoid(p_gate.reshape(bsz, T, N_BRANCH, D_MODEL))
    mixed = jnp.sum(gates * up, axis=2) @ lp['w_out']
    x = x + _rms_norm(mixed, lp['norm_post_mix'])

    h = _rms_norm(x, lp['norm_pre_ca'])
    qc = (h @ lp['ca_w_q']).reshape(bsz, T, CA_HEADS, CA_HEAD_DIM)
    s = jnp.einsum('bthd,bshd->bhts', qc, mem_k).astype(f32) * CA_HEAD_DIM ** -0.5
    pa = jax.nn.softmax(s, axis=-1).astype(mem_v.dtype)
    ca = jnp.einsum('bhts,bshd->bthd', pa, mem_v).reshape(bsz, T, D_MODEL) @ lp['ca_w_o']
    x = x + _rms_norm(ca, lp['norm_post_ca'])

    h = _rms_norm(x, lp['norm_pre_ffn'])
    a_up, g_up = jnp.split(h @ lp['ffn_w_up'], 2, axis=-1)
    a_full = jnp.concatenate([conv_s.astype(a_up.dtype), a_up], axis=1)
    conv = lp['ffn_conv_b'] + a_full[:, 0:T] * lp['ffn_conv_w'][0]
    for j in range(1, CONV_W):
        conv = conv + a_full[:, j:j + T] * lp['ffn_conv_w'][j]
    f = (jax.nn.gelu(conv, approximate=False) * g_up) @ lp['ffn_w_down']
    x = x + _rms_norm(f, lp['norm_post_ffn'])
    conv_new = a_full[:, T:]

    new_state = (ckv.astype(dt), kpe.astype(dt), gla_new.astype(dt), rwkv_new.astype(dt), shift_new.astype(dt),
                 mc_new.astype(dt), mn_new.astype(dt), mm_new.astype(dt), conv_new.astype(dt))
    return x, new_state

def _stack_field(per_layer, i):
    return jnp.stack([st[i] for st in per_layer], axis=0)

def setup_inputs(seed: int = 0) -> dict:
    key = jax.random.key(seed)
    ks = iter(jax.random.split(key, 64))
    f32 = jnp.float32

    def nrm(shape, scale=1.0):
        return scale * jax.random.normal(next(ks), shape, f32)

    def gain(shape):
        return 1.0 + 0.02 * jax.random.normal(next(ks), shape, f32)

    L, D, BW = DEPTH, D_MODEL, BRANCH_WIDTH
    n_pages = PAST_LEN // PAGE_SIZE
    n_used = DEC_BATCH * n_pages
    n_pool = n_used + n_used // 4
    x_prompt = nrm((BATCH, SEQ, D))
    x_sample = nrm((DEC_BATCH, DEC_SEQ, D))
    mem_prompt = nrm((BATCH, MEM_LEN, D))
    cache_ckv = nrm((L, n_pool, PAGE_SIZE, MLA_KV_LORA))
    cache_kpe = nrm((L, n_pool, PAGE_SIZE, MLA_ROPE_DIM))
    page_table = jax.random.permutation(next(ks), n_pool)[:n_used].reshape(DEC_BATCH, n_pages).astype(jnp.int32)
    return {
        'x_prompt': x_prompt,
        'x_sample': x_sample,
        'mem_prompt': mem_prompt,
        'cache_ckv': cache_ckv,
        'cache_kpe': cache_kpe,
        'page_table': page_table,
        'cache_mem_k': nrm((L, DEC_BATCH, MEM_LEN, CA_HEADS, CA_HEAD_DIM)),
        'cache_mem_v': nrm((L, DEC_BATCH, MEM_LEN, CA_HEADS, CA_HEAD_DIM)),
        'state_gla': nrm((L, DEC_BATCH, GLA_HEADS, GLA_HEAD_K, GLA_HEAD_V), 0.3),
        'state_rwkv': nrm((L, DEC_BATCH, RWKV_HEADS, RWKV_HEAD, RWKV_HEAD), 0.3),
        'state_rwkv_shift': nrm((L, DEC_BATCH, RWKV_PROJ)),
        'state_mlstm_c': nrm((L, DEC_BATCH, MLSTM_HEADS, MLSTM_HEAD_QK, MLSTM_HEAD_V), 0.3),
        'state_mlstm_n': nrm((L, DEC_BATCH, MLSTM_HEADS, MLSTM_HEAD_QK), 0.3),
        'state_mlstm_m': nrm((L, DEC_BATCH, MLSTM_HEADS)),
        'state_conv': nrm((L, DEC_BATCH, CONV_W - 1, D_FF)),
        'norm_pre_mix': gain((L, D)),
        'norm_post_mix': gain((L, D)),
        'norm_pre_ca': gain((L, D)),
        'norm_post_ca': gain((L, D)),
        'norm_pre_ffn': gain((L, D)),
        'norm_post_ffn': gain((L, D)),
        'w_in': nrm((L, D, PROJ_TOTAL), D ** -0.5),
        'gla_w_gate2': nrm((L, GLA_GATE_RANK, GLA_HEADS * GLA_HEAD_K), GLA_GATE_RANK ** -0.5),
        'gla_b_gate': nrm((L, GLA_HEADS * GLA_HEAD_K), 0.1),
        'gla_norm': gain((L, GLA_HEAD_V)),
        'mla_norm_q': gain((L, MLA_Q_LORA)),
        'mla_norm_kv': gain((L, MLA_KV_LORA)),
        'mla_w_uq': nrm((L, MLA_Q_LORA, MLA_HEADS * (MLA_NOPE_DIM + MLA_ROPE_DIM)), MLA_Q_LORA ** -0.5),
        'mla_w_uk': nrm((L, MLA_HEADS, MLA_KV_LORA, MLA_NOPE_DIM), MLA_KV_LORA ** -0.5),
        'mla_w_uv': nrm((L, MLA_HEADS, MLA_KV_LORA, MLA_V_DIM), MLA_KV_LORA ** -0.5),
        'rwkv_mu': jax.random.uniform(next(ks), (L, RWKV_PROJ), f32),
        'rwkv_w0': nrm((L, BW), 2.0) - 2.0,
        'rwkv_w2': nrm((L, RWKV_DECAY_LORA, BW), 0.1),
        'rwkv_a0': nrm((L, BW), 0.5),
        'rwkv_a2': nrm((L, RWKV_A_LORA, BW), 0.5 * RWKV_A_LORA ** -0.5),
        'rwkv_g2': nrm((L, RWKV_GATE_LORA, BW), RWKV_GATE_LORA ** -0.5),
        'rwkv_k_k': 0.85 + nrm((L, BW), 0.05),
        'rwkv_k_a': 1.0 + nrm((L, BW), 0.05),
        'rwkv_r_k': nrm((L, RWKV_HEADS, RWKV_HEAD), 0.1),
        'rwkv_ln_w': gain((L, BW)),
        'rwkv_ln_b': nrm((L, BW), 0.01),
        'mlstm_i_bias': nrm((L, MLSTM_HEADS), 0.1),
        'mlstm_f_bias': 4.0 + nrm((L, MLSTM_HEADS), 0.5),
        'mlstm_norm': gain((L, MLSTM_HEADS * MLSTM_HEAD_V)),
        'w_branch': nrm((L, N_BRANCH, BW, D), BW ** -0.5),
        'w_out': nrm((L, D, D), D ** -0.5),
        'ca_norm_mem': gain((L, D)),
        'ca_w_q': nrm((L, D, D), D ** -0.5),
        'ca_w_k': nrm((L, D, D), D ** -0.5),
        'ca_w_v': nrm((L, D, D), D ** -0.5),
        'ca_w_o': nrm((L, D, D), D ** -0.5),
        'ffn_w_up': nrm((L, D, 2 * D_FF), D ** -0.5),
        'ffn_conv_w': nrm((L, CONV_W, D_FF), CONV_W ** -0.5),
        'ffn_conv_b': nrm((L, D_FF), 0.02),
        'ffn_w_down': nrm((L, D_FF, D), D_FF ** -0.5),
    }

def reference(x_prompt, x_sample, mem_prompt, cache_ckv, cache_kpe, page_table, cache_mem_k, cache_mem_v,
              state_gla, state_rwkv, state_rwkv_shift, state_mlstm_c, state_mlstm_n, state_mlstm_m, state_conv,
              norm_pre_mix, norm_post_mix, norm_pre_ca, norm_post_ca, norm_pre_ffn, norm_post_ffn,
              w_in, gla_w_gate2, gla_b_gate, gla_norm,
              mla_norm_q, mla_norm_kv, mla_w_uq, mla_w_uk, mla_w_uv,
              rwkv_mu, rwkv_w0, rwkv_w2, rwkv_a0, rwkv_a2, rwkv_g2, rwkv_k_k, rwkv_k_a, rwkv_r_k, rwkv_ln_w, rwkv_ln_b,
              mlstm_i_bias, mlstm_f_bias, mlstm_norm,
              w_branch, w_out,
              ca_norm_mem, ca_w_q, ca_w_k, ca_w_v, ca_w_o,
              ffn_w_up, ffn_conv_w, ffn_conv_b, ffn_w_down):
    dt = x_prompt.dtype
    b_p = x_prompt.shape[0]
    b_s = x_sample.shape[0]
    past_len = page_table.shape[1] * cache_ckv.shape[2]

    st_p = (jnp.zeros((b_p, GLA_HEADS, GLA_HEAD_K, GLA_HEAD_V), dt),
            jnp.zeros((b_p, RWKV_HEADS, RWKV_HEAD, RWKV_HEAD), dt),
            jnp.zeros((b_p, RWKV_PROJ), dt),
            jnp.zeros((b_p, MLSTM_HEADS, MLSTM_HEAD_QK, MLSTM_HEAD_V), dt),
            jnp.zeros((b_p, MLSTM_HEADS, MLSTM_HEAD_QK), dt),
            jnp.zeros((b_p, MLSTM_HEADS), dt),
            jnp.zeros((b_p, CONV_W - 1, D_FF), dt))

    xp, xs = x_prompt, x_sample
    new_p, new_s, mem_k_new, mem_v_new = [], [], [], []
    for l in range(DEPTH):
        lp = {
            'norm_pre_mix': norm_pre_mix[l], 'norm_post_mix': norm_post_mix[l],
            'norm_pre_ca': norm_pre_ca[l], 'norm_post_ca': norm_post_ca[l],
            'norm_pre_ffn': norm_pre_ffn[l], 'norm_post_ffn': norm_post_ffn[l],
            'w_in': w_in[l], 'gla_w_gate2': gla_w_gate2[l], 'gla_b_gate': gla_b_gate[l], 'gla_norm': gla_norm[l],
            'mla_norm_q': mla_norm_q[l], 'mla_norm_kv': mla_norm_kv[l], 'mla_w_uq': mla_w_uq[l],
            'mla_w_uk': mla_w_uk[l], 'mla_w_uv': mla_w_uv[l],
            'rwkv_mu': rwkv_mu[l], 'rwkv_w0': rwkv_w0[l], 'rwkv_w2': rwkv_w2[l], 'rwkv_a0': rwkv_a0[l],
            'rwkv_a2': rwkv_a2[l], 'rwkv_g2': rwkv_g2[l], 'rwkv_k_k': rwkv_k_k[l], 'rwkv_k_a': rwkv_k_a[l],
            'rwkv_r_k': rwkv_r_k[l], 'rwkv_ln_w': rwkv_ln_w[l], 'rwkv_ln_b': rwkv_ln_b[l],
            'mlstm_i_bias': mlstm_i_bias[l], 'mlstm_f_bias': mlstm_f_bias[l], 'mlstm_norm': mlstm_norm[l],
            'w_branch': w_branch[l], 'w_out': w_out[l], 'ca_w_q': ca_w_q[l], 'ca_w_o': ca_w_o[l],
            'ffn_w_up': ffn_w_up[l], 'ffn_conv_w': ffn_conv_w[l], 'ffn_conv_b': ffn_conv_b[l],
            'ffn_w_down': ffn_w_down[l],
        }
        mem_n = _rms_norm(mem_prompt, ca_norm_mem[l])
        mk = (mem_n @ ca_w_k[l]).reshape(b_p, -1, CA_HEADS, CA_HEAD_DIM)
        mv = (mem_n @ ca_w_v[l]).reshape(b_p, -1, CA_HEADS, CA_HEAD_DIM)
        xp, st_new_p = _layer(xp, lp, st_p, 0.0, None, mk, mv)
        new_p.append(st_new_p)
        mem_k_new.append(mk)
        mem_v_new.append(mv)

        ckv_past = cache_ckv[l][page_table].reshape(b_s, past_len, MLA_KV_LORA)
        kpe_past = cache_kpe[l][page_table].reshape(b_s, past_len, MLA_ROPE_DIM)
        st_s = (state_gla[l], state_rwkv[l], state_rwkv_shift[l], state_mlstm_c[l], state_mlstm_n[l],
                state_mlstm_m[l], state_conv[l])
        xs, st_new_s = _layer(xs, lp, st_s, float(past_len), (ckv_past, kpe_past), cache_mem_k[l], cache_mem_v[l])
        new_s.append(st_new_s)

    return (xp, xs,
            _stack_field(new_p, 0), _stack_field(new_p, 1), _stack_field(new_s, 0), _stack_field(new_s, 1),
            jnp.stack(mem_k_new, axis=0), jnp.stack(mem_v_new, axis=0),
            _stack_field(new_p, 2), _stack_field(new_s, 2),
            _stack_field(new_p, 3), _stack_field(new_s, 3),
            _stack_field(new_p, 4), _stack_field(new_s, 4),
            _stack_field(new_p, 5), _stack_field(new_s, 5),
            _stack_field(new_p, 6), _stack_field(new_s, 6),
            _stack_field(new_p, 7), _stack_field(new_s, 7),
            _stack_field(new_p, 8), _stack_field(new_s, 8))


_drawn_inputs = setup_inputs


def setup_inputs(seed=0):
    import zlib

    import numpy as np

    out = dict(_drawn_inputs(seed))
    spreads = {}
    factors = {'norm_pre_ca': 3.06,
     'norm_post_ca': 2.838,
     'norm_post_ffn': 3.506,
     'gla_norm': 3.853,
     'mla_norm_q': 8.0,
     'mla_norm_kv': 3.002,
     'rwkv_ln_w': 4.131,
     'rwkv_ln_b': 7.071,
     'mlstm_norm': 4.409,
     'ffn_conv_b': 3.496}
    for name, (base, spread) in spreads.items():
        noise = np.random.default_rng([zlib.crc32(name.encode()), seed]).standard_normal(out[name].shape)
        drawn = base * np.exp(spread * noise) if base else spread * noise
        out[name] = __import__('jax').numpy.asarray(drawn.astype(out[name].dtype))
    for name, factor in factors.items():
        out[name] = (out[name] * factor).astype(out[name].dtype)
    return out
```

```python
from contextlib import ExitStack

import numpy as np

import concourse.bass as bass
from concourse import mybir

F32 = mybir.dt.float32
I32 = mybir.dt.int32
ALU = mybir.AluOpType
ACT = mybir.ActivationFunctionType
AX = mybir.AxisListType

P = 128
D = 1024
KD = D // P
L = 2
TP, NB, TS = 256, 8, 4
NS = NB * TS
N = TP + NS
PAGES, PAGE = 16, 128
POOL = NB * PAGES * 5 // 4
KEYS = PAGES * PAGE
FF = 2816
KF = FF // P
MEM = 256
CH = 64
NCH = TP // CH
TT = [(0, 128), (128, 128), (256, NS)]
EXT = 1 + TP + NB * (1 + TS)
EXC = 2 + TP + NB * (2 + TS)
NEG = -1e30
DECAY = float(np.exp(-0.5))
SCALE_MLA = 96.0 ** -0.5
SCALE_CA = 256.0 ** -0.5

GQ, GK, GR, CQ, CKV, MIX1, MIX2, MQ, MK, MO, RW = 0, 1, 2, 4, 6, 7, 8, 9, 11, 13, 15
NF = 23
I_AT, GLO_AT, KR_AT, KRS_AT = 0, 32, 64, 96

_v, VEC = 0, {}
for _name, _n in (("pre_mix", 8), ("post_mix", 8), ("pre_ca", 8), ("post_ca", 8), ("pre_ffn", 8), ("post_ffn", 8),
                  ("mem", 8), ("mu", 8), ("w0", 2), ("a0", 2), ("k_k", 2), ("k_a", 2), ("r_k", 2), ("ln_w", 2),
                  ("ln_b", 2), ("ml_norm", 2), ("gla_norm", 1), ("gla_b", 1), ("norm_q", 2), ("norm_kv", 1),
                  ("conv_w", 3 * KF), ("conv_b", KF), ("i_bias", 1), ("f_bias", 1)):
    VEC[_name] = _v
    _v += _n
NVEC = _v
_v, MAT = 0, {}
for _name, _n in (("gate2", 128), ("uq", 2 * 512), ("uk", 2 * 128), ("uv", 4 * 64), ("wa", 256), ("g2", 256)):
    MAT[_name] = _v
    _v += _n
NMAT = _v
_v, CON = 0, {}
for _name, _n in (("ident", 128), ("ones", 128), ("blk64", 128), ("upper", 128), ("strict", 128), ("upper_s", NS),
                  ("strict_s", NS), ("level", 6 * 128), ("level0", 128), ("bias_tok", 128), ("bias_m", 416),
                  ("bias_own", NB * NS), ("sel_h", 4 * 128), ("sel_p", 2 * 128), ("batch", NB), ("cos", N), ("sin", N),
                  ("reset", N), ("reset_m", N), ("eps", 1), ("eps_r", 1), ("one", 1), ("kk_b", 1)):
    CON[_name] = _v
    _v += _n
NCON = _v

SLOT = 16
RING = 5
GEMM_BANKS = 4


def plan():
    tiles, at = [], 0

    def add(stage, index, n, reader, hold=False):
        nonlocal at
        tiles.append((stage, index, at, n, reader))
        if not hold:
            at += n

    for j in range(NF):
        add("in", j, KD, "act")
    at += (-at) % SLOT
    for i in range(3):
        add("in_tok", i, 4 * KD, "act", hold=i < 2)
    for d in range(KD):
        for n in range(4):
            add("gate", (d, n), KD, "act")
            add("up", (d, n), 2, "dve")
    for j in range(KD):
        add("mem_k", j, KD, "act")
    for half in range(2):
        add("mem_v", (half, 0), 4 * KD, "act", hold=True)
        add("mem_v", (half, 1), 4 * KD, "act")
    for stage in ("out", "ca_q", "ca_o"):
        for j in range(KD):
            add(stage, j, KD, "act")
    for j in range(KF):
        add("ffn_a", j, KD, "act")
        add("ffn_g", j, KD, "dve")
    for j in range(KD):
        add("down", j, KF, "act")
    return tiles, at


TILES, NBLOCK = plan()
NSLOT = -(-NBLOCK // SLOT)
READER = [t[4] for t in TILES]
READ_NO = [READER[:g].count(READER[g]) + 1 for g in range(len(TILES))]


def tiles_of(*stages):
    return [(g, t) for g, t in enumerate(TILES) if t[0] in stages]


def slot_done(s):
    end = min((s + 1) * SLOT, NBLOCK)
    return next(g + 1 for g, t in enumerate(TILES) if t[2] + t[3] >= end and
                not any(u[2] < end and u[2] + u[3] > s * SLOT for u in TILES[g + 1:]))


STAGES = {
    "norm_squares": ("pre_mix_sq", "mem_sq", "post_mix_sq", "pre_ca_sq", "post_ca_sq", "pre_ffn_sq", "post_ffn_sq"),
    "norm_sums": ("pre_mix_ss", "mem_ss", "post_mix_ss", "pre_ca_ss", "post_ca_ss", "pre_ffn_ss", "post_ffn_ss"),
    "norm_scales": ("pre_mix_rstd", "mem_rstd", "post_mix_rstd", "pre_ca_rstd", "post_ca_rstd", "pre_ffn_rstd",
                    "post_ffn_rstd"),
    "norm_applied": ("pre_mix_done", "mem_done", "post_mix_done", "pre_ca_done", "post_ca_done", "pre_ffn_done",
                     "post_ffn_done"),
    "gla_tensor": ("gla_z", "gla_turned", "gla_att", "gla_ds", "gla_o", "gla_ss"),
    "gla_scalar": ("gla_log", "gla_exp", "gla_sq", "gla_r"),
    "gla_vector": ("gla_abs", "gla_cum", "gla_k", "gla_kt", "gla_attm", "gla_state", "gla_done"),
    "mla_tensor": ("mla_ss", "mla_q", "mla_ql", "mla_o"),
    "mla_scalar": ("mla_sq", "mla_r", "mla_qlc", "mla_done"),
    "mla_vector": ("mla_norm", "mla_qn", "mla_qs"),
    "mlstm_tensor": ("ml_turned", "ml_num", "ml_mean", "ml_ds", "ml_ss"),
    "mlstm_scalar": ("ml_log", "ml_exp", "ml_sq", "ml_r"),
    "mlstm_vector": ("ml_abs", "ml_rows", "ml_gw", "ml_k", "ml_h", "ml_c", "ml_state", "ml_done"),
    "rwkv_tensor": ("rw_lora", "rw_kks", "rw_bonus", "rw_ut", "rw_mean", "rw_ss"),
    "rwkv_scalar": ("rw_tw", "rw_sig", "rw_inv", "rw_exp", "rw_utok", "rw_yc", "rw_sq", "rw_r"),
    "rwkv_vector": ("rw_pm", "rw_kk", "rw_clamped", "rw_cum", "rw_vec", "rw_bo", "rw_utc", "rw_state", "rw_c", "rw_done"),
}
SERIES = {stage: series for series, stages in STAGES.items() for stage in stages}
PLACE = {stage: k for stages in STAGES.values() for k, stage in enumerate(stages)}


def program(nc, t_in, t_out):
    with ExitStack() as ctx:
        def sb(name, shape, dt=F32):
            return ctx.enter_context(nc.sbuf_tensor(name, shape, dt))

        sems = {}

        def S(name):
            name = SERIES.get(name, name)
            if name not in sems:
                sems[name] = ctx.enter_context(nc.semaphore(name))
            return sems[name]

        def at(name, n=1):
            return S(name), n + PLACE.get(name, 0)

        ring = sb("weight_ring", [P, RING, SLOT * P])
        con = sb("constants", [P, NCON])
        mat = sb("small_matrices", [P, NMAT])
        vec = sb("vectors", [P, NVEC])
        pages = sb("pages", [1, NB * PAGES], I32)
        X = sb("x_residual", [P, KD, N])
        H = sb("h_normed", [P, KD, N])
        O = sb("o_branches", [P, KD, N])
        SQ = sb("squares", [P, KD, N])
        PR = sb("projected", [P, RW, N])
        RE = sb("rwkv_projected", [P, 8, EXT])
        VT = sb("values_by_token", [P, 3, 512])
        RS = sb("rstd", [P, N])
        r_hs = sb("rwkv_last_rows", [P, 8, NB])
        WORK = 17500
        work = sb("work", [P, WORK])
        ps = ctx.enter_context(nc.psum_tensor("banks", [P, 8, 512], F32))

        def carve(word, *shape):
            n = int(np.prod(shape))
            assert word + n <= WORK, (word, n)
            a = work[:, word:word + n]
            if len(shape) == 2:
                a = a.rearrange("p (a b) -> p a b", a=shape[0])
            elif len(shape) == 3:
                a = a.rearrange("p (a b c) -> p a b c", a=shape[0], b=shape[1])
            return a, word + n

        def C(name, n=None, rows=P, r0=0):
            n = {"ident": P, "ones": P}.get(name, 1) if n is None else n
            return con[r0:r0 + rows, CON[name]:CON[name] + n]

        def V(name, j=0, rows=P):
            return vec[0:rows, VEC[name] + j:VEC[name] + j + 1]

        def M(name, a, b, r0=0, r1=P):
            return mat[r0:r1, MAT[name] + a:MAT[name] + b]

        ident = C("ident")
        eps, eps_r, one = C("eps"), C("eps_r"), C("one")

        kv, w0 = [], 0
        for i in range(2):
            a, w0 = carve(w0, PAGES, 256)
            kv.append(a)
        kpe = []
        for i in range(2):
            a, w0 = carve(w0, 512)
            kpe.append(a)
        g0 = w0
        g_t1, w0 = carve(g0, N)
        g_t2, w0 = carve(w0, N)
        g_t3, w0 = carve(w0, N)
        g_cum, w0 = carve(w0, N)
        g_eb, w0 = carve(w0, N)
        g_enb, w0 = carve(w0, N)
        g_ebe, w0 = carve(w0, N)
        g_q, w0 = carve(w0, N)
        g_k, w0 = carve(w0, N)
        g_ke, w0 = carve(w0, N)
        g_ktok, w0 = carve(w0, 3, P)
        g_att, w0 = carve(w0, 3, 512)
        g_vb, w0 = carve(w0, 4, NB * 64)
        g_st, w0 = carve(w0, NCH + 1, 64)
        g_ra, w0 = carve(w0, 2, N)
        g_s0, w0 = carve(w0, NB, 64)
        g_s1, _ = carve(g0, NB, 64)
        m_cqn, w0 = carve(g0, 2, N)
        m_ck, w0 = carve(w0, N)
        m_cktok, w0 = carve(w0, 3, P)
        m_ta, w0 = carve(w0, N)
        m_tb, w0 = carve(w0, N)
        m_kp, w0 = carve(w0, N)
        m_qn, w0 = carve(w0, 2, N)
        m_qp, w0 = carve(w0, N)
        m_ql, w0 = carve(w0, 4, N)
        m_qls, w0 = carve(w0, NB, 16)
        m_qps, w0 = carve(w0, NB, 16)
        m_ol, w0 = carve(w0, 4, N)
        m_mx, w0 = carve(w0, 4)
        m_nm, w0 = carve(w0, 4)
        m_sum, w0 = carve(w0, 4)
        m_rec, w0 = carve(w0, 4)
        m_diag, w0 = carve(w0, 16)
        m_pts, w0 = carve(w0, 17 * 16)
        m_rr, w0 = carve(w0, 2, N)
        sqf = SQ[:, :, :].rearrange("p a b -> p (a b)")
        m_p = sqf[:, 0:1024].rearrange("p (h s) -> p h s", h=4)
        m_pt = sqf[:, 1024:2048].rearrange("p (b h t) -> p b h t", b=2, h=4)
        m_ps = sqf[0:16, 0:KEYS + NS]
        l_x, w0 = carve(0, N)
        l_t, w0 = carve(w0, N)
        l_fe, w0 = carve(w0, EXT)
        l_ie, w0 = carve(w0, EXT)
        l_me, w0 = carve(w0, EXT)
        l_b, w0 = carve(w0, N)
        l_nm, w0 = carve(w0, N)
        l_g, w0 = carve(w0, N)
        L_WE, L_EM, L_WI, L_SO = 0, N, 2 * N, 2 * N + NS
        l_rows, w0 = carve(w0, 2 * N + NS + NB)
        l_mo, w0 = carve(w0, 1 + NB)
        l_m0, w0 = carve(w0, NB)
        l_gw, w0 = carve(w0, 24)
        l_kw, w0 = carve(w0, 3, 256)
        l_w, w0 = carve(w0, 4, 416)
        l_vb, w0 = carve(w0, 4, NB * 64)
        l_c0, w0 = carve(w0, 2, NB * 64)
        l_n0, w0 = carve(w0, 2, NB)
        l_nbc, w0 = carve(w0, 2, NB, 64)
        l_so, w0 = carve(w0, 2, NB)
        l_qw, w0 = carve(w0, 2, NS)
        l_den, w0 = carve(w0, 2, N)
        l_h, w0 = carve(w0, 2, N)
        l_r, w0 = carve(w0, 2, N)
        l_cp, w0 = carve(w0, 2, 64)
        l_np, w0 = carve(w0, 2)
        r_tw, w0 = carve(0, N)
        r_sg, w0 = carve(w0, N)
        r_s, w0 = carve(w0, 2, N)
        r_a, w0 = carve(w0, 2, N)
        r_g, w0 = carve(w0, 2, N)
        r_kk, w0 = carve(w0, 2, N)
        r_t, w0 = carve(w0, 2, N)
        r_cs, w0 = carve(w0, 2, N)
        r_csx, w0 = carve(w0, 2, N)
        r_cse, w0 = carve(w0, 2, N)
        r_rk, w0 = carve(w0, 2, N)
        r_al, w0 = carve(w0, 2, N)
        r_be, w0 = carve(w0, 2, N)
        r_ka, w0 = carve(w0, 2, N)
        r_rh, w0 = carve(w0, 2, N)
        r_bo, w0 = carve(w0, 2, N)
        r_d = work[:, w0 - 5 * 2 * N:w0 - 5 * 2 * N + 8 * (EXT - 1)].rearrange("p (a b) -> p a b", a=8)
        r_tok, w0 = carve(w0, 4, 256)
        r_at, w0 = carve(w0, 4, P)
        r_tm, w0 = carve(w0, 4, P)
        r_tt, w0 = carve(w0, 4, P)
        r_x, w0 = carve(w0, 4, P)
        r_off, w0 = carve(w0, 4, P)
        r_bt, w0 = carve(w0, 4, P)
        r_rb, w0 = carve(w0, 4, P)
        r_rkm, w0 = carve(w0, 4, P)
        r_bv, w0 = carve(w0, 256)
        r_gt, w0 = carve(w0, 2, P)
        r_u, w0 = carve(w0, 256)
        r_st, w0 = carve(w0, 2, 64)
        r_s0, w0 = carve(w0, 2, NB * 64)
        prf = PR[:, :, :].rearrange("p a b -> p (a b)")
        r_ub = prf[:, 0:2048].rearrange("p (h n) -> p h n", h=4)
        r_vb = prf[:, 2048:4096].rearrange("p (h n) -> p h n", h=4)
        r_sh, _ = carve(w0, 8, 1 + NB)
        c_mem, w0 = carve(0, KD, MEM)
        c_mkt, w0 = carve(w0, KD, MEM)
        c_mv, w0 = carve(w0, 2, D)
        c_k, c_v = [], []
        for i in range(2):
            a, w0 = carve(w0, KD, MEM)
            c_k.append(a)
            a, w0 = carve(w0, 2, D)
            c_v.append(a)
        c_mx, w0 = carve(w0, 4)
        c_nm, w0 = carve(w0, 4)
        c_sum, w0 = carve(w0, 4)
        c_rec, w0 = carve(w0, 4)
        c_p = sqf[:, 0:1024].rearrange("p (h s) -> p h s", h=4)
        c_pt = sqf[:, 1024:2048].rearrange("p (b h t) -> p b h t", b=2, h=4)
        c_ps = sqf[:, 0:MEM]
        c_pts = sqf[:, 1024:1280].rearrange("p (b t) -> p b t", b=2)
        f_f, w0 = carve(0, KF, N)
        f_a, w0 = carve(w0, 2, EXC)
        f_c, w0 = carve(w0, 2, EXC - 2)
        f_s, w0 = carve(w0, KF, 2 * NB)
        f_o, w0 = carve(w0, KF, 2 * (1 + NB))

        def per_batch(ap, n):
            return ap.rearrange("p (b t) -> p b t", t=n)

        def smp(ap):
            return per_batch(ap[:, TP:N], TS)

        def ext_prompt(ap):
            return ap[:, 1:1 + TP]

        def ext_sample(ap):
            return per_batch(ap[:, 1 + TP:EXT], 1 + TS)[:, :, 1:1 + TS]

        def chunks(ap):
            return ap[:, 0:TP].rearrange("p (c t) -> p c t", t=CH)

        def bc(ap, shape):
            return ap.broadcast_to(shape)

        def read_done(eng, stage):
            g = tiles_of(stage)[-1][0]
            eng.wait_ge(*at("bank_read_" + READER[g], READ_NO[g]))

        class Steps:

            def __init__(self, eng, chain):
                self.eng, self.chain, self.n = eng, chain, {}

            def __call__(self, ins, signal=None):
                name = SERIES.get(signal or self.chain, signal or self.chain)
                self.n[name] = self.n.get(name, 0) + 1
                assert signal not in PLACE or self.n[name] == PLACE[signal] + 1, signal
                ins.then_inc(S(name), 1)
                self.eng.wait_ge(S(name), self.n[name])

        dq = {}

        def dma(eng, name, dst, src):
            dq[name] = dq.get(name, 0) + 16
            eng.dma_start(dst, src).then_inc(S(name), 16)

        with nc.Block() as block:
            @block.sync
            def _(sp):
                sp.dma_start(con[:, :], t_in["const"]).then_inc(S("load_once"), 16)
                sp.dma_start(X[:, :, :], t_in["x"]).then_inc(S("load_once"), 16)
                sp.dma_start(pages[:, :], t_in["pages"]).then_inc(S("load_once"), 16)
                sp.wait_ge(*at("load_once", 48))

        with nc.Fori(0, L) as layer:
            def dram(name, group=t_in):
                a = group[name][bass.ds(layer, 1)]
                k = len(a.shape)
                if k == 3:
                    return a.rearrange("o p a -> (o p) a")
                if k == 4:
                    return a.rearrange("o p a b -> (o p) a b")
                return a.rearrange("o p a b c -> (o p) a b c")

            def dram_out(name):
                return dram(name, t_out)

            with nc.Block() as block:
                @block.sync
                def _(sp):
                    def slot(s):
                        if s >= RING:
                            sp.wait_ge(*at("gemm_done", slot_done(s - RING)))
                        src = t_in["w"][bass.ds(layer, 1), s].rearrange("o p a -> (o p) a")
                        sp.dma_start(ring[:, s % RING, :], src).then_inc(S(f"slot_full{s % RING}"), 16)

                    def cache(b):
                        if b >= 2:
                            sp.wait_ge(*at("mla_ol_s", b - 1))
                        for p in range(PAGES):
                            page = sp.value_load(pages[0:1, b * PAGES + p:b * PAGES + p + 1],
                                                 min_val=0, max_val=POOL - 1)
                            src = t_in["kv"][bass.ds(layer, 1), bass.ds(page, 1)].rearrange("o g p a -> (o g p) a")
                            sp.dma_start(kv[b % 2][:, p, :], src).then_inc(S(f"kv_full{b % 2}"), 16)
                            src = t_in["kpe"][bass.ds(layer, 1), bass.ds(page, 1)].rearrange("o g p a -> (o g p) a")
                            q = p // 4
                            sp.dma_start(kpe[b % 2][32 * q:32 * q + 32, p % 4 * P:(p % 4 + 1) * P], src)\
                                .then_inc(S(f"kv_full{b % 2}"), 16)

                    n_in = tiles_of("gate")[0][1][2] // SLOT
                    for s in range(n_in):
                        slot(s)
                    cache(0)
                    cache(1)
                    for s in range(n_in, n_in + RING):
                        slot(s)
                    for b in range(2, NB):
                        cache(b)
                    for s in range(n_in + RING, NSLOT):
                        slot(s)

                @block.gpsimd
                def _(pool):
                    dma(pool, "load_vec", vec[:, :], dram("vec"))
                    dma(pool, "load_mat", mat[:, :], dram("mat"))
                    dma(pool, "load_shift", r_hs[:, :, :], dram("shift"))
                    dma(pool, "load_gla", g_s0[:, :, :], dram("gla"))
                    pool.wait_ge(*at("gla_state"))
                    dma(pool, "stores", dram_out("gla_p"), g_st[:, NCH, :])
                    dma(pool, "stores", dram_out("gla_s"), g_s1[:, :, :])
                    pool.wait_ge(*at("mla_norm"))
                    dma(pool, "stores", dram_out("ckv"), m_ck[:, :])
                    dma(pool, "stores", dram_out("kpe"), m_kp[0:32, :])
                    pool.wait_ge(*at("mla_done"))
                    pool.wait_ge(*at("stores", 64))
                    dma(pool, "load_ml", l_c0[:, :, :], dram("ml_c"))
                    dma(pool, "load_ml", l_n0[:, :, :], dram("ml_n"))
                    dma(pool, "load_ml", l_m0[0:4, :], dram("ml_m"))
                    pool.wait_ge(*at("ml_state"))
                    dma(pool, "stores_ml", dram_out("ml_c_s"), l_c0[:, :, :])
                    dma(pool, "stores_ml", dram_out("ml_n_s"), l_n0[:, :, :])
                    dma(pool, "stores_ml", dram_out("ml_c_p"), l_cp[:, :, :])
                    dma(pool, "stores_ml", dram_out("ml_n_p"), l_np[:, :])
                    dma(pool, "stores_ml", dram_out("ml_m_ps"), l_mo[0:4, :])
                    pool.wait_ge(*at("stores_ml", 80))
                    pool.wait_ge(*at("ml_done"))
                    dma(pool, "load_rw", r_s0[:, :, :], dram("rwkv"))
                    pool.wait_ge(*at("rw_state"))
                    dma(pool, "stores_rw", dram_out("rwkv_s"), r_s0[:, :, :])
                    dma(pool, "stores_rw", dram_out("rwkv_p"), r_st[:, :, :])
                    dma(pool, "stores_rw", dram_out("shift_ps"), r_sh[:, :, :])
                    pool.wait_ge(*at("rw_done"))
                    pool.wait_ge(*at("stores_rw", 48))
                    dma(pool, "load_mem", c_mem[:, :, :], t_in["mem"])
                    for b in range(NB):
                        if b >= 2:
                            pool.wait_ge(*at("ca_o_s", b - 1))
                        dma(pool, f"ca_k_full{b % 2}", c_k[b % 2][:, :, :], t_in["mem_k"][bass.ds(layer, 1), b].rearrange("o p a b -> (o p) a b"))
                        dma(pool, f"ca_v_full{b % 2}", c_v[b % 2][:, :, :], t_in["mem_v"][bass.ds(layer, 1), b].rearrange("o (t p) d -> p (o t) d", p=P))
                        if b == 1:
                            read_done(pool, "mem_v")
                            dma(pool, "stores_mem", dram_out("mem_kt"), c_mkt[:, :, :])
                            dma(pool, "stores_mem", dram_out("mem_v"), c_mv[:, :, :])
                    pool.wait_ge(*at("ca_oc", 2 + NB))
                    pool.wait_ge(*at("stores_mem", 32))
                    dma(pool, "load_conv", f_s[:, :, :], dram("conv"))
                    pool.wait_ge(*at("conv_state", KF))
                    dma(pool, "stores_conv", dram_out("conv_ps"), f_o[:, :, :])
                    pool.wait_ge(*at("stores_conv", 16))

                @block.tensor
                def _(pe):
                    mm = nc.tensor.matmul

                    def add(out, lhs, rhs):
                        return mm(out, lhs, rhs, start=False, stop=True, skip_group_check=True)

                    def put(out, lhs, rhs):
                        return mm(out, lhs, rhs, start=True, stop=True, skip_group_check=True)

                    def turn(out, in_):
                        k = in_.shape[0]
                        return nc.tensor.transpose(out, in_, ident[0:k, 0:k])

                    fences = [0]

                    def fence(ins):
                        fences[0] += 1
                        ins.then_inc(S("rows_free"), 1)
                        pe.wait_ge(*at("rows_free", fences[0]))

                    def block_of(i):
                        return ring[:, i // SLOT % RING, i % SLOT * P:(i % SLOT + 1) * P]

                    arrived = [0]

                    def gemm(g, rhs, lhs=None, width=N):
                        stage, _, first, n, _ = TILES[g]
                        if g >= GEMM_BANKS:
                            h = g - GEMM_BANKS
                            pe.wait_ge(*at("bank_read_" + READER[h], READ_NO[h]))
                        bank = g % GEMM_BANKS
                        if lhs is None:
                            for k in range(n):
                                slot_here(first + k)
                                last = mm(ps[:, bank, 0:width], block_of(first + k), rhs(k), start=k == 0, stop=k == n - 1)
                        else:
                            for k in range(n // 4):
                                slot_here(first + 4 * k)
                                i = first + 4 * k
                                four = ring[:, i // SLOT % RING, i % SLOT * P:(i % SLOT + 4) * P]
                                a = lhs(k)
                                last = mm(ps[0:a.shape[1], bank, :], a, four, start=k == 0, stop=k == n // 4 - 1)
                        last.then_inc(S("gemm_done"), 1)

                    def slot_here(i):
                        s = i // SLOT
                        if s >= arrived[0]:
                            pe.wait_ge(*at(f"slot_full{s % RING}", 16 * (s // RING + 1)))
                            arrived[0] = s + 1

                    def sum_squares(name, width=N):
                        pe.wait_ge(*at(name + "_sq"))
                        for k in range(KD):
                            last = mm(ps[:, 7, 0:width], C("ones"), SQ[:, k, 0:width], start=k == 0, stop=k == KD - 1)
                        last.then_inc(S(name + "_ss"), 1)

                    sum_squares("pre_mix")
                    pe.wait_ge(*at("pre_mix_done"))
                    for g, t in tiles_of("in"):
                        gemm(g, lambda k: H[:, k, :])
                    for g, t in tiles_of("in_tok"):
                        c0, n = TT[t[1]]
                        gemm(g, None, lhs=lambda k: H[:, k, c0:c0 + n])

                    read_done(pe, "in_tok")
                    pe.wait_ge(*at("load_mat", 16))
                    put(ps[:, 4, 0:N], M("gate2", 0, P, GLO_AT, GLO_AT + 16), PR[GLO_AT:GLO_AT + 16, MIX1, :])\
                        .then_inc(S("gla_z"), 1)
                    pe.wait_ge(*at("gla_k"))
                    for i, (c0, n) in enumerate(TT):
                        last = turn(ps[0:n, 3, i * P:(i + 1) * P], g_ke[:, c0:c0 + n])
                    last.then_inc(S("gla_turned"), 1)
                    for h in range(4):
                        r = slice(32 * h, 32 * h + 32)
                        if h:
                            fence(last)
                        for i, (c0, n) in enumerate(TT):
                            last = put(ps[0:n, i, h * n:(h + 1) * n], g_k[r, c0:c0 + n], g_q[r, c0:c0 + n])
                    last.then_inc(S("gla_att"), 1)
                    pe.wait_ge(*at("gla_kt"))
                    for odd in range(2):
                        b0 = 64 * odd
                        for h in range(4):
                            r = slice(32 * h, 32 * h + 32)
                            for c in range(odd, NCH, 2):
                                last = put(ps[r, 4, c * 64:(c + 1) * 64], g_ktok[b0:b0 + 64, c // 2, r],
                                           VT[b0:b0 + 64, c // 2, h * 64:(h + 1) * 64])
                        if not odd:
                            fence(last)
                    for h in range(4):
                        r = slice(32 * h, 32 * h + 32)
                        last = put(ps[r, 5, :], g_ktok[0:NS, 2, r], g_vb[0:NS, h, :])
                    last.then_inc(S("gla_ds"), 1)
                    pe.wait_ge(*at("gla_attm"))
                    pe.wait_ge(*at("gla_state"))
                    o_heads = [(h, slice(32 * h, 32 * h + 32), ps[64 * (h % 2):64 * (h % 2) + 64, 6 + h // 2, :]) for h in range(4)]
                    for h, r, out in o_heads:
                        for i, (c0, n) in enumerate(TT[:2]):
                            last = put(out[:, c0:c0 + n], VT[0:n, i, h * 64:(h + 1) * 64], g_att[0:n, i, h * n:(h + 1) * n])
                            for c in (2 * i, 2 * i + 1):
                                if c:
                                    last = add(out[:, c * CH:(c + 1) * CH], g_st[r, c, :], g_q[r, c * CH:(c + 1) * CH])
                    fence(last)
                    for h, r, out in o_heads:
                        last = put(out[:, TP:N], VT[0:NS, 2, h * 64:(h + 1) * 64], g_att[0:NS, 2, h * NS:(h + 1) * NS])
                    fence(last)
                    for h, r, out in o_heads:
                        for b in range(NB):
                            j = TP + b * TS
                            last = add(out[:, j:j + TS], g_s0[r, b, :], g_q[r, j:j + TS])
                    last.then_inc(S("gla_o"), 1)
                    pe.wait_ge(*at("gla_sq"))
                    for j in range(2):
                        last = put(ps[:, j, 0:N], C("blk64", P), SQ[:, j, :])
                    last.then_inc(S("gla_ss"), 1)

                    pe.wait_ge(*at("mla_sq"))
                    pe.wait_ge(*at("gla_r"))
                    mm(ps[:, 2, 0:N], C("ones"), SQ[:, 2, :], start=True, stop=False)
                    mm(ps[:, 2, 0:N], C("ones"), SQ[:, 3, :], start=False, stop=True)
                    put(ps[:, 3, 0:N], C("ones"), SQ[:, 4, :]).then_inc(S("mla_ss"), 1)
                    pe.wait_ge(*at("mla_norm"))
                    for j in range(4):
                        for k in range(2):
                            last = mm(ps[:, 2 + j, 0:N], M("uq", k * 512 + j * P, k * 512 + (j + 1) * P), m_cqn[:, k, :],
                                      start=k == 0, stop=k == 1)
                    pe.wait_ge(*at("gla_done"))
                    for i, (c0, n) in enumerate(TT):
                        last = turn(ps[0:n, 6, i * P:(i + 1) * P], m_ck[:, c0:c0 + n])
                    last.then_inc(S("mla_q"), 1)
                    pe.wait_ge(*at("mla_qn"))
                    for h in range(4):
                        hb, hp = 64 * (h % 2), h // 2
                        last = put(ps[:, h, 0:N], M("uk", hp * P, (hp + 1) * P, hb, hb + 64), m_qn[hb:hb + 64, hp, :])
                    last.then_inc(S("mla_ql"), 1)
                    pe.wait_ge(*at("mla_qlc"))
                    for qt in range(2):
                        nk = (qt + 1) * P
                        q = slice(qt * P, (qt + 1) * P)
                        for h in range(4):
                            r = slice(32 * h, 32 * h + 32)
                            put(ps[:, h, 0:nk], m_ql[:, h, q], m_ck[:, 0:nk])
                            add(ps[:, h, 0:nk], m_qp[r, q], m_kp[r, 0:nk])
                            last = add(ps[:, h, q], ident, C("bias_tok", P))
                        last.then_inc(S("mla_s"), 1)
                        pe.wait_ge(*at("mla_pn", qt + 1))
                        for b in range(qt + 1):
                            for h in range(4):
                                last = turn(ps[:, 4 + b, h * P:(h + 1) * P], m_p[:, h, b * P:(b + 1) * P])
                        last.then_inc(S("mla_pt"), 1)
                        pe.wait_ge(*at("mla_ptc", qt + 1))
                        for h in range(4):
                            for b in range(qt + 1):
                                last = mm(ps[:, 6, h * P:(h + 1) * P], m_cktok[:, b, :], m_pt[:, b, h, :],
                                          start=b == 0, stop=b == qt)
                        last.then_inc(S("mla_ol"), 1)
                    pe.wait_ge(*at("mla_qs"))
                    for b in range(NB):
                        pe.wait_ge(*at(f"kv_full{b % 2}", 16 * 2 * PAGES * (b // 2 + 1)))
                        pe.wait_ge(*at("mla_olc", 2 + b))
                        for q in range(4):
                            put(ps[0:16, q, :], m_qls[:, b, :], kv[b % 2][:, 4 * q:4 * q + 4, P:2 * P])
                            r = slice(32 * q, 32 * q + 32)
                            add(ps[0:16, q, :], m_qps[r, b, :], kpe[b % 2][r, :])
                        put(ps[0:16, 4, 0:NS], m_qls[:, b, :], m_ck[:, TP:N])
                        add(ps[0:16, 4, 0:NS], m_qps[0:32, b, :], m_kp[0:32, TP:N])
                        add(ps[0:16, 4, 0:NS], ident[0:16, 0:16], C("bias_own", NB * NS, 16)[:, b * NS:(b + 1) * NS])\
                            .then_inc(S("mla_ss_s"), 1)
                        pe.wait_ge(*at("mla_d_s", b + 1))
                        for p in range(PAGES):
                            put(ps[:, 5, p * 16:(p + 1) * 16], m_ps[:, p * P:(p + 1) * P], m_diag[0:16, :])
                        put(ps[0:NS, 5, 256:272], m_ps[:, KEYS:KEYS + NS], m_diag[0:16, :]).then_inc(S("mla_pt_s"), 1)
                        pe.wait_ge(*at("mla_ptc_s", b + 1))
                        for p in range(PAGES):
                            mm(ps[:, 6, 0:16], kv[b % 2][:, p, 0:P], m_pts[:, p * 16:(p + 1) * 16], start=p == 0, stop=False)
                        mm(ps[:, 6, 0:16], m_cktok[0:NS, 2, :], m_pts[0:NS, 256:272], start=False, stop=True)\
                            .then_inc(S("mla_ol_s"), 1)
                    pe.wait_ge(*at("mla_olc", 2 + NB))
                    for h in range(4):
                        hb = 64 * (h % 2)
                        last = put(ps[hb:hb + 64, h // 2, 0:N], M("uv", h * 64, (h + 1) * 64), m_ol[:, h, :])
                    last.then_inc(S("mla_o"), 1)

                    pe.wait_ge(*at("ml_exp"))
                    pe.wait_ge(*at("mla_done"))
                    for i, (c0, n) in enumerate(TT):
                        turn(ps[0:n, 0, i * 8:i * 8 + 4], l_g[0:4, c0:c0 + n])
                        turn(ps[0:n, 0, i * 8 + 4:i * 8 + 8], l_rows[0:4, L_WE + c0:L_WE + c0 + n])
                    for hp in range(2):
                        sel = C("sel_p", 2 * P, 4)[:, hp * P:(hp + 1) * P]
                        put(ps[:, 1 + hp, 0:N], sel, l_rows[0:4, L_EM:L_EM + N])
                        put(ps[:, 3, hp * NS:(hp + 1) * NS], sel, l_rows[0:4, L_WI:L_WI + NS])
                        put(ps[:, 3, 64 + hp * NB:64 + (hp + 1) * NB], sel, l_rows[0:4, L_SO:L_SO + NB])
                    for i, (c0, n) in enumerate(TT):
                        for hp in range(2):
                            c = i % 2 * 256 + hp * P
                            last = turn(ps[0:n, 4 + i // 2, c:c + P], PR[:, MK + hp, c0:c0 + n])
                    last.then_inc(S("ml_turned"), 1)
                    pe.wait_ge(*at("ml_k"))
                    for h in range(4):
                        if h >= 2:
                            pe.wait_ge(*at("ml_w", h - 1))
                        bias, qk = ps[:, 4 + h % 2, :], ps[:, 6 + h % 2, :]
                        sel = C("sel_h", 4 * P, 4)[:, h * P:(h + 1) * P]
                        put(bias[:, 0:416], ident, C("bias_m", 416))
                        add(bias[:, 0:256], sel, l_nm[0:4, 0:TP])
                        add(bias[:, 256:384], sel, l_nm[0:4, P:TP])
                        add(bias[:, 384:416], sel, l_nm[0:4, TP:N])
                        r, hp = slice(64 * (h % 2), 64 * (h % 2) + 64), h // 2
                        k, q = PR[r, MK + hp, :], PR[r, MQ + hp, :]
                        put(qk[:, 0:256], k[:, 0:P], q[:, 0:TP])
                        put(qk[:, 256:384], k[:, P:TP], q[:, P:TP])
                        put(qk[0:NS, 384:416], k[:, TP:N], q[:, TP:N]).then_inc(S("ml_s"), 1)
                    pe.wait_ge(*at("ml_w", 4))
                    for h in range(4):
                        r, hp = slice(64 * (h % 2), 64 * (h % 2) + 64), h // 2
                        for out, lhs, st in (
                                (ps[r, 4 + hp, :], lambda i, n: VT[0:n, i, 256 + h * 64:256 + (h + 1) * 64],
                                 lambda b: l_c0[r, hp, b * 64:(b + 1) * 64]),
                                (ps[r, 6 + hp, :], lambda i, n: C("ones", 64, n), lambda b: l_nbc[r, hp, b, :])):
                            put(out[:, 0:P], lhs(0, P), l_w[:, h, 0:P])
                            put(out[:, P:TP], lhs(0, P), l_w[:, h, P:TP])
                            add(out[:, P:TP], lhs(1, P), l_w[:, h, 256:384])
                            put(out[:, TP:N], lhs(2, NS), l_w[0:NS, h, 384:416])
                            for b in range(NB):
                                last = add(out[:, TP + b * TS:TP + (b + 1) * TS], st(b), l_qw[r, hp, b * TS:(b + 1) * TS])
                    last.then_inc(S("ml_num"), 1)
                    pe.wait_ge(*at("ml_h"))
                    for hp in range(2):
                        last = put(ps[:, 4 + hp, 0:N], C("blk64", P), l_h[:, hp, :])
                    last.then_inc(S("ml_mean"), 1)
                    for h in range(4):
                        r, hp = slice(64 * (h % 2), 64 * (h % 2) + 64), h // 2
                        hc = slice(h * 64, (h + 1) * 64)
                        for i in range(2):
                            mm(ps[r, 3, hp * 64:(hp + 1) * 64], l_kw[:, i, hc], VT[:, i, 256 + h * 64:256 + (h + 1) * 64],
                               start=i == 0, stop=i == 1)
                        for i in range(2):
                            mm(ps[r, 3, P + hp:P + hp + 1], l_kw[:, i, hc], C("ones", 1), start=i == 0, stop=i == 1)
                        put(ps[r, 3, 136 + hp * NB:136 + (hp + 1) * NB], l_kw[0:NS, 2, hc], C("batch", NB, NS))
                        last = put(ps[r, 1 + hp, :], l_kw[0:NS, 2, hc], l_vb[0:NS, h, :])
                    last.then_inc(S("ml_ds"), 1)
                    pe.wait_ge(*at("ml_sq"))
                    for hp in range(2):
                        last = put(ps[:, 6 + hp, 0:N], C("blk64", P), SQ[:, hp, :])
                    last.then_inc(S("ml_ss"), 1)

                    pe.wait_ge(*at("rw_tw"))
                    pe.wait_ge(*at("ml_state"))
                    pe.wait_ge(*at("ml_done"))
                    for hp in range(2):
                        c = slice(hp * P, (hp + 1) * P)
                        put(ps[:, hp, 0:N], M("wa", c.start, c.stop, 0, 64), r_tw[0:64, :])
                        put(ps[:, 2 + hp, 0:N], M("wa", c.start, c.stop, 64, P), SQ[64:P, 6, :])
                        last = put(ps[:, 4 + hp, 0:N], M("g2", c.start, c.stop), r_sg[:, :])
                    last.then_inc(S("rw_lora"), 1)
                    pe.wait_ge(*at("rw_kk"))
                    for hp in range(2):
                        last = put(ps[:, 6 + hp, 0:N], C("blk64", P), r_t[:, hp, :])
                    last.then_inc(S("rw_kks"), 1)
                    pe.wait_ge(*at("rw_vec"))
                    for hp in range(2):
                        last = put(ps[:, 6 + hp, 0:N], C("blk64", P), r_bo[:, hp, :])
                    last.then_inc(S("rw_bonus"), 1)
                    halves = [(h, slice(64 * (h % 2), 64 * (h % 2) + 64), h // 2) for h in range(4)]
                    levels = 0
                    for i, (c0, n) in enumerate(TT):
                        t = slice(c0, c0 + n)
                        if i:
                            pe.wait_ge(*at("rw_st", 2 * i))
                            pe.wait_ge(*at("rw_uc", 2 * i))
                        for odd in range(2):
                            for bank, a, b in ((0, r_be, r_al), (1, r_al, r_be), (2, r_rk, r_al), (3, r_be, r_rh), (4, r_rk, r_rh)):
                                for h, r, hp in halves[odd::2]:
                                    last = put(ps[0:n, bank, h * n:(h + 1) * n], a[r, hp, t], b[r, hp, t])
                            if not odd:
                                fence(last)
                        last.then_inc(S("rw_pair"), 1)
                        for kind, src in ((0, r_al), (1, r_kk)):
                            for hp in range(2):
                                c = kind * 256 + hp * P
                                last = turn(ps[0:n, 5, c:c + P], src[:, hp, t])
                        last.then_inc(S("rw_tok"), 1)
                        pe.wait_ge(*at("rw_pairm", i + 1))
                        for kind, src in ((0, r_cs), (1, SQ[:, 4:6, :])):
                            for hp in range(2):
                                c = kind * 256 + hp * P
                                last = turn(ps[0:n, 0, c:c + P], src[:, hp, t])
                        last.then_inc(S("rw_tok"), 1)
                        for j in range(1, 6 if i < 2 else 2):
                            levels += 1
                            pe.wait_ge(*at("rw_off", levels))
                            for h, r, hp in halves:
                                last = put(ps[0:n, 1, h * n:(h + 1) * n], r_off[0:n, h, 0:n], r_tm[0:n, h, 0:n])
                            last.then_inc(S("rw_x"), 1)
                            pe.wait_ge(*at("rw_xc", levels))
                            for h, r, hp in halves:
                                put(ps[0:n, 2, h * n:(h + 1) * n], r_tt[0:n, h, 0:n], r_x[0:n, h, 0:n])
                                last = put(ps[0:n, 3, h * n:(h + 1) * n], r_x[0:n, h, 0:n], r_tt[0:n, h, 0:n])
                            last.then_inc(S("rw_y"), 1)
                        pe.wait_ge(*at("rw_tokc", 2 * i + 2))
                        pe.wait_ge(*at("rw_t", levels))
                        for h, r, hp in halves:
                            hc = slice(h * 64, (h + 1) * 64)
                            put(ps[0:n, 4, hc], r_bt[0:n, h, 0:n], r_tok[0:n, 3, hc])
                            last = put(ps[r, 5, hp * n:(hp + 1) * n], r_tok[0:n, 0, hc], r_tt[0:n, h, 0:n])
                        last.then_inc(S("rw_bg"), 1)
                        pe.wait_ge(*at("rw_bgc", i + 1))
                        if i == 0:
                            pe.wait_ge(*at("rw_bo"))
                        if i < 2:
                            for c in (2 * i, 2 * i + 1):
                                s = slice(64 * (c % 2), 64 * (c % 2) + 64)
                                cc = slice(c * CH, (c + 1) * CH)
                                if c:
                                    pe.wait_ge(*at("rw_st", c))
                                for h, r, hp in halves:
                                    hc = slice(h * 64, (h + 1) * 64)
                                    last = mm(ps[s, 0, hc], r_tt[s, h, s], r_bv[s, hc], start=h == 0, stop=c == 0,
                                              skip_group_check=True)
                                for odd in ((c % 2, 1 - c % 2) if c else ()):
                                    if odd != c % 2:
                                        fence(last)
                                    for h, r, hp in halves[odd::2]:
                                        last = add(ps[s, 0, h * 64:(h + 1) * 64], r_gt[r, hp, s], r_st[r, hp, :])
                                last.then_inc(S("rw_u"), 1)
                                pe.wait_ge(*at("rw_uc", c + 1))
                                for h, r, hp in halves:
                                    hc = slice(h * 64, (h + 1) * 64)
                                    put(ps[r, 1, hp * 64:(hp + 1) * 64], r_tok[s, 1, hc], r_u[s, hc])
                                    last = add(ps[r, 1, hp * 64:(hp + 1) * 64], r_tok[s, 2, hc], r_tok[s, 3, hc])
                                for h, r, hp in halves:
                                    hc = slice(h * 64, (h + 1) * 64)
                                    put(ps[r, 6 + hp, cc], r_u[s, hc], r_rb[s, h, s])
                                    last = add(ps[r, 6 + hp, cc], r_tok[s, 3, hc], r_rkm[s, h, s])
                                if c:
                                    fence(last)
                                    for h, r, hp in halves:
                                        last = add(ps[r, 6 + hp, cc], r_st[r, hp, :], r_rh[r, hp, cc])
                                last.then_inc(S("rw_ds"), 1)
                        else:
                            pe.wait_ge(*at("load_rw", 16))
                            for h, r, hp in halves:
                                hc = slice(h * 64, (h + 1) * 64)
                                put(ps[r, 0, hp * NS:(hp + 1) * NS], r_bv[0:NS, hc], r_tt[0:NS, h, 0:NS])
                                for b in range(NB):
                                    j = hp * NS + b * TS
                                    last = add(ps[r, 0, j:j + TS], r_s0[r, hp, b * 64:(b + 1) * 64],
                                               r_gt[r, hp, b * TS:(b + 1) * TS])
                            last.then_inc(S("rw_u"), 1)
                            pe.wait_ge(*at("rw_uc", 5))
                            for hp in range(2):
                                last = turn(ps[0:NS, 1, hp * P:(hp + 1) * P], r_x[:, hp, 0:NS])
                            last.then_inc(S("rw_ut"), 1)
                            pe.wait_ge(*at("rw_utc"))
                            for h, r, hp in halves:
                                hc = slice(h * 64, (h + 1) * 64)
                                put(ps[r, 2 + hp, :], r_tok[0:NS, 1, hc], r_ub[0:NS, h, :])
                                add(ps[r, 2 + hp, :], r_tok[0:NS, 2, hc], r_vb[0:NS, h, :])
                                put(ps[r, 6 + hp, TP:N], r_u[0:NS, hc], r_rb[0:NS, h, 0:NS])
                                add(ps[r, 6 + hp, TP:N], r_tok[0:NS, 3, hc], r_rkm[0:NS, h, 0:NS])
                                for b in range(NB):
                                    j = TP + b * TS
                                    last = add(ps[r, 6 + hp, j:j + TS], r_s0[r, hp, b * 64:(b + 1) * 64], r_rh[r, hp, j:j + TS])
                            last.then_inc(S("rw_ds"), 1)
                    pe.wait_ge(*at("rw_yc"))
                    for hp in range(2):
                        last = put(ps[:, hp, 0:N], C("blk64", P), r_a[:, hp, :])
                    last.then_inc(S("rw_mean"), 1)
                    pe.wait_ge(*at("rw_sq"))
                    for hp in range(2):
                        last = put(ps[:, 4 + hp, 0:N], C("blk64", P), r_t[:, hp, :])
                    last.then_inc(S("rw_ss"), 1)

                    pe.wait_ge(*at("rw_done"))
                    for g, t in tiles_of("gate", "up"):
                        if t[0] == "gate":
                            gemm(g, lambda k: H[:, k, :])
                        else:
                            gemm(g, lambda k: O[:, 2 * t[1][1] + k, :])

                    read_done(pe, "gate")
                    pe.wait_ge(*at("mixed", KD))
                    sum_squares("mem", MEM)
                    pe.wait_ge(*at("mem_done"))
                    for g, t in tiles_of("mem_k"):
                        gemm(g, lambda k: c_mem[:, k, :], width=MEM)
                    for g, t in tiles_of("mem_v"):
                        tok = t[1][1]
                        gemm(g, None, lhs=lambda k: c_mem[:, k, tok * P:(tok + 1) * P])

                    for g, t in tiles_of("out"):
                        gemm(g, lambda k: PR[:, k, :])
                    sum_squares("post_mix")

                    sum_squares("pre_ca")
                    pe.wait_ge(*at("pre_ca_done"))
                    for g, t in tiles_of("ca_q"):
                        gemm(g, lambda k: H[:, k, :])
                    read_done(pe, "ca_q")
                    for qt in range(2):
                        q = slice(qt * P, (qt + 1) * P)
                        for h in range(4):
                            for j in range(2):
                                last = mm(ps[:, h, 0:MEM], O[:, 2 * h + j, q], c_mkt[:, 2 * h + j, :], start=j == 0, stop=j == 1)
                        last.then_inc(S("ca_s"), 1)
                        pe.wait_ge(*at("ca_pn", qt + 1))
                        for b in range(2):
                            for h in range(4):
                                last = turn(ps[:, 4 + b, h * P:(h + 1) * P], c_p[:, h, b * P:(b + 1) * P])
                        last.then_inc(S("ca_pt"), 1)
                        pe.wait_ge(*at("ca_ptc", qt + 1))
                        for h in range(4):
                            for j in range(2):
                                d = 2 * h + j
                                for b in range(2):
                                    last = mm(ps[:, 6 + d // 4, d % 4 * P:(d % 4 + 1) * P], c_mv[:, b, d * P:(d + 1) * P],
                                              c_pt[:, b, h, :], start=b == 0, stop=b == 1)
                        last.then_inc(S("ca_o"), 1)
                    for b in range(NB):
                        pe.wait_ge(*at(f"ca_k_full{b % 2}", 16 * (b // 2 + 1)))
                        pe.wait_ge(*at("ca_oc", 2 + b))
                        for h in range(4):
                            for j in range(2):
                                last = mm(ps[32 * h:32 * h + 32, 0, 0:MEM], O[:, 2 * h + j, TP:N], c_k[b % 2][:, 2 * h + j, :],
                                          start=j == 0, stop=j == 1)
                        last.then_inc(S("ca_ss_s"), 1)
                        pe.wait_ge(*at("ca_pn_s", b + 1))
                        for s in range(2):
                            last = turn(ps[:, 1, s * P:(s + 1) * P], c_ps[:, s * P:(s + 1) * P])
                        last.then_inc(S("ca_pt_s"), 1)
                        pe.wait_ge(*at("ca_ptc_s", b + 1))
                        pe.wait_ge(*at(f"ca_v_full{b % 2}", 16 * (b // 2 + 1)))
                        for d in range(8):
                            h = d // 2
                            for s in range(2):
                                last = mm(ps[:, 2, d * TS:(d + 1) * TS], c_v[b % 2][:, s, d * P:(d + 1) * P],
                                          c_pts[:, s, 32 * h + b * TS:32 * h + (b + 1) * TS], start=s == 0, stop=s == 1)
                        last.then_inc(S("ca_o_s"), 1)
                    pe.wait_ge(*at("ca_oc", 2 + NB))
                    for g, t in tiles_of("ca_o"):
                        gemm(g, lambda k: H[:, k, :])
                    sum_squares("post_ca")

                    sum_squares("pre_ffn")
                    pe.wait_ge(*at("pre_ffn_done"))
                    for g, t in tiles_of("ffn_a", "ffn_g"):
                        gemm(g, lambda k: H[:, k, :])
                    read_done(pe, "ffn_g")
                    for g, t in tiles_of("down"):
                        gemm(g, lambda k: f_f[:, k, :])
                    sum_squares("post_ffn")

                @block.scalar
                def _(act):
                    step = Steps(act, "act_step")
                    A = nc.scalar.activation

                    def copy(out, in_, signal=None):
                        step(A(out, in_, ACT.Copy), signal)

                    def wait(name, n=1):
                        act.wait_ge(*at(name, n))

                    def tile_ready(g):
                        wait("gemm_done", g + 1)

                    def rstd(name, width=N):
                        wait(name + "_ss")
                        step(A(RS[:, 0:width], ps[:, 7, 0:width], ACT.Ln, bias=eps, scale=1.0 / D))
                        step(A(RS[:, 0:width], RS[:, 0:width], ACT.Exp, scale=-0.5), name + "_rstd")

                    def squares(name, src, width=N):
                        step(A(SQ[:, :, 0:width], src, ACT.Square), name + "_sq")

                    squares("pre_mix", X[:, :, :])
                    rstd("pre_mix")
                    wait("halo")
                    for g, t in tiles_of("in"):
                        tile_ready(g)
                        j, src = t[1], ps[:, g % GEMM_BANKS, :]
                        if j >= RW:
                            step(A(ext_prompt(RE[:, j - RW, :]), src[:, 0:TP], ACT.Copy))
                            copy(ext_sample(RE[:, j - RW, :]), per_batch(src[:, TP:N], TS), "bank_read_act")
                        else:
                            f = ACT.Silu if j in (GR, GR + 1) else ACT.Sigmoid if j in (MO, MO + 1) else ACT.Copy
                            step(A(PR[:, j, :], src[:, 0:N], f), "bank_read_act")
                    for g, t in tiles_of("in_tok"):
                        tile_ready(g)
                        n = TT[t[1]][1]
                        copy(VT[0:n, t[1], :], ps[0:n, g % GEMM_BANKS, :], "bank_read_act")

                    wait("gla_abs")
                    step(A(g_t3, g_t2, ACT.Exp))
                    step(A(g_t3, g_t3, ACT.Ln, bias=one), "gla_log")
                    wait("gla_cum")
                    step(A(g_eb, g_cum, ACT.Exp, scale=1.0 / 16))
                    step(A(g_enb, g_cum, ACT.Exp, scale=-1.0 / 16))
                    step(A(g_ebe, g_t2, ACT.Exp, scale=1.0 / 16), "gla_exp")
                    wait("gla_o")
                    step(A(SQ[:, 0:2, :], ps[:, 6:8, 0:N], ACT.Square), "gla_sq")
                    step(A(SQ[:, 2:5, :], PR[:, CQ:CQ + 3, :], ACT.Square), "mla_sq")
                    wait("gla_ss")
                    step(A(g_ra, ps[:, 0:2, 0:N], ACT.Ln, bias=eps, scale=1.0 / 64))
                    step(A(g_ra, g_ra, ACT.Exp, scale=-0.5), "gla_r")

                    wait("mla_ss")
                    step(A(m_rr[:, 0, :], ps[:, 2, 0:N], ACT.Ln, bias=eps, scale=1.0 / 256))
                    step(A(m_rr[:, 1, :], ps[:, 3, 0:N], ACT.Ln, bias=eps, scale=1.0 / 128))
                    step(A(m_rr, m_rr, ACT.Exp, scale=-0.5), "mla_r")
                    wait("mla_ql")
                    copy(m_ql, ps[:, 0:4, 0:N], "mla_qlc")
                    for qt in range(2):
                        nk = (qt + 1) * P
                        wait("mla_max", qt + 1)
                        for h in range(4):
                            step(A(m_p[:, h, 0:nk], ps[:, h, 0:nk], ACT.Exp, bias=m_nm[:, h:h + 1], scale=SCALE_MLA,
                                   accum_out=m_sum[:, h:h + 1]), "mla_p" if h == 3 else None)
                        wait("mla_pt", qt + 1)
                        for b in range(qt + 1):
                            copy(m_pt[:, b, :, :], ps[:, 4 + b, :].rearrange("p (h t) -> p h t", h=4),
                                 "mla_ptc" if b == qt else None)
                        wait("mla_ol", qt + 1)
                        copy(m_ol[:, :, qt * P:(qt + 1) * P], ps[:, 6, :].rearrange("p (h t) -> p h t", h=4), "mla_olc")
                    for b in range(NB):
                        wait("mla_max_s", b + 1)
                        step(A(m_ps[:, 0:KEYS], ps[0:16, 0:4, :].rearrange("p a b -> p (a b)"), ACT.Exp,
                               bias=m_nm[0:16, 0:1], scale=SCALE_MLA, accum_out=m_sum[0:16, 0:1]))
                        step(A(m_ps[:, KEYS:KEYS + NS], ps[0:16, 4, 0:NS], ACT.Exp, bias=m_nm[0:16, 0:1],
                               scale=SCALE_MLA, accum_out=m_sum[0:16, 1:2]), "mla_p_s")
                        wait("mla_pt_s", b + 1)
                        copy(m_pts[:, 0:256], ps[:, 5, 0:256])
                        copy(m_pts[0:NS, 256:272], ps[0:NS, 5, 256:272], "mla_ptc_s")
                        wait("mla_ol_s", b + 1)
                        j = TP + b * TS
                        copy(m_ol[:, :, j:j + TS], ps[:, 6, 0:16].rearrange("p (h t) -> p h t", h=4), "mla_olc")
                    wait("mla_o")
                    copy(O[:, 2:4, :], ps[:, 0:2, 0:N], "mla_done")

                    wait("ml_abs")
                    step(A(l_t[0:4, :], l_t[0:4, :], ACT.Exp))
                    step(A(l_t[0:4, :], l_t[0:4, :], ACT.Ln, bias=one[0:4, :]), "ml_log")
                    wait("ml_rows")
                    step(A(l_rows[0:4, :], l_rows[0:4, :], ACT.Exp), "ml_exp")
                    wait("ml_gw")
                    for h in range(4):
                        wait("ml_s", h + 1)
                        for a, b, i, n in ((0, 256, 0, P), (256, 384, 1, P), (384, 416, 2, NS)):
                            step(A(l_w[0:n, h, a:b], ps[0:n, 4 + h % 2, a:b], ACT.Exp, bias=l_gw[0:n, i * 8 + h:i * 8 + h + 1]),
                                 "ml_e" if i == 2 else None)
                    wait("ml_c")
                    step(A(SQ[:, 0:2, :], l_h, ACT.Square), "ml_sq")
                    wait("ml_ss")
                    step(A(l_r, ps[:, 6:8, 0:N], ACT.Ln, bias=eps, scale=1.0 / 64))
                    step(A(l_r, l_r, ACT.Exp, scale=-0.5), "ml_r")

                    wait("rw_pm")
                    step(A(r_tw[0:64, :], SQ[0:64, 6, :], ACT.Tanh))
                    step(A(r_sg, SQ[:, 7, :], ACT.Sigmoid), "rw_tw")
                    wait("rw_lora")
                    for hp in range(2):
                        step(A(r_s[:, hp, :], ps[:, hp, 0:N], ACT.Sigmoid, bias=V("w0", hp)))
                        step(A(r_a[:, hp, :], ps[:, 2 + hp, 0:N], ACT.Sigmoid, bias=V("a0", hp)))
                    copy(r_g, ps[:, 4:6, 0:N], "rw_sig")
                    wait("rw_clamped")
                    step(A(r_t, r_t, ACT.Ln))
                    step(A(r_t, r_t, ACT.Exp, bias=C("kk_b"), scale=-0.5), "rw_inv")
                    wait("rw_cum")
                    step(A(r_rh, r_cs, ACT.Exp, scale=-DECAY))
                    step(A(r_cs, r_cs, ACT.Exp, scale=DECAY))
                    step(A(r_csx, r_csx, ACT.Exp, scale=-DECAY))
                    step(A(r_cse, r_cse, ACT.Exp, scale=-DECAY), "rw_exp")
                    levels = 0
                    uc = 0
                    for i, (c0, n) in enumerate(TT):
                        wait("rw_tok", 2 * i + 1)
                        copy(r_tok[0:n, 0:2, :], ps[0:n, 5, :].rearrange("p (a b) -> p a b", a=2), "rw_tokc")
                        wait("rw_tok", 2 * i + 2)
                        copy(r_tok[0:n, 2:4, :], ps[0:n, 0, :].rearrange("p (a b) -> p a b", a=2), "rw_tokc")
                        for j in range(1, 6 if i < 2 else 2):
                            levels += 1
                            wait("rw_x", levels)
                            copy(r_x[0:n, :, 0:n], ps[0:n, 1, 0:4 * n].rearrange("p (h s) -> p h s", h=4), "rw_xc")
                        wait("rw_bg", i + 1)
                        copy(r_bv[0:n, :], ps[0:n, 4, 0:256])
                        copy(r_gt[:, :, 0:n], ps[:, 5, 0:2 * n].rearrange("p (a b) -> p a b", a=2), "rw_bgc")
                        if i < 2:
                            for c in (2 * i, 2 * i + 1):
                                s = slice(64 * (c % 2), 64 * (c % 2) + 64)
                                wait("rw_u", c + 1)
                                copy(r_u[s, :], ps[s, 0, 0:256], "rw_uc")
                        else:
                            wait("rw_u", 5)
                            copy(r_x[:, 0:2, 0:NS], ps[:, 0, 0:2 * NS].rearrange("p (a b) -> p a b", a=2), "rw_uc")
                            wait("rw_ut")
                            copy(r_u[0:NS, :], ps[0:NS, 1, 0:256], "rw_utok")
                    wait("rw_ds", 5)
                    copy(r_a, ps[:, 6:8, 0:N], "rw_yc")
                    wait("rw_c")
                    step(A(r_t, r_a, ACT.Square), "rw_sq")
                    wait("rw_ss")
                    step(A(r_s, ps[:, 4:6, 0:N], ACT.Ln, bias=eps_r, scale=1.0 / 64))
                    step(A(r_s, r_s, ACT.Exp, scale=-0.5), "rw_r")

                    for g, t in tiles_of("gate"):
                        d, n = t[1]
                        if d >= 1:
                            wait("bank_read_dve", 4 * (d - 1) + n + 1)
                        tile_ready(g)
                        step(A(SQ[:, n, :], ps[:, g % GEMM_BANKS, 0:N], ACT.Sigmoid), "bank_read_act")

                    wait("load_mem", 16)
                    wait("mixed", KD)
                    squares("mem", c_mem, MEM)
                    rstd("mem", MEM)
                    for g, t in tiles_of("mem_k"):
                        tile_ready(g)
                        copy(c_mkt[:, t[1], :], ps[:, g % GEMM_BANKS, 0:MEM], "bank_read_act")
                    for g, t in tiles_of("mem_v"):
                        half, tok = t[1]
                        tile_ready(g)
                        copy(c_mv[:, tok, half * 512:(half + 1) * 512], ps[:, g % GEMM_BANKS, :], "bank_read_act")

                    def into(stage, dst):
                        for g, t in tiles_of(stage):
                            tile_ready(g)
                            copy(dst[:, t[1], :], ps[:, g % GEMM_BANKS, 0:N], "bank_read_act")

                    into("out", O)
                    squares("post_mix", O[:, :, :])
                    rstd("post_mix")

                    wait("post_mix_done")
                    squares("pre_ca", X[:, :, :])
                    rstd("pre_ca")
                    into("ca_q", O)
                    for qt in range(2):
                        wait("ca_max", qt + 1)
                        for h in range(4):
                            step(A(c_p[:, h, :], ps[:, h, 0:MEM], ACT.Exp, bias=c_nm[:, h:h + 1], scale=SCALE_CA,
                                   accum_out=c_sum[:, h:h + 1]), "ca_p" if h == 3 else None)
                        wait("ca_pt", qt + 1)
                        copy(c_pt, ps[:, 4:6, :].rearrange("p b (h t) -> p b h t", h=4), "ca_ptc")
                        wait("ca_o", qt + 1)
                        copy(H[:, :, qt * P:(qt + 1) * P].rearrange("p (a d) t -> p a d t", a=2),
                             ps[:, 6:8, :].rearrange("p a (d t) -> p a d t", d=4), "ca_oc")
                    for b in range(NB):
                        wait("ca_max_s", b + 1)
                        step(A(c_ps, ps[:, 0, 0:MEM], ACT.Exp, bias=c_nm[:, 0:1], scale=SCALE_CA,
                               accum_out=c_sum[:, 0:1]), "ca_p_s")
                        wait("ca_pt_s", b + 1)
                        copy(c_pts, ps[:, 1, 0:256].rearrange("p (b t) -> p b t", b=2), "ca_ptc_s")
                        wait("ca_o_s", b + 1)
                        j = TP + b * TS
                        copy(H[:, :, j:j + TS], ps[:, 2, 0:8 * TS].rearrange("p (d t) -> p d t", d=8),
                             "ca_oc")
                    into("ca_o", O)
                    squares("post_ca", O[:, :, :])
                    rstd("post_ca")

                    wait("post_ca_done")
                    squares("pre_ffn", X[:, :, :])
                    rstd("pre_ffn")
                    wait("conv_halo", 2)
                    a_tiles = tiles_of("ffn_a")
                    for k in range(KF + 1):
                        if k < KF:
                            g, t = a_tiles[k]
                            tile_ready(g)
                            if k >= 2:
                                wait("conv_state", k - 1)
                            step(A(f_a[:, k % 2, 2:2 + TP], ps[:, g % GEMM_BANKS, 0:TP], ACT.Copy))
                            copy(per_batch(f_a[:, k % 2, 2 + TP:EXC], 2 + TS)[:, :, 2:2 + TS],
                                 per_batch(ps[:, g % GEMM_BANKS, TP:N], TS), "bank_read_act")
                        if k >= 1:
                            wait("conv", k)
                            step(A(f_c[:, (k - 1) % 2, :], f_c[:, (k - 1) % 2, :], ACT.Gelu), "gelu")
                    into("down", O)
                    squares("post_ffn", O[:, :, :])
                    rstd("post_ffn")

                @block.vector
                def _(dve):
                    step = Steps(dve, "dve_step")
                    v = nc.vector

                    def wait(name, n=1):
                        dve.wait_ge(*at(name, n))

                    def tt(out, a, b, op, signal=None):
                        step(v.tensor_tensor(out, a, b, op), signal)

                    def ts(out, a, s1, s2, op0, op1=None, signal=None):
                        if op1 is None:
                            step(v.tensor_scalar(out, a, s1, None, op0), signal)
                        else:
                            step(v.tensor_scalar(out, a, s1, s2, op0, op1), signal)

                    def stt(out, a, s, b, op0, op1, signal=None):
                        step(v.scalar_tensor_tensor(out, a, s, b, op0, op1), signal)

                    def copy(out, in_, signal=None):
                        step(v.tensor_copy(out, in_), signal)

                    def fill(out, value, signal=None):
                        step(v.memset(out, value), signal)

                    MUL, ADD, SUB, MAX, MIN = ALU.mult, ALU.add, ALU.subtract, ALU.max, ALU.min

                    def normed(name, dst, src, width=N):
                        wait(name + "_rstd")
                        for k in range(KD):
                            stt(dst[:, k, :], src[:, k, :], V(name, k), RS[:, 0:width], MUL, MUL,
                                name + "_done" if k == KD - 1 else None)

                    def residual(name):
                        wait(name + "_rstd")
                        for k in range(KD):
                            stt(O[:, k, :], O[:, k, :], V(name, k), RS[:, :], MUL, MUL)
                        tt(X[:, :, :], X[:, :, :], O[:, :, :], ADD, name + "_done")

                    wait("load_vec", 16)
                    wait("load_shift", 16)
                    fill(RE[:, :, 0:1], 0.0)
                    copy(RE[:, :, 1 + TP:EXT].rearrange("p a (b t) -> p a b t", t=1 + TS)[:, :, :, 0], r_hs[:, :, :], "halo")
                    normed("pre_mix", H, X)

                    wait("gla_z")
                    ts(g_t1, ps[:, 4, 0:N], V("gla_b"), None, ADD)
                    stt(g_t2, g_t1, -1.0, g_t1, MUL, MIN, "gla_abs")
                    wait("gla_log")
                    stt(g_t2, g_t1, 0.0, g_t3, MIN, SUB)
                    step(v.tensor_tensor_scan(g_cum, C("reset", N), g_t2, 0.0, MUL, ADD))
                    tt(chunks(g_t2), bc(chunks(g_cum)[:, :, CH - 1:CH], [P, NCH, CH]), chunks(g_cum), SUB)
                    tt(smp(g_t2), bc(smp(g_cum)[:, :, TS - 1:TS], [P, NB, TS]), smp(g_cum), SUB, "gla_cum")
                    tt(g_vb.rearrange("p h (b v) -> p h b v", b=NB)[0:NS],
                       VT[0:NS, 2, 0:256].rearrange("p (h o v) -> p h o v", h=4, o=1).broadcast_to([NS, 4, NB, 64]),
                       C("batch", NB, NS).rearrange("p (o b u) -> p o b u", o=1, u=1).broadcast_to([NS, 4, NB, 64]), MUL)
                    wait("gla_exp")
                    stt(g_q, PR[:, GQ, :], 32.0 ** -0.5, g_eb, MUL, MUL)
                    tt(g_k, PR[:, GK, :], g_enb, MUL)
                    tt(g_ke, PR[:, GK, :], g_ebe, MUL, "gla_k")
                    wait("gla_turned")
                    copy(g_ktok[:, 0:2, :], ps[:, 3, 0:2 * P].rearrange("p (a b) -> p a b", a=2))
                    copy(g_ktok[0:NS, 2, :], ps[0:NS, 3, 2 * P:3 * P], "gla_kt")
                    wait("gla_att")
                    for i, (c0, n) in enumerate(TT):
                        m = C("upper", P) if i < 2 else C("upper_s", NS, NS)
                        tt(g_att[0:n, i, 0:4 * n].rearrange("p (h t) -> p h t", h=4),
                           ps[0:n, i, 0:4 * n].rearrange("p (h t) -> p h t", h=4),
                           m.rearrange("p (o t) -> p o t", o=1).broadcast_to([n, 4, n]), MUL, "gla_attm" if i == 2 else None)
                    wait("gla_ds")
                    wait("load_gla", 16)
                    copy(g_st[:, 1, :], ps[:, 4, 0:64])
                    for c in range(1, NCH):
                        e = (c + 1) * CH - 1
                        stt(g_st[:, c + 1, :], g_st[:, c, :], g_eb[:, e:e + 1], ps[:, 4, c * 64:(c + 1) * 64], MUL, ADD)
                    tt(g_s1, g_s0, bc(smp(g_eb)[:, :, TS - 1:TS], [P, NB, 64]), MUL)
                    tt(g_s1, g_s1, ps[:, 5, :].rearrange("p (b v) -> p b v", b=NB), ADD, "gla_state")
                    wait("gla_r")
                    stt(O[:, 0:2, :], ps[:, 6:8, 0:N], V("gla_norm"), g_ra, MUL, MUL)
                    tt(O[:, 0:2, :], O[:, 0:2, :], PR[:, GR:GR + 2, :], MUL, "gla_done")

                    wait("mla_r")
                    wait("stores", 32)
                    for j in range(2):
                        stt(m_cqn[:, j, :], PR[:, CQ + j, :], V("norm_q", j), m_rr[:, 0, :], MUL, MUL)
                    stt(m_ck, PR[:, CKV, :], V("norm_kv"), m_rr[:, 1, :], MUL, MUL)
                    tt(m_ta[0:32, :], PR[64:96, MIX1, :], C("cos", N, 32, 64), MUL)
                    tt(m_tb[0:32, :], PR[96:128, MIX1, :], C("sin", N, 32, 96), MUL)
                    tt(m_kp[0:32, :], m_ta[0:32, :], m_tb[0:32, :], ADD)
                    for r in (32, 64, 96):
                        copy(m_kp[r:r + 32, :], m_kp[0:32, :], "mla_norm" if r == 96 else None)
                    wait("mla_q")
                    copy(m_qn, ps[:, 2:4, 0:N])
                    tt(m_ta, ps[:, 4, 0:N], C("cos", N), MUL)
                    tt(m_tb, ps[:, 5, 0:N], C("sin", N), MUL)
                    tt(m_qp, m_ta, m_tb, ADD)
                    copy(m_cktok[:, 0:2, :], ps[:, 6, 0:2 * P].rearrange("p (a b) -> p a b", a=2))
                    copy(m_cktok[0:NS, 2, :], ps[0:NS, 6, 2 * P:3 * P], "mla_qn")
                    for h in range(4):
                        copy(m_qps[0:32, :, h * TS:(h + 1) * TS], smp(m_qp)[32 * h:32 * h + 32])
                    for r in (32, 64, 96):
                        copy(m_qps[r:r + 32], m_qps[0:32])
                    wait("mla_qlc")
                    for h in range(4):
                        copy(m_qls[:, :, h * TS:(h + 1) * TS], smp(m_ql[:, h, :]), "mla_qs" if h == 3 else None)
                    for qt in range(2):
                        nk = (qt + 1) * P
                        wait("mla_s", qt + 1)
                        step(v.tensor_reduce(m_mx[:, :], ps[:, 0:4, 0:nk], AX.X, MAX))
                        ts(m_nm, m_mx, -SCALE_MLA, None, MUL, signal="mla_max")
                        wait("mla_p", qt + 1)
                        step(v.reciprocal(m_rec, m_sum))
                        tt(m_p[:, :, 0:nk], m_p[:, :, 0:nk],
                           m_rec.rearrange("p (h o) -> p h o", o=1).broadcast_to([P, 4, nk]), MUL, "mla_pn")
                    for b in range(NB):
                        wait("mla_ss_s", b + 1)
                        step(v.tensor_reduce(m_mx[0:16, 0:1], ps[0:16, 0:4, :].rearrange("p a b -> p (a b)"), AX.X, MAX))
                        step(v.tensor_reduce(m_mx[0:16, 1:2], ps[0:16, 4, 0:NS], AX.X, MAX))
                        tt(m_mx[0:16, 2:3], m_mx[0:16, 0:1], m_mx[0:16, 1:2], MAX)
                        ts(m_nm[0:16, 0:1], m_mx[0:16, 2:3], -SCALE_MLA, None, MUL, signal="mla_max_s")
                        wait("mla_p_s", b + 1)
                        tt(m_rec[0:16, 0:1], m_sum[0:16, 0:1], m_sum[0:16, 1:2], ADD)
                        step(v.reciprocal(m_rec[0:16, 1:2], m_rec[0:16, 0:1]))
                        ts(m_diag[0:16, :], ident[0:16, 0:16], m_rec[0:16, 1:2], None, MUL, signal="mla_d_s")

                    wait("mla_done")
                    wait("load_ml", 48)
                    ts(l_x[0:4, :], PR[0:4, MIX2, :], V("f_bias", 0, 4), None, ADD)
                    stt(l_t[0:4, :], l_x[0:4, :], -1.0, l_x[0:4, :], MUL, MIN, "ml_abs")
                    fill(l_fe[0:4, :], NEG)
                    fill(l_ie[0:4, :], 0.0)
                    ts(ext_prompt(l_ie[0:4]), PR[0:4, MIX1, 0:TP], V("i_bias", 0, 4), None, ADD)
                    ts(ext_sample(l_ie[0:4]), smp(PR[0:4, MIX1, :]), V("i_bias", 0, 4), None, ADD)
                    copy(per_batch(l_ie[0:4, 1 + TP:EXT], 1 + TS)[:, :, 0:1], l_m0[0:4, :].rearrange("p (b o) -> p b o", o=1))
                    wait("ml_log")
                    stt(l_x[0:4, :], l_x[0:4, :], 0.0, l_t[0:4, :], MIN, SUB)
                    copy(ext_prompt(l_fe[0:4]), l_x[0:4, 0:TP])
                    copy(ext_sample(l_fe[0:4]), smp(l_x[0:4]))
                    step(v.tensor_tensor_scan(l_me[0:4, :], l_fe[0:4, :], l_ie[0:4, :], 0.0, ADD, MAX))
                    step(v.tensor_tensor_scan(l_b[0:4, :], C("reset_m", N, 4), l_x[0:4, :], 0.0, MUL, ADD))
                    tt(l_nm[0:4, 0:TP], l_b[0:4, 0:TP], ext_prompt(l_me[0:4]), SUB)
                    tt(smp(l_nm[0:4]), smp(l_b[0:4]), ext_sample(l_me[0:4]), SUB)
                    tt(l_g[0:4, 0:TP], ext_prompt(l_ie[0:4]), l_b[0:4, 0:TP], SUB)
                    tt(smp(l_g[0:4]), ext_sample(l_ie[0:4]), smp(l_b[0:4]), SUB)
                    rows = l_rows[0:4]
                    tt(rows[:, L_EM:L_EM + N], l_nm[0:4, :], l_b[0:4, :], SUB)
                    m0 = l_m0[0:4, :].rearrange("p (b o) -> p b o", o=1)
                    tt(per_batch(rows[:, L_WI:L_WI + NS], TS), smp(l_nm[0:4]), bc(m0, [4, NB, TS]), ADD)
                    ts(rows[:, L_WE:L_WE + TP], l_g[0:4, 0:TP], l_nm[0:4, TP - 1:TP], None, ADD)
                    nm_end = smp(l_nm[0:4])[:, :, TS - 1:TS]
                    tt(per_batch(rows[:, L_WE + TP:L_WE + N], TS), smp(l_g[0:4]), bc(nm_end, [4, NB, TS]), ADD)
                    copy(l_mo[0:4, 0:1], l_me[0:4, TP:TP + 1])
                    copy(l_mo[0:4, 1:1 + NB].rearrange("p (b o) -> p b o", o=1), ext_sample(l_me[0:4])[:, :, TS - 1:TS])
                    tt(rows[:, L_SO:L_SO + NB].rearrange("p (b o) -> p b o", o=1), m0, nm_end, ADD, "ml_rows")
                    tt(l_vb.rearrange("p h (b v) -> p h b v", b=NB)[0:NS],
                       VT[0:NS, 2, 256:512].rearrange("p (h o v) -> p h o v", h=4, o=1).broadcast_to([NS, 4, NB, 64]),
                       C("batch", NB, NS).rearrange("p (o b u) -> p o b u", o=1, u=1).broadcast_to([NS, 4, NB, 64]), MUL)
                    copy(l_nbc, l_n0.rearrange("p a (b o) -> p a b o", o=1).broadcast_to([P, 2, NB, 64]))
                    wait("ml_turned")
                    copy(l_gw[:, 0:16], ps[:, 0, 0:16])
                    copy(l_gw[0:NS, 16:24], ps[0:NS, 0, 16:24], "ml_gw")
                    for i, (c0, n) in enumerate(TT):
                        c = i % 2 * 256
                        tt(l_kw[0:n, i, :].rearrange("p (h k) -> p h k", h=4),
                           ps[0:n, 4 + i // 2, c:c + 256].rearrange("p (h k) -> p h k", h=4),
                           l_gw[0:n, i * 8 + 4:i * 8 + 8].rearrange("p (h o) -> p h o", o=1).broadcast_to([n, 4, 64]), MUL)
                    stt(l_qw, ps[:, 3, 0:2 * NS].rearrange("p (a b) -> p a b", a=2), 0.125, PR[:, MQ:MQ + 2, TP:N], MUL, MUL)
                    copy(l_so, ps[:, 3, 64:64 + 2 * NB].rearrange("p (a b) -> p a b", a=2), "ml_k")
                    for h in range(4):
                        wait("ml_e", h + 1)
                        qk = ps[:, 6 + h % 2, :]
                        stt(l_w[:, h, 0:384], qk[:, 0:384], 0.125, l_w[:, h, 0:384], MUL, MUL)
                        stt(l_w[0:NS, h, 384:416], qk[0:NS, 384:416], 0.125, l_w[0:NS, h, 384:416], MUL, MUL, "ml_w")
                    wait("ml_num")
                    copy(l_h, ps[:, 1:3, 0:N])
                    copy(l_den, ps[:, 6:8, 0:N])
                    stt(l_den, l_den, -1.0, l_den, MUL, MAX)
                    tt(l_den, l_den, l_h, MAX)
                    step(v.reciprocal(l_den, l_den))
                    tt(l_h, ps[:, 4:6, 0:N], l_den, MUL, "ml_h")
                    wait("ml_mean")
                    stt(l_h, ps[:, 4:6, 0:N], -1.0 / 64, l_h, MUL, ADD, "ml_c")
                    wait("ml_ds")
                    for hp in range(2):
                        c0 = l_c0[:, hp, :].rearrange("p (b v) -> p b v", b=NB)
                        tt(c0, c0, l_so[:, hp, :].rearrange("p (b o) -> p b o", o=1).broadcast_to([P, NB, 64]), MUL)
                        tt(l_c0[:, hp, :], l_c0[:, hp, :], ps[:, 1 + hp, :], ADD)
                    tt(l_n0, l_n0, l_so, MUL)
                    tt(l_n0, l_n0, ps[:, 3, 136:136 + 2 * NB].rearrange("p (a b) -> p a b", a=2), ADD)
                    copy(l_cp, ps[:, 3, 0:P].rearrange("p (a b) -> p a b", a=2))
                    copy(l_np, ps[:, 3, P:P + 2], "ml_state")
                    wait("ml_r")
                    for hp in range(2):
                        stt(l_h[:, hp, :], l_h[:, hp, :], V("ml_norm", hp), l_r[:, hp, :], MUL, MUL)
                    tt(O[:, 6:8, :], l_h, PR[:, MO:MO + 2, :], MUL, "ml_done")

                    wait("stores_ml", 80)
                    tt(r_d, RE[:, :, 0:EXT - 1], RE[:, :, 1:EXT], SUB)
                    for j in range(8):
                        stt(SQ[:, j, 0:TP], r_d[:, j, 0:TP], V("mu", j), ext_prompt(RE[:, j, :]), MUL, ADD)
                        stt(smp(SQ[:, j, :]), per_batch(r_d[:, j, TP:EXT - 1], 1 + TS)[:, :, 1:1 + TS], V("mu", j), ext_sample(RE[:, j, :]), MUL, ADD,
                            "rw_pm" if j == 7 else None)
                    copy(r_sh[:, :, 0:1], RE[:, :, TP:TP + 1])
                    copy(r_sh[:, :, 1:1 + NB], RE[:, :, 1 + TP:EXT].rearrange("p a (b t) -> p a b t", t=1 + TS)[:, :, :, TS])
                    rr, rk, rv = SQ[:, 0:2, :], SQ[:, 2:4, :], SQ[:, 4:6, :]
                    for hp in range(2):
                        ts(r_kk[:, hp, :], rk[:, hp, :], V("k_k", hp), None, MUL)
                    tt(r_t, r_kk, r_kk, MUL, "rw_kk")
                    wait("rw_kks")
                    ts(r_t, ps[:, 6:8, 0:N], 1e-24, 2.0 ** 20, MAX, MUL, "rw_clamped")
                    wait("rw_sig")
                    for hp in range(2):
                        step(v.tensor_tensor_scan(r_cs[:, hp, :], C("reset", N), r_s[:, hp, :], 0.0, MUL, ADD))
                    tt(r_csx, r_cs, r_s, SUB)
                    for hp in range(2):
                        a, b = r_cse[:, hp, :], r_cs[:, hp, :]
                        tt(chunks(a), bc(chunks(b)[:, :, CH - 1:CH], [P, NCH, CH]), chunks(b), SUB)
                        tt(smp(a), bc(smp(b)[:, :, TS - 1:TS], [P, NB, TS]), smp(b), SUB, "rw_cum" if hp == 1 else None)
                    wait("rw_inv")
                    tt(r_kk, r_kk, r_t, MUL)
                    tt(r_ka, r_kk, r_a, MUL)
                    for hp in range(2):
                        ts(r_t[:, hp, :], r_a[:, hp, :], 1.0, V("k_a", hp), SUB, MUL)
                    stt(r_rk, r_t, 1.0, rk, ADD, MUL)
                    for hp in range(2):
                        stt(r_bo[:, hp, :], rr[:, hp, :], V("r_k", hp), r_rk[:, hp, :], MUL, MUL)
                    wait("rw_exp")
                    tt(r_al, r_kk, r_csx, MUL)
                    stt(r_be, r_ka, -1.0, r_cs, MUL, MUL)
                    stt(r_kk, r_ka, -1.0, r_cse, MUL, MUL)
                    tt(r_csx, r_rk, r_cs, MUL)
                    tt(r_cs, r_rk, r_cse, MUL)
                    copy(r_rk, r_csx)
                    copy(r_s, r_rh)
                    tt(r_rh, rr, r_rh, MUL, "rw_vec")
                    wait("rw_bonus")
                    tt(r_bo, ps[:, 6:8, 0:N], rv, MUL, "rw_bo")
                    levels = 0
                    for i, (c0, n) in enumerate(TT):
                        def heads(a):
                            return a.rearrange("p (h t) -> p h t", h=4)

                        def bank(j):
                            return heads(ps[0:n, j, 0:4 * n])

                        def mask(name, j=0):
                            o = CON[name] + j * P
                            return con[0:n, o:o + n].rearrange("p (o t) -> p o t", o=1).broadcast_to([n, 4, n])

                        tm, tr, ato = r_tm[0:n, :, 0:n], r_tt[0:n, :, 0:n], r_at[0:n, :, 0:n]
                        wait("rw_pair", i + 1)
                        sfx = "" if i < 2 else "_s"
                        tt(ato, bank(0), mask("strict" + sfx), MUL)
                        tt(tr, ato, mask("level"), MUL)
                        tt(tr, tr, mask("ident"), ADD)
                        tt(tm, bank(1), mask("level0"), MUL)
                        tt(tm, tm, mask("ident"), ADD)
                        tt(r_bt[0:n, :, 0:n], bank(2), mask("strict" + sfx), MUL)
                        tt(r_rb[0:n, :, 0:n], bank(3), mask("upper" + sfx), MUL)
                        tt(r_rkm[0:n, :, 0:n], bank(4), mask("upper" + sfx), MUL, "rw_pairm")
                        for j in range(1, 6 if i < 2 else 2):
                            levels += 1
                            tt(r_off[0:n, :, 0:n], ato, mask("level", j), MUL, "rw_off")
                            wait("rw_y", levels)
                            tt(tm, tm, bank(2), ADD)
                            tt(tr, tr, bank(3), ADD, "rw_t")
                        if i < 2:
                            for c in (2 * i, 2 * i + 1):
                                e = (c + 1) * CH - 1
                                wait("rw_ds", c + 1)
                                for hp in range(2):
                                    src = ps[:, 1, hp * 64:(hp + 1) * 64]
                                    sig = "rw_st" if hp else None
                                    if c:
                                        stt(r_st[:, hp, :], r_st[:, hp, :], r_s[:, hp, e:e + 1], src, MUL, ADD, sig)
                                    else:
                                        copy(r_st[:, hp, :], src, sig)
                        else:
                            def spread(out, src, signal=None):
                                tt(out.rearrange("p h (b v) -> p h b v", b=NB)[0:NS],
                                   src.rearrange("p (h o v) -> p h o v", h=4, o=1).broadcast_to([NS, 4, NB, 64]),
                                   C("batch", NB, NS).rearrange("p (o b u) -> p o b u", o=1, u=1)
                                   .broadcast_to([NS, 4, NB, 64]), MUL, signal)
                            wait("rw_tokc", 6)
                            spread(r_vb, r_tok[0:NS, 3, :])
                            wait("rw_utok")
                            spread(r_ub, r_u[0:NS, :], "rw_utc")
                            wait("rw_ds", 5)
                            for hp in range(2):
                                s0 = r_s0[:, hp, :].rearrange("p (b v) -> p b v", b=NB)
                                tt(s0, s0, bc(smp(r_s[:, hp, :])[:, :, TS - 1:TS], [P, NB, 64]), MUL)
                                tt(r_s0[:, hp, :], r_s0[:, hp, :], ps[:, 2 + hp, :], ADD, "rw_state" if hp else None)
                    wait("rw_mean")
                    stt(r_a, ps[:, 0:2, 0:N], -1.0 / 64, r_a, MUL, ADD, "rw_c")
                    wait("rw_r")
                    for hp in range(2):
                        stt(r_t[:, hp, :], r_a[:, hp, :], V("ln_w", hp), r_s[:, hp, :], MUL, MUL)
                        stt(r_t[:, hp, :], r_t[:, hp, :], V("ln_b", hp), r_bo[:, hp, :], ADD, ADD)
                    tt(O[:, 4:6, :], r_t, r_g, MUL, "rw_done")

                    for g, t in tiles_of("up"):
                        d, n = t[1]
                        wait("gemm_done", g + 1)
                        wait("bank_read_act", READ_NO[g - 1])
                        dst = PR[:, d, :] if n == 0 else RS[:, :]
                        tt(dst, ps[:, g % GEMM_BANKS, 0:N], SQ[:, n, :], MUL, "bank_read_dve")
                        if n:
                            tt(PR[:, d, :], PR[:, d, :], RS[:, :], ADD, "mixed" if n == 3 else None)

                    normed("mem", c_mem, c_mem, MEM)
                    residual("post_mix")
                    normed("pre_ca", H, X)

                    for qt in range(2):
                        wait("ca_s", qt + 1)
                        step(v.tensor_reduce(c_mx[:, :], ps[:, 0:4, 0:MEM], AX.X, MAX))
                        ts(c_nm, c_mx, -SCALE_CA, None, MUL, signal="ca_max")
                        wait("ca_p", qt + 1)
                        step(v.reciprocal(c_rec, c_sum))
                        tt(c_p, c_p, c_rec.rearrange("p (h o) -> p h o", o=1).broadcast_to([P, 4, MEM]), MUL, "ca_pn")
                    for b in range(NB):
                        wait("ca_ss_s", b + 1)
                        step(v.tensor_reduce(c_mx[:, 0:1], ps[:, 0, 0:MEM], AX.X, MAX))
                        ts(c_nm[:, 0:1], c_mx[:, 0:1], -SCALE_CA, None, MUL, signal="ca_max_s")
                        wait("ca_p_s", b + 1)
                        step(v.reciprocal(c_rec[:, 0:1], c_sum[:, 0:1]))
                        ts(c_ps, c_ps, c_rec[:, 0:1], None, MUL, signal="ca_pn_s")
                    residual("post_ca")
                    normed("pre_ffn", H, X)

                    wait("load_conv", 16)
                    wait("ca_oc", 2 + NB)
                    for i in range(2):
                        fill(f_a[:, i, 0:2], 0.0, "conv_halo")
                    g_tiles = tiles_of("ffn_g")
                    for k in range(KF + 1):
                        if k < KF:
                            a = f_a[:, k % 2, :]
                            copy(per_batch(a[:, 2 + TP:EXC], 2 + TS)[:, :, 0:2], per_batch(f_s[:, k, :], 2))
                            wait("bank_read_act", READ_NO[tiles_of("ffn_a")[k][0]])
                            c = f_c[:, k % 2, :]
                            w = [V("conv_w", 3 * k + j) for j in range(3)]
                            ts(c, a[:, 0:EXC - 2], w[0], V("conv_b", k), MUL, ADD)
                            stt(c, a[:, 1:EXC - 1], w[1], c, MUL, ADD)
                            stt(c, a[:, 2:EXC], w[2], c, MUL, ADD, "conv")
                            copy(f_o[:, k, 0:2], a[:, TP:TP + 2])
                            copy(per_batch(f_o[:, k, 2:2 + 2 * NB], 2), per_batch(a[:, 2 + TP:EXC], 2 + TS)[:, :, TS:TS + 2],
                                 "conv_state")
                        if k >= 1:
                            j = k - 1
                            g, t = g_tiles[j]
                            wait("gelu", k)
                            wait("gemm_done", g + 1)
                            c, src = f_c[:, j % 2, :], ps[:, g % GEMM_BANKS, :]
                            tt(f_f[:, j, 0:TP], c[:, 0:TP], src[:, 0:TP], MUL)
                            tt(smp(f_f[:, j, :]), per_batch(c[:, TP:EXC - 2], 2 + TS)[:, :, 2:2 + TS],
                               per_batch(src[:, TP:N], TS), MUL, "bank_read_dve")
                    residual("post_ffn")

            with nc.Block() as block:
                @block.gpsimd
                def _(pool):
                    pool.dma_reset()
                    for name in sorted(sems):
                        if name != "load_once":
                            pool.sem_clear(sems[name])

        with nc.Block() as block:
            @block.sync
            def _(sp):
                sp.dma_start(t_out["y"], X[:, :, :]).then_inc(S("store_y"), 16)
                sp.wait_ge(S("store_y"), 16)


OUT = {
    "y": (P, KD, N), "ckv": (L, P, N), "kpe": (L, 32, N), "mem_kt": (L, P, KD, MEM), "mem_v": (L, P, 2, D),
    "gla_p": (L, P, 64), "gla_s": (L, P, NB, 64), "rwkv_p": (L, P, 2, 64), "rwkv_s": (L, P, 2, NB * 64),
    "shift_ps": (L, P, 8, 1 + NB), "ml_c_p": (L, P, 2, 64), "ml_c_s": (L, P, 2, NB * 64), "ml_n_p": (L, P, 2),
    "ml_n_s": (L, P, 2, NB), "ml_m_ps": (L, 4, 1 + NB), "conv_ps": (L, P, KF, 2 * (1 + NB)),
}


def constants():
    c = np.zeros((P, NCON), np.float32)

    def put(name, a):
        c[:a.shape[0], CON[name]:CON[name] + a.shape[1]] = a

    i = np.arange(P)
    row, col = i[:, None], i[None, :]
    put("ident", np.eye(P))
    put("ones", np.ones((P, P)))
    put("blk64", (row // 64 == col // 64) * 1.0)
    same, r4, c4 = row // CH == col // CH, row[:NS], col[:, :NS]
    put("upper", (same & (row <= col)) * 1.0)
    put("strict", (same & (row < col)) * 1.0)
    same4 = r4 // TS == c4 // TS
    put("upper_s", (same4 & (r4 <= c4)) * 1.0)
    put("strict_s", (same4 & (r4 < c4)) * 1.0)
    for j in range(6):
        s = 1 << j
        later = (row // (2 * s) == col // (2 * s)) & (row // s % 2 == 0) & (col // s % 2 == 1)
        c[:, CON["level"] + j * P:CON["level"] + (j + 1) * P] = later
        if j == 0:
            put("level0", later.T * 1.0)
    put("bias_tok", np.where(col <= row, 0.0, NEG))
    m = np.zeros((P, 416))
    m[:, 0:128] = m[:, 256:384] = np.where(row <= col, 0.0, NEG)
    m[:NS, 384:416] = np.where(same4 & (r4 <= c4), 0.0, NEG)
    put("bias_m", m)
    t, b, k = np.arange(16)[:, None, None] % TS, np.arange(NB)[None, :, None], np.arange(NS)[None, None, :]
    put("bias_own", np.where((k // TS == b) & (k % TS <= t), 0.0, NEG).reshape(16, NB * NS))
    for h in range(4):
        c[h, CON["sel_h"] + h * P:CON["sel_h"] + (h + 1) * P] = 1
        at = CON["sel_p"] + h // 2 * P + h % 2 * 64
        c[h, at:at + 64] = 1
    put("batch", (np.arange(NS)[:, None] // TS == np.arange(NB)[None, :]) * 1.0)
    half = 16
    freq = (np.float32(10000.0) ** (-np.arange(half, dtype=np.float32) / np.float32(half))).astype(np.float32)
    pos = np.concatenate([np.arange(TP), PAGES * PAGE + np.arange(NS) % TS]).astype(np.float32)
    ang = (pos[None, :] * freq[:, None]).astype(np.float32).astype(np.float64)
    put("cos", np.tile(np.cos(ang), (8, 1)))
    put("sin", np.tile(np.concatenate([-np.sin(ang), np.sin(ang)]), (4, 1)))
    first = np.r_[np.arange(TP) % CH == 0, np.arange(NS) % TS == 0]
    put("reset", np.tile(1.0 - first, (P, 1)))
    first[1:TP] = False
    put("reset_m", np.tile(1.0 - first, (P, 1)))
    for name, value in (("eps", 1e-6), ("eps_r", 64e-5), ("one", 1.0), ("kk_b", 10 * np.log(2.0))):
        put(name, np.full((P, 1), value))
    return c


def col(a, n):
    return np.moveaxis(a.reshape(a.shape[:-1] + (n, P)), -2, -1)


def blocks(w, order="j"):
    k, m = w.shape
    return w.reshape(k // P, P, m // P, P).transpose(2, 0, 1, 3).reshape(-1, P, P)


def wide(w):
    k, m = w.shape
    return w.reshape(k // P, P, m // 512, 4, P).transpose(2, 0, 3, 1, 4).reshape(-1, P, P)


def stream(i, l):
    w = i["w_in"][l]
    z = lambda n: np.zeros((D, n), np.float32)
    o_mla, o_rw, o_ml, o_g = 784, 1200, 2224, 3256
    kr = w[:, o_mla + 384:o_mla + 416]
    mix1 = np.concatenate([w[:, o_ml + 768:o_ml + 772], z(28), w[:, 512:528], z(16), kr, kr[:, 16:], kr[:, :16]], 1)
    mix2 = np.concatenate([w[:, o_ml + 772:o_ml + 776], z(124)], 1)
    feat = np.concatenate([w[:, 0:256], w[:, 528:784], w[:, o_mla:o_mla + 384], mix1, mix2, w[:, o_ml:o_ml + 512],
                           w[:, o_ml + 776:o_ml + 1032], w[:, o_rw:o_rw + 1024]], 1)
    tok = np.concatenate([w[:, 256:512], w[:, o_ml + 512:o_ml + 768]], 1)
    parts = [blocks(feat)]
    parts.append(np.zeros((-len(parts[0]) % SLOT, P, P), np.float32))
    parts.append(wide(tok))
    gate = blocks(w[:, o_g:]).reshape(4, KD, KD, P, P)
    up = np.stack([blocks(i["w_branch"][l, n]).reshape(KD, 2, P, P) for n in range(4)])
    parts.append(np.concatenate([gate, up], 2).transpose(1, 0, 2, 3, 4).reshape(-1, P, P))
    parts += [blocks(i["ca_w_k"][l]), wide(i["ca_w_v"][l]), blocks(i["w_out"][l]), blocks(i["ca_w_q"][l]),
              blocks(i["ca_w_o"][l])]
    f = blocks(i["ffn_w_up"][l]).reshape(2, KF, KD, P, P)
    parts.append(f.transpose(1, 0, 2, 3, 4).reshape(-1, P, P))
    parts.append(blocks(i["ffn_w_down"][l]))
    s = np.concatenate(parts)
    assert len(s) == NBLOCK, (len(s), NBLOCK)
    s = np.concatenate([s, np.zeros((NSLOT * SLOT - NBLOCK, P, P), np.float32)])
    return s.reshape(NSLOT, SLOT, P, P).transpose(0, 2, 1, 3).reshape(NSLOT, P, SLOT * P)


def kernel(**inputs):
    import concourse.bacc as bacc
    from concourse.bass_utils import run_bass_kernel_spmd

    i = {k: np.asarray(a) for k, a in inputs.items()}
    f32 = np.float32
    a = {"const": constants()}
    x = np.concatenate([i["x_prompt"].reshape(TP, D), i["x_sample"].reshape(NS, D)])
    feat = lambda t: np.ascontiguousarray(t.T.reshape(-1, P, t.shape[0]).transpose(1, 0, 2))
    a["x"] = feat(x)
    a["mem"] = feat(i["mem_prompt"].reshape(MEM, D))
    a["pages"] = np.ascontiguousarray(i["page_table"].reshape(1, NB * PAGES).astype(np.int32))
    a["w"] = np.stack([stream(i, l) for l in range(L)])
    v = np.zeros((L, P, NVEC), f32)

    def vec(name, t):
        v[:, :t.shape[1], VEC[name]:VEC[name] + t.shape[2]] = t

    for name in ("pre_mix", "post_mix", "pre_ca", "post_ca", "pre_ffn", "post_ffn"):
        vec(name, col(i["norm_" + name], KD))
    vec("mem", col(i["ca_norm_mem"], KD))
    vec("mu", col(i["rwkv_mu"], 8))
    for name, src in (("w0", "rwkv_w0"), ("a0", "rwkv_a0"), ("k_k", "rwkv_k_k"), ("k_a", "rwkv_k_a"), ("ln_w", "rwkv_ln_w"),
                      ("ln_b", "rwkv_ln_b"), ("ml_norm", "mlstm_norm"), ("norm_q", "mla_norm_q")):
        vec(name, col(i[src], 2))
    vec("r_k", col(i["rwkv_r_k"].reshape(L, 256), 2))
    vec("gla_norm", np.tile(i["gla_norm"], (1, 2))[:, :, None])
    vec("gla_b", i["gla_b_gate"][:, :, None])
    vec("norm_kv", i["mla_norm_kv"][:, :, None])
    vec("conv_w", i["ffn_conv_w"].reshape(L, 3, KF, P).transpose(0, 3, 2, 1).reshape(L, P, 3 * KF))
    vec("conv_b", col(i["ffn_conv_b"], KF))
    vec("i_bias", i["mlstm_i_bias"][:, :, None])
    vec("f_bias", i["mlstm_f_bias"][:, :, None])
    a["vec"] = v
    m = np.zeros((L, P, NMAT), f32)

    def mat(name, t, r0=0):
        m[:, r0:r0 + t.shape[1], MAT[name]:MAT[name] + t.shape[2]] = t

    mat("gate2", i["gla_w_gate2"], GLO_AT)
    uq = i["mla_w_uq"].reshape(L, 256, 4, 96)
    rope = uq[..., 64:]
    swap = np.concatenate([rope[..., 16:], rope[..., :16]], -1)
    uq = np.concatenate([uq[..., :64].reshape(L, 256, 256), rope.reshape(L, 256, P), swap.reshape(L, 256, P)], -1)
    mat("uq", uq.reshape(L, 2, P, 512).transpose(0, 2, 1, 3).reshape(L, P, 1024))
    mat("uk", i["mla_w_uk"].transpose(0, 1, 3, 2).reshape(L, 2, P, P).transpose(0, 2, 1, 3).reshape(L, P, 256))
    mat("uv", i["mla_w_uv"].transpose(0, 2, 1, 3).reshape(L, P, 256))
    mat("wa", i["rwkv_w2"])
    mat("wa", i["rwkv_a2"], 64)
    mat("g2", i["rwkv_g2"])
    a["mat"] = m
    ckv, kpe = i["cache_ckv"], i["cache_kpe"]
    a["kv"] = np.concatenate([ckv, ckv.transpose(0, 1, 3, 2)], -1)
    a["kpe"] = np.ascontiguousarray(kpe.transpose(0, 1, 3, 2))
    mk = i["cache_mem_k"].reshape(L, NB, MEM, KD, P)
    a["mem_k"] = np.ascontiguousarray(mk.transpose(0, 1, 4, 3, 2))
    a["mem_v"] = np.ascontiguousarray(i["cache_mem_v"].reshape(L, NB, MEM, D))
    a["gla"] = np.ascontiguousarray(i["state_gla"].reshape(L, NB, P, 64).transpose(0, 2, 1, 3))
    two = lambda t: np.ascontiguousarray(t.reshape(L, NB, 2, P, 64).transpose(0, 3, 2, 1, 4).reshape(L, P, 2, NB * 64))
    a["rwkv"] = two(i["state_rwkv"].transpose(0, 1, 2, 4, 3))
    a["shift"] = np.ascontiguousarray(i["state_rwkv_shift"].reshape(L, NB, 8, P).transpose(0, 3, 2, 1))
    a["ml_c"] = two(i["state_mlstm_c"])
    a["ml_n"] = np.ascontiguousarray(i["state_mlstm_n"].reshape(L, NB, 2, P).transpose(0, 3, 2, 1))
    a["ml_m"] = np.ascontiguousarray(i["state_mlstm_m"].transpose(0, 2, 1))
    a["conv"] = np.ascontiguousarray(i["state_conv"].reshape(L, NB, 2, KF, P).transpose(0, 4, 3, 1, 2)
                                     .reshape(L, P, KF, 2 * NB))

    nc = bacc.Bacc("TRN2", target_bir_lowering=False, num_devices=1)
    t_in = {k: nc.dram_tensor("in_" + k, t.shape, mybir.dt.from_np(t.dtype), kind="ExternalInput").ap()
            for k, t in a.items()}
    t_out = {k: nc.dram_tensor("out_" + k, s, F32, kind="ExternalOutput").ap() for k, s in OUT.items()}
    program(nc, t_in, t_out)
    r = run_bass_kernel_spmd(nc, [{"in_" + k: t for k, t in a.items()}], core_ids=[0]).results[0]
    o = {k: r["out_" + k] for k in OUT}

    y = o["y"].transpose(2, 1, 0).reshape(N, D)
    tok = lambda t: t.transpose(0, 2, 1)
    ckv, kpe = tok(o["ckv"]), tok(o["kpe"])
    two = lambda t: t.reshape(L, 2, 64, 2, -1, 64).transpose(0, 4, 3, 1, 2, 5).reshape(L, -1, 4, 64, 64)
    shift = o["shift_ps"].transpose(0, 3, 2, 1).reshape(L, 1 + NB, D)
    rows = lambda t: t.transpose(0, 3, 2, 1).reshape(L, -1, 4, 64)
    conv = o["conv_ps"].transpose(0, 3, 2, 1).reshape(L, 1 + NB, 2, FF)
    mm = tok(o["ml_m_ps"])
    return (y[:TP].reshape(1, TP, D), y[TP:].reshape(NB, TS, D),
            ckv[:, :TP].reshape(L, 1, TP, P), kpe[:, :TP].reshape(L, 1, TP, 32),
            ckv[:, TP:].reshape(L, NB, TS, P), kpe[:, TP:].reshape(L, NB, TS, 32),
            o["mem_kt"].transpose(0, 3, 2, 1).reshape(L, 1, MEM, 4, 256),
            o["mem_v"].transpose(0, 2, 1, 3).reshape(L, 1, MEM, 4, 256),
            o["gla_p"].reshape(L, 1, 4, 32, 64), o["gla_s"].transpose(0, 2, 1, 3).reshape(L, NB, 4, 32, 64),
            two(o["rwkv_p"]).transpose(0, 1, 2, 4, 3), two(o["rwkv_s"]).transpose(0, 1, 2, 4, 3),
            shift[:, :1], shift[:, 1:],
            two(o["ml_c_p"]), two(o["ml_c_s"]),
            rows(o["ml_n_p"].reshape(L, P, 2, 1)), rows(o["ml_n_s"]),
            mm[:, :1], mm[:, 1:], conv[:, :1], conv[:, 1:])
```

```python
from contextlib import ExitStack

import numpy as np

import concourse.bass as bass
from concourse import mybir

F32 = mybir.dt.float32
I32 = mybir.dt.int32
ALU = mybir.AluOpType
ACT = mybir.ActivationFunctionType
AX = mybir.AxisListType

P = 128
D = 1024
KD = D // P
L = 2
TP, NB, TS = 256, 8, 4
NS = NB * TS
N = TP + NS
PAGES, PAGE = 16, 128
KV_SLOTS = 4
POOL = NB * PAGES * 5 // 4
KEYS = PAGES * PAGE
FF = 2816
KF = FF // P
MEM = 256
CH = 64
NCH = TP // CH
TT = [(0, 128), (128, 128), (256, NS)]
EXT = 1 + TP + NB * (1 + TS)
EXC = 2 + TP + NB * (2 + TS)
NEG = -1e30
DECAY = float(np.exp(-0.5))
SCALE_MLA = 96.0 ** -0.5
SCALE_CA = 256.0 ** -0.5

GQ, GK, GR, CQ, CKV, MIX1, MIX2, MQ, MK, MO, RW = 0, 1, 2, 4, 6, 7, 8, 9, 11, 13, 15
NF = 23
I_AT, GLO_AT, KR_AT, KRS_AT = 0, 32, 64, 96

_v, VEC = 0, {}
for _name, _n in (("pre_mix", 8), ("post_mix", 8), ("pre_ca", 8), ("post_ca", 8), ("pre_ffn", 8), ("post_ffn", 8),
                  ("mem", 8), ("mu", 8), ("w0", 2), ("a0", 2), ("k_k", 2), ("k_a", 2), ("r_k", 2), ("ln_w", 2),
                  ("ln_b", 2), ("ml_norm", 2), ("gla_norm", 1), ("gla_b", 1), ("norm_q", 2), ("norm_kv", 1),
                  ("conv_w", 3 * KF), ("conv_b", KF), ("i_bias", 1), ("f_bias", 1)):
    VEC[_name] = _v
    _v += _n
NVEC = _v
_v, MAT = 0, {}
for _name, _n in (("gate2", 128), ("uq", 2 * 512), ("uk", 2 * 128), ("uv", 4 * 64), ("wa", 256), ("g2", 256)):
    MAT[_name] = _v
    _v += _n
NMAT = _v
_v, CON = 0, {}
for _name, _n in (("ident", 128), ("ones", 128), ("blk64", 128), ("upper", 128), ("strict", 128), ("upper_s", NS),
                  ("strict_s", NS), ("level", 6 * 128), ("level0", 128), ("bias_tok", 128), ("bias_m", 416),
                  ("bias_own", 128), ("sum_own", 64), ("mem_own", NB), ("sel_h", 4 * 128), ("sel_p", 2 * 128), ("batch", NB), ("cos", N), ("sin", N),
                  ("reset", N), ("reset_m", N), ("eps", 1), ("eps_r", 1), ("one", 1), ("kk_b", 1)):
    CON[_name] = _v
    _v += _n
NCON = _v

SLOT = 16
RING = 5
ROW = 160
GEMM_BANKS = 4


def plan():
    tiles, at = [], 0

    def add(stage, index, n, reader, hold=False):
        nonlocal at
        tiles.append((stage, index, at, n, reader))
        if not hold:
            at += n

    for j in range(NF):
        add("in", j, KD, "act")
    at += (-at) % SLOT
    for i in range(3):
        add("in_tok", i, 4 * KD, "act", hold=i < 2)
    for d in range(KD):
        for n in range(4):
            add("gate", (d, n), KD, "act")
            add("up", (d, n), 2, "dve")
    for j in range(KD):
        add("mem_k", j, KD, "act")
    for half in range(2):
        add("mem_v", (half, 0), 4 * KD, "act", hold=True)
        add("mem_v", (half, 1), 4 * KD, "act")
    for stage in ("out", "ca_q", "ca_o"):
        for j in range(KD):
            add(stage, j, KD, "act")
    for j in range(KF):
        add("ffn_a", j, KD, "act")
        add("ffn_g", j, KD, "dve")
    for j in range(KD):
        add("down", j, KF, "act")
    return tiles, at


MEM_SQUARES_AT, MEM_SUMS_AT = (2, 3), (3, 3)
TILES, NBLOCK = plan()
NSLOT = -(-NBLOCK // SLOT)
READER = [t[4] for t in TILES]
READ_NO = [READER[:g].count(READER[g]) + 1 for g in range(len(TILES))]


def tiles_of(*stages):
    return [(g, t) for g, t in enumerate(TILES) if t[0] in stages]


def slot_done(s):
    end = min((s + 1) * SLOT, NBLOCK)
    return next(g + 1 for g, t in enumerate(TILES) if t[2] + t[3] >= end and
                not any(u[2] < end and u[2] + u[3] > s * SLOT for u in TILES[g + 1:]))


STAGES = {
    "norm_squares": ("pre_mix_sq", "mem_sq", "post_mix_sq", "pre_ca_sq", "post_ca_sq", "pre_ffn_sq", "post_ffn_sq"),
    "norm_sums": ("pre_mix_ss", "mem_ss", "post_mix_ss", "pre_ca_ss", "post_ca_ss", "pre_ffn_ss", "post_ffn_ss"),
    "norm_scales": ("pre_mix_rstd", "mem_rstd", "post_mix_rstd", "pre_ca_rstd", "post_ca_rstd", "pre_ffn_rstd",
                    "post_ffn_rstd"),
    "norm_applied": ("pre_mix_done", "mem_done", "post_mix_done", "pre_ca_done", "post_ca_done", "pre_ffn_done",
                     "post_ffn_done"),
    "gla_tensor": ("gla_z", "gla_turned", "gla_att", "gla_ds", "gla_o", "gla_ss"),
    "gla_scalar": ("gla_log", "gla_exp", "gla_sq", "gla_r"),
    "gla_vector": ("gla_abs", "gla_cum", "gla_k", "gla_kt", "gla_attm", "gla_state", "gla_done"),
    "mla_tensor": ("mla_ss", "mla_q", "mla_ql", "mla_own", "mla_o"),
    "ca_sample": ("ca_po", "ca_oc_s"),
    "mla_scalar": ("mla_sq", "mla_r", "mla_qlc", "mla_done"),
    "mla_vector": ("mla_norm", "mla_qn", "mla_qs", "mla_own_max"),
    "mlstm_tensor": ("ml_turned", "ml_num", "ml_mean", "ml_ds", "ml_ss"),
    "mlstm_scalar": ("ml_log", "ml_exp", "ml_sq", "ml_r"),
    "mlstm_vector": ("ml_abs", "ml_rows", "ml_gw", "ml_k", "ml_h", "ml_c", "ml_state", "ml_done"),
    "rwkv_tensor": ("rw_lora", "rw_kks", "rw_bonus", "rw_ut", "rw_mean", "rw_ss"),
    "rwkv_scalar": ("rw_tw", "rw_sig", "rw_inv", "rw_exp", "rw_utok", "rw_yc", "rw_sq", "rw_r"),
    "rwkv_vector": ("rw_pm", "rw_kk", "rw_clamped", "rw_cum", "rw_vec", "rw_bo", "rw_utc", "rw_state", "rw_c", "rw_done"),
}
SERIES = {stage: series for series, stages in STAGES.items() for stage in stages}
TIMES = {series: KD if series in ("norm_squares", "norm_applied") else 1 for series in STAGES}
PLACE = {stage: k * TIMES[series] for series, stages in STAGES.items() for k, stage in enumerate(stages)}


def program(nc, t_in, t_out):
    with ExitStack() as ctx:
        def sb(name, shape, dt=F32):
            return ctx.enter_context(nc.sbuf_tensor(name, shape, dt))

        sems = {}

        def S(name):
            name = SERIES.get(name, name)
            if name not in sems:
                sems[name] = ctx.enter_context(nc.semaphore(name))
            return sems[name]

        def at(name, n=1):
            return S(name), n + PLACE.get(name, 0)

        ring = sb("weight_ring", [P, RING, SLOT * P])
        con = sb("constants", [P, NCON])
        mat = sb("small_matrices", [P, NMAT])
        vec = sb("vectors", [P, NVEC])
        pages = sb("pages", [1, NB * PAGES], I32)
        X = sb("x_residual", [P, KD, N])
        H = sb("h_normed", [P, KD, N])
        O = sb("o_branches", [P, KD, N])
        SQ = sb("squares", [P, KD, N])
        PR = sb("projected", [P, RW, N])
        RE = sb("rwkv_projected", [P, 8, EXT])
        VT = sb("values_by_token", [P, 3, 512])
        RS = sb("rstd", [P, N])[:, :]
        r_hs = sb("rwkv_last_rows", [P, 8, NB])
        WORK = 17500
        work = sb("work", [P, WORK])
        ps = ctx.enter_context(nc.psum_tensor("banks", [P, 8, 512], F32))

        def carve(word, *shape):
            n = int(np.prod(shape))
            assert word + n <= WORK, (word, n)
            a = work[:, word:word + n]
            if len(shape) == 2:
                a = a.rearrange("p (a b) -> p a b", a=shape[0])
            elif len(shape) == 3:
                a = a.rearrange("p (a b c) -> p a b c", a=shape[0], b=shape[1])
            return a, word + n

        def C(name, n=None, rows=P, r0=0):
            n = {"ident": P, "ones": P}.get(name, 1) if n is None else n
            return con[r0:r0 + rows, CON[name]:CON[name] + n]

        def V(name, j=0, rows=P):
            return vec[0:rows, VEC[name] + j:VEC[name] + j + 1]

        def M(name, a, b, r0=0, r1=P):
            return mat[r0:r1, MAT[name] + a:MAT[name] + b]

        ident = C("ident")
        eps, eps_r, one = C("eps"), C("eps_r"), C("one")

        kv, w0 = [], 0
        for i in range(KV_SLOTS):
            a, w0 = carve(w0, PAGES, ROW)
            kv.append(a)
        g0 = w0
        g_t1, w0 = carve(g0, N)
        g_t2, w0 = carve(w0, N)
        g_t3, w0 = carve(w0, N)
        g_cum, w0 = carve(w0, N)
        g_eb, w0 = carve(w0, N)
        g_enb, w0 = carve(w0, N)
        g_ebe, w0 = carve(w0, N)
        g_q, w0 = carve(w0, N)
        g_k, w0 = carve(w0, N)
        g_ke, w0 = carve(w0, N)
        g_ktok, w0 = carve(w0, 3, P)
        g_att, w0 = carve(w0, 3, 512)
        sqf = SQ[:, :, :].rearrange("p a b -> p (a b)")
        g_vb = sqf[:, 0:4 * NB * 64].rearrange("p (h n) -> p h n", h=4)
        g_st, w0 = carve(w0, NCH + 1, 64)
        g_ra, w0 = carve(w0, 2, N)
        g_s0, w0 = carve(w0, NB, 64)
        g_s1, _ = carve(g0, NB, 64)
        m_cqn, w0 = carve(g0, 2, N)
        m_qn, w0 = carve(w0, 2, N)
        m_rr, w0 = carve(w0, 2, N)
        m_ta, w0 = carve(w0, N)
        m_tb, w0 = carve(w0, N)
        m_kt, _ = carve(g0, 4, 512)
        m_ck, w0 = carve(w0, N)
        m_cktok, w0 = carve(w0, 3, P)
        m_kp, w0 = carve(w0, N)
        m_qp, w0 = carve(w0, N)
        m_ql, w0 = carve(w0, 4, N)
        m_qz, w0 = carve(w0, 64 * NB + 48)
        m_qpz, w0 = carve(w0, 64 * NB)
        m_ol, w0 = carve(w0, 4, N)
        m_mx, w0 = carve(w0, 4)
        m_nm, w0 = carve(w0, 4)
        m_sum, w0 = carve(w0, 4)
        m_rec, w0 = carve(w0, 4)
        m_top, w0 = carve(w0, NB // 2)
        m_otop, w0 = carve(w0, NB // 2)
        m_p = sqf[:, 0:1024].rearrange("p (h s) -> p h s", h=4)
        m_pt = sqf[:, 1024:2048].rearrange("p (b h t) -> p b h t", b=2, h=4)
        m_ps = sqf[:, 0:512]
        m_pts = sqf[:, 512:1024].rearrange("p (i r) -> p i r", i=4)
        m_own = sqf[:, 1024:1024 + P]
        m_po = sqf[:, 1152:1152 + NS]
        m_pot = sqf[0:NS, 1280:1280 + P]
        m_os = sqf[0:64, 1408:1408 + P]
        m_row = sqf[0:1, 1536:1536 + P]
        m_tops = sqf[0:1, 1664:1664 + NS]
        m_sums = sqf[:, 1700:1702]
        m_recs = sqf[0:64, 1702:1703]
        m_krt = sqf[:, 1792:2304]
        m_kr = [O[:, :, :].rearrange("p a b -> p (a b)")[:, 4 * N + i * 512:4 * N + (i + 1) * 512] for i in range(2)]
        l_x, w0 = carve(0, N)
        l_t, w0 = carve(w0, N)
        l_fe, w0 = carve(w0, EXT)
        l_ie, w0 = carve(w0, EXT)
        l_me, w0 = carve(w0, EXT)
        l_b, w0 = carve(w0, N)
        l_nm, w0 = carve(w0, N)
        l_g, w0 = carve(w0, N)
        L_WE, L_EM, L_WI, L_SO = 0, N, 2 * N, 2 * N + NS
        l_rows, w0 = carve(w0, 2 * N + NS + NB)
        l_mo, w0 = carve(w0, 1 + NB)
        l_m0, w0 = carve(w0, NB)
        l_gw, w0 = carve(w0, 24)
        l_kw, w0 = carve(w0, 3, 256)
        l_w, w0 = carve(w0, 4, 416)
        l_vb, w0 = carve(w0, 4, NB * 64)
        l_c0, w0 = carve(w0, 2, NB * 64)
        l_n0, w0 = carve(w0, 2, NB)
        l_nbc, w0 = carve(w0, 2, NB, 64)
        l_so, w0 = carve(w0, 2, NB)
        l_qw, w0 = carve(w0, 2, NS)
        l_den, w0 = carve(w0, 2, N)
        l_h, w0 = carve(w0, 2, N)
        l_r, w0 = carve(w0, 2, N)
        l_cp, w0 = carve(w0, 2, 64)
        l_np, w0 = carve(w0, 2)
        r_tw, w0 = carve(0, N)
        r_sg, w0 = carve(w0, N)
        r_s, w0 = carve(w0, 2, N)
        r_a, w0 = carve(w0, 2, N)
        r_g, w0 = carve(w0, 2, N)
        r_kk, w0 = carve(w0, 2, N)
        r_t, w0 = carve(w0, 2, N)
        r_cs, w0 = carve(w0, 2, N)
        r_csx, w0 = carve(w0, 2, N)
        r_cse, w0 = carve(w0, 2, N)
        r_rk, w0 = carve(w0, 2, N)
        r_al, w0 = carve(w0, 2, N)
        r_be, w0 = carve(w0, 2, N)
        r_ka, w0 = carve(w0, 2, N)
        r_rh, w0 = carve(w0, 2, N)
        r_bo, w0 = carve(w0, 2, N)
        r_d = work[:, w0 - 5 * 2 * N:w0 - 5 * 2 * N + 8 * (EXT - 1)].rearrange("p (a b) -> p a b", a=8)
        r_tok, w0 = carve(w0, 4, 256)
        r_at, w0 = carve(w0, 4, P)
        r_tm, w0 = carve(w0, 4, P)
        r_tt, w0 = carve(w0, 4, P)
        r_x, w0 = carve(w0, 4, P)
        r_off, w0 = carve(w0, 4, P)
        r_bt, w0 = carve(w0, 4, P)
        r_rb, w0 = carve(w0, 4, P)
        r_rkm, w0 = carve(w0, 4, P)
        r_bv, w0 = carve(w0, 256)
        r_gt, w0 = carve(w0, 2, P)
        r_u, w0 = carve(w0, 256)
        r_st, w0 = carve(w0, 2, 64)
        r_s0, w0 = carve(w0, 2, NB * 64)
        prf = PR[:, :, :].rearrange("p a b -> p (a b)")
        r_ub = prf[:, 0:2048].rearrange("p (h n) -> p h n", h=4)
        r_vb = prf[:, 2048:4096].rearrange("p (h n) -> p h n", h=4)
        r_sh, _ = carve(w0, 8, 1 + NB)
        c_mem, w0 = carve(0, KD, MEM)
        c_mkt, w0 = carve(w0, KD, MEM)
        c_mv, w0 = carve(w0, 2, D)
        c_rs = c_mv[:, 0, 0:MEM]
        c_kv = []
        for i in range(4):
            a, w0 = carve(w0, 2 * D)
            c_kv.append(a)
        c_pts, w0 = carve(w0, NB, 2, P)
        c_mx, w0 = carve(w0, 8)
        c_nm, w0 = carve(w0, 8)
        c_sum, w0 = carve(w0, 8)
        c_rec, w0 = carve(w0, 8)
        c_p = sqf[:, 0:1024].rearrange("p (h s) -> p h s", h=4)
        c_pt = sqf[:, 1024:2048].rearrange("p (b h t) -> p b h t", b=2, h=4)
        c_ps = sqf[:, 0:NB * MEM].rearrange("p (b s) -> p b s", b=NB)
        c_po = sqf[:, NB * MEM:NB * MEM + 256]
        f_f, w0 = carve(0, KF, N)
        f_a, w0 = carve(w0, 2, EXC)
        f_c, w0 = carve(w0, 2, EXC - 2)
        f_s, w0 = carve(w0, KF, 2 * NB)
        f_o, w0 = carve(w0, KF, 2 * (1 + NB))

        def per_batch(ap, n):
            return ap.rearrange("p (b t) -> p b t", t=n)

        def smp(ap):
            return per_batch(ap[:, TP:N], TS)

        def ext_prompt(ap):
            return ap[:, 1:1 + TP]

        def ext_sample(ap):
            return per_batch(ap[:, 1 + TP:EXT], 1 + TS)[:, :, 1:1 + TS]

        def chunks(ap):
            return ap[:, 0:TP].rearrange("p (c t) -> p c t", t=CH)

        def bc(ap, shape):
            return ap.broadcast_to(shape)

        def read_done(eng, stage):
            g = tiles_of(stage)[-1][0]
            eng.wait_ge(*at("bank_read_" + READER[g], READ_NO[g]))

        class Steps:

            def __init__(self, eng, chain):
                self.eng, self.chain, self.n = eng, chain, {}

            def __call__(self, ins, signal=None):
                name = SERIES.get(signal or self.chain, signal or self.chain)
                self.n[name] = self.n.get(name, 0) + 1
                assert signal not in PLACE or 0 < self.n[name] - PLACE[signal] <= TIMES[name], signal
                ins.then_inc(S(name), 1)
                self.eng.wait_ge(S(name), self.n[name])

        dq = {}

        def dma(eng, name, dst, src):
            dq[name] = dq.get(name, 0) + 16
            eng.dma_start(dst, src).then_inc(S(name), 16)

        with nc.Block() as block:
            @block.sync
            def _(sp):
                sp.dma_start(con[:, :], t_in["const"]).then_inc(S("load_once"), 16)
                sp.dma_start(X[:, :, :], t_in["x"]).then_inc(S("load_once"), 16)
                sp.dma_start(pages[:, :], t_in["pages"]).then_inc(S("load_once"), 16)
                sp.wait_ge(*at("load_once", 48))

        with nc.Fori(0, L) as layer:
            def dram(name, group=t_in):
                a = group[name][bass.ds(layer, 1)]
                k = len(a.shape)
                if k == 3:
                    return a.rearrange("o p a -> (o p) a")
                if k == 4:
                    return a.rearrange("o p a b -> (o p) a b")
                return a.rearrange("o p a b c -> (o p) a b c")

            def dram_out(name):
                return dram(name, t_out)

            with nc.Block() as block:
                @block.sync
                def _(sp):
                    def slot(s):
                        if s >= RING:
                            sp.wait_ge(*at("gemm_done", slot_done(s - RING)))
                        src = t_in["w"][bass.ds(layer, 1), s].rearrange("o p a -> (o p) a")
                        sp.dma_start(ring[:, s % RING, :], src).then_inc(S(f"slot_full{s % RING}"), 16)

                    def cache(b):
                        at_b = [sp.value_load(pages[0:1, b * PAGES + p:b * PAGES + p + 1], min_val=0, max_val=POOL - 1)
                                for p in range(PAGES)]
                        if b >= KV_SLOTS:
                            sp.wait_ge(*at("mla_pv", b - KV_SLOTS + 1))
                        for p, page in enumerate(at_b):
                            src = t_in["pool"][bass.ds(layer, 1), bass.ds(page, 1)].rearrange("o g p a -> (o g p) a")
                            sp.dma_start(kv[b % KV_SLOTS][:, p, :], src).then_inc(S(f"kv_full{b % KV_SLOTS}"), 16)

                    n_in = tiles_of("gate")[0][1][2] // SLOT
                    for s in range(n_in):
                        slot(s)
                    for b in range(KV_SLOTS):
                        cache(b)
                    for s in range(n_in, n_in + RING):
                        slot(s)
                    for b in range(KV_SLOTS, NB):
                        cache(b)
                    for s in range(n_in + RING, NSLOT):
                        slot(s)

                @block.gpsimd
                def _(pool):
                    dma(pool, "load_vec", vec[:, :], dram("vec"))
                    dma(pool, "load_mat", mat[:, :], dram("mat"))
                    dma(pool, "load_shift", r_hs[:, :, :], dram("shift"))
                    dma(pool, "load_gla", g_s0[:, :, :], dram("gla"))
                    pool.wait_ge(*at("gla_state"))
                    dma(pool, "stores", dram_out("gla_p"), g_st[:, NCH, :])
                    dma(pool, "stores", dram_out("gla_s"), g_s1[:, :, :])
                    pool.wait_ge(*at("mla_norm"))
                    dma(pool, "stores", dram_out("ckv"), m_ck[:, :])
                    dma(pool, "stores", dram_out("kpe"), m_kp[0:32, :])
                    pool.wait_ge(*at("mla_done"))
                    pool.wait_ge(*at("stores", 64))
                    dma(pool, "load_ml", l_c0[:, :, :], dram("ml_c"))
                    dma(pool, "load_ml", l_n0[:, :, :], dram("ml_n"))
                    dma(pool, "load_ml", l_m0[0:4, :], dram("ml_m"))
                    pool.wait_ge(*at("ml_state"))
                    dma(pool, "stores_ml", dram_out("ml_c_s"), l_c0[:, :, :])
                    dma(pool, "stores_ml", dram_out("ml_n_s"), l_n0[:, :, :])
                    dma(pool, "stores_ml", dram_out("ml_c_p"), l_cp[:, :, :])
                    dma(pool, "stores_ml", dram_out("ml_n_p"), l_np[:, :])
                    dma(pool, "stores_ml", dram_out("ml_m_ps"), l_mo[0:4, :])
                    pool.wait_ge(*at("stores_ml", 80))
                    pool.wait_ge(*at("ml_done"))
                    dma(pool, "load_rw", r_s0[:, :, :], dram("rwkv"))
                    pool.wait_ge(*at("rw_state"))
                    dma(pool, "stores_rw", dram_out("rwkv_s"), r_s0[:, :, :])
                    dma(pool, "stores_rw", dram_out("rwkv_p"), r_st[:, :, :])
                    dma(pool, "stores_rw", dram_out("shift_ps"), r_sh[:, :, :])
                    pool.wait_ge(*at("rw_done"))
                    pool.wait_ge(*at("stores_rw", 48))
                    dma(pool, "load_mem", c_mem[:, :, :], t_in["mem"])
                    for i in range(2 * NB):
                        if i >= 4:
                            pool.wait_ge(*at("ca_ss_s", i - 3) if i < 4 + NB else at("ca_o_s", i - 3 - NB))
                        src = t_in["mem_k" if i < NB else "mem_v"][bass.ds(layer, 1), i % NB].rearrange("o p a -> (o p) a")
                        dma(pool, f"ca_full{i % 4}", c_kv[i % 4][:, :], src)
                        if i == 3:
                            read_done(pool, "mem_v")
                            dma(pool, "stores_mem", dram_out("mem_kt"), c_mkt[:, :, :])
                            dma(pool, "stores_mem", dram_out("mem_v"), c_mv[:, :, :])
                    pool.wait_ge(*at("ca_oc_s"))
                    pool.wait_ge(*at("stores_mem", 32))
                    dma(pool, "load_conv", f_s[:, :, :], dram("conv"))
                    pool.wait_ge(*at("conv_state", KF))
                    dma(pool, "stores_conv", dram_out("conv_ps"), f_o[:, :, :])
                    pool.wait_ge(*at("stores_conv", 16))

                @block.tensor
                def _(pe):
                    mm = nc.tensor.matmul

                    def add(out, lhs, rhs):
                        return mm(out, lhs, rhs, start=False, stop=True, skip_group_check=True)

                    def put(out, lhs, rhs):
                        return mm(out, lhs, rhs, start=True, stop=True, skip_group_check=True)

                    def turn(out, in_):
                        k = in_.shape[0]
                        return nc.tensor.transpose(out, in_, ident[0:k, 0:k])

                    fences = [0]

                    def fence(ins):
                        fences[0] += 1
                        ins.then_inc(S("rows_free"), 1)
                        pe.wait_ge(*at("rows_free", fences[0]))

                    def block_of(i):
                        return ring[:, i // SLOT % RING, i % SLOT * P:(i % SLOT + 1) * P]

                    arrived = [0]

                    def gemm(g, rhs, lhs=None, width=N, normed=None):
                        stage, _, first, n, _ = TILES[g]
                        if g >= GEMM_BANKS:
                            h = g - GEMM_BANKS
                            pe.wait_ge(*at("bank_read_" + READER[h], READ_NO[h]))
                        bank = g % GEMM_BANKS
                        if lhs is None:
                            for k in range(n):
                                slot_here(first + k)
                                if normed:
                                    pe.wait_ge(*at(normed + "_done", k + 1))
                                last = mm(ps[:, bank, 0:width], block_of(first + k), rhs(k), start=k == 0, stop=k == n - 1)
                        else:
                            for k in range(n // 4):
                                slot_here(first + 4 * k)
                                i = first + 4 * k
                                four = ring[:, i // SLOT % RING, i % SLOT * P:(i % SLOT + 4) * P]
                                a = lhs(k)
                                last = mm(ps[0:a.shape[1], bank, :], a, four, start=k == 0, stop=k == n // 4 - 1)
                        last.then_inc(S("gemm_done"), 1)

                    def slot_here(i):
                        s = i // SLOT
                        if s >= arrived[0]:
                            pe.wait_ge(*at(f"slot_full{s % RING}", 16 * (s // RING + 1)))
                            arrived[0] = s + 1

                    def sum_squares(name, ks=range(KD), sq=SQ):
                        for k in ks:
                            pe.wait_ge(*at(name + "_sq", k + 1))
                            last = mm(ps[:, 7, 0:sq.shape[2]], C("ones"), sq[:, k, :], start=k == 0, stop=k == KD - 1)
                            if k == KD - 1:
                                last.then_inc(S(name + "_ss"), 1)

                    def projection(stage, rhs, norm):
                        for g, t in tiles_of(stage):
                            gemm(g, rhs)
                            if t[1]:
                                sum_squares(norm, [t[1] - 1])
                        sum_squares(norm, [KD - 1])

                    sum_squares("pre_mix")
                    for g, t in tiles_of("in"):
                        gemm(g, lambda k: H[:, k, :], normed="pre_mix" if t[1] == 0 else None)
                    for g, t in tiles_of("in_tok"):
                        c0, n = TT[t[1]]
                        gemm(g, None, lhs=lambda k: H[:, k, c0:c0 + n])

                    read_done(pe, "in_tok")
                    pe.wait_ge(*at("load_mat", 16))
                    put(ps[:, 4, 0:N], M("gate2", 0, P, GLO_AT, GLO_AT + 16), PR[GLO_AT:GLO_AT + 16, MIX1, :])\
                        .then_inc(S("gla_z"), 1)
                    pe.wait_ge(*at("gla_k"))
                    for i, (c0, n) in enumerate(TT):
                        last = turn(ps[0:n, 3, i * P:(i + 1) * P], g_ke[:, c0:c0 + n])
                    last.then_inc(S("gla_turned"), 1)
                    for h in range(4):
                        r = slice(32 * h, 32 * h + 32)
                        if h:
                            fence(last)
                        for i, (c0, n) in enumerate(TT):
                            last = put(ps[0:n, i, h * n:(h + 1) * n], g_k[r, c0:c0 + n], g_q[r, c0:c0 + n])
                    last.then_inc(S("gla_att"), 1)
                    pe.wait_ge(*at("gla_kt"))
                    for odd in range(2):
                        b0 = 64 * odd
                        for h in range(4):
                            r = slice(32 * h, 32 * h + 32)
                            for c in range(odd, NCH, 2):
                                last = put(ps[r, 4, c * 64:(c + 1) * 64], g_ktok[b0:b0 + 64, c // 2, r],
                                           VT[b0:b0 + 64, c // 2, h * 64:(h + 1) * 64])
                        if not odd:
                            fence(last)
                    for h in range(4):
                        r = slice(32 * h, 32 * h + 32)
                        last = put(ps[r, 5, :], g_ktok[0:NS, 2, r], g_vb[0:NS, h, :])
                    last.then_inc(S("gla_ds"), 1)
                    pe.wait_ge(*at("gla_attm"))
                    pe.wait_ge(*at("gla_state"))
                    o_heads = [(h, slice(32 * h, 32 * h + 32), ps[64 * (h % 2):64 * (h % 2) + 64, 6 + h // 2, :]) for h in range(4)]
                    for h, r, out in o_heads:
                        for i, (c0, n) in enumerate(TT[:2]):
                            last = put(out[:, c0:c0 + n], VT[0:n, i, h * 64:(h + 1) * 64], g_att[0:n, i, h * n:(h + 1) * n])
                            for c in (2 * i, 2 * i + 1):
                                if c:
                                    last = add(out[:, c * CH:(c + 1) * CH], g_st[r, c, :], g_q[r, c * CH:(c + 1) * CH])
                    fence(last)
                    for h, r, out in o_heads:
                        last = put(out[:, TP:N], VT[0:NS, 2, h * 64:(h + 1) * 64], g_att[0:NS, 2, h * NS:(h + 1) * NS])
                    fence(last)
                    for h, r, out in o_heads:
                        for b in range(NB):
                            j = TP + b * TS
                            last = add(out[:, j:j + TS], g_s0[r, b, :], g_q[r, j:j + TS])
                    last.then_inc(S("gla_o"), 1)
                    pe.wait_ge(*at("gla_sq"))
                    for j in range(2):
                        last = put(ps[:, j, 0:N], C("blk64", P), SQ[:, j, :])
                    last.then_inc(S("gla_ss"), 1)

                    pe.wait_ge(*at("mla_sq"))
                    pe.wait_ge(*at("gla_r"))
                    mm(ps[:, 2, 0:N], C("ones"), SQ[:, 2, :], start=True, stop=False)
                    mm(ps[:, 2, 0:N], C("ones"), SQ[:, 3, :], start=False, stop=True)
                    put(ps[:, 3, 0:N], C("ones"), SQ[:, 4, :]).then_inc(S("mla_ss"), 1)
                    pe.wait_ge(*at("mla_norm"))
                    for j in range(4):
                        for k in range(2):
                            last = mm(ps[:, 2 + j, 0:N], M("uq", k * 512 + j * P, k * 512 + (j + 1) * P), m_cqn[:, k, :],
                                      start=k == 0, stop=k == 1)
                    pe.wait_ge(*at("gla_done"))
                    for i, (c0, n) in enumerate(TT):
                        last = turn(ps[0:n, 6, i * P:(i + 1) * P], m_ck[:, c0:c0 + n])
                    last.then_inc(S("mla_q"), 1)
                    pe.wait_ge(*at("mla_qn"))
                    for h in range(4):
                        hb, hp = 64 * (h % 2), h // 2
                        last = put(ps[:, h, 0:N], M("uk", hp * P, (hp + 1) * P, hb, hb + 64), m_qn[hb:hb + 64, hp, :])
                    last.then_inc(S("mla_ql"), 1)
                    pe.wait_ge(*at("mla_qlc"))
                    for qt in range(2):
                        nk = (qt + 1) * P
                        q = slice(qt * P, (qt + 1) * P)
                        for h in range(4):
                            r = slice(32 * h, 32 * h + 32)
                            put(ps[:, h, 0:nk], m_ql[:, h, q], m_ck[:, 0:nk])
                            add(ps[:, h, 0:nk], m_qp[r, q], m_kp[r, 0:nk])
                            last = add(ps[:, h, q], ident, C("bias_tok", P))
                        last.then_inc(S("mla_s"), 1)
                        pe.wait_ge(*at("mla_pn", qt + 1))
                        for b in range(qt + 1):
                            for h in range(4):
                                last = turn(ps[:, 4 + b, h * P:(h + 1) * P], m_p[:, h, b * P:(b + 1) * P])
                        last.then_inc(S("mla_pt"), 1)
                        pe.wait_ge(*at("mla_ptc", qt + 1))
                        for h in range(4):
                            for b in range(qt + 1):
                                last = mm(ps[:, 6, h * P:(h + 1) * P], m_cktok[:, b, :], m_pt[:, b, h, :],
                                          start=b == 0, stop=b == qt)
                        last.then_inc(S("mla_ol"), 1)
                    pe.wait_ge(*at("mla_qs"))
                    def q_rows(b, k):
                        c = 64 * b + 48 - 16 * k
                        return m_qz[:, c:c + 64]

                    for b in range(NB):
                        out = ps[64 * (b % 2):64 * (b % 2) + 64, 7, NS * (b // 2):NS * (b // 2) + NS]
                        mm(out, q_rows(b, 0), m_ck[:, TP:N], start=b < 2, stop=False, skip_group_check=True)
                        add(out, m_qpz[0:32, 64 * b:64 * b + 64], m_kp[0:32, TP:N])
                    add(ps[:, 7, 0:P], ident, C("bias_own", P)).then_inc(S("mla_own"), 1)

                    def turns(b, j):
                        n = 5 * b + j
                        if j == 0:
                            pe.wait_ge(*at("rotated_packed", b + 1))
                        if n >= 2:
                            pe.wait_ge(*at("pages_copied", n - 1))
                        for i in range(4):
                            src = kv[b % KV_SLOTS][:, 4 * i + j - 1, 0:P] if j else m_kr[b % 2][:, i * P:(i + 1) * P]
                            last = turn(ps[:, 4 + n % 2, i * P:(i + 1) * P], src)
                        last.then_inc(S("pages_turned"), 1)

                    def scores(b, j):
                        out = ps[64 * (b % 2):64 * (b % 2) + 64, b // 2, :]
                        if j == 0:
                            pe.wait_ge(*at("pages_copied", 5 * b + 1))
                            mm(out, m_qpz[:, 64 * b:64 * b + 64], m_krt, start=True, stop=False)
                        pe.wait_ge(*at("pages_copied", 5 * b + j + 2))
                        last = mm(out, q_rows(b, j), m_kt[:, j, :], start=False, stop=j == 3)
                        last.then_inc(S("page_scores"), 1)

                    def maxima(g):
                        pe.wait_ge(*at("mla_top", g + 1))
                        turn(ps[0:1, 7, 0:P], m_top[:, g:g + 1]).then_inc(S("mla_topt"), 1)

                    def maxima_back(g):
                        pe.wait_ge(*at("mla_max_s", g + 1))
                        turn(ps[:, 7, P:P + 1], m_row).then_inc(S("mla_maxt"), 1)

                    def attend(g):
                        pe.wait_ge(*at("mla_p_s", g + 1))
                        for i in range(4):
                            turn(ps[:, 6, i * P:(i + 1) * P], m_ps[:, i * P:(i + 1) * P])
                        turn(ps[0:NS, 7, 2 * P:3 * P], m_po).then_inc(S("mla_pt_s"), 1)
                        pe.wait_ge(*at("mla_pts", g + 1))
                        put(ps[0:64, 7, 384:385], C("sum_own", 64), m_sums[:, 0:1])
                        add(ps[0:64, 7, 384:385], C("sum_own", 64), m_sums[:, 1:2])
                        for b in (2 * g, 2 * g + 1):
                            f = b % 2
                            out = ps[32 * f:32 * f + 16, 7, P:2 * P]
                            for p in range(PAGES):
                                r = 64 * f + 16 * (p % 4)
                                mm(out, m_pts[:, p // 4, r:r + 16], kv[b % KV_SLOTS][:, p, 0:P], start=p == 0, stop=False)
                            last = mm(out, m_pot[:, 64 * f:64 * f + 16], m_cktok[0:NS, 2, :], start=False, stop=True)
                            last.then_inc(S("mla_pv"), 1)

                    def outputs(g):
                        pe.wait_ge(*at("mla_os", g + 1))
                        turn(ps[:, 7, 0:64], m_os).then_inc(S("mla_ot"), 1)

                    for b in range(NB):
                        g = b // 2 - 1
                        turns(b, 0)
                        turns(b, 1)
                        for j in range(4):
                            if j < 3:
                                turns(b, j + 2)
                            scores(b, j)
                            if b % 2 == 0 and g >= 0:
                                if j == 0:
                                    maxima(g)
                                if j == 1:
                                    maxima_back(g)
                            elif b % 2 and g >= 0 and j == 0:
                                outputs(g)
                        if b % 2 == 0 and g >= 0:
                            attend(g)
                    g = NB // 2 - 1
                    maxima(g)
                    maxima_back(g)
                    attend(g)
                    outputs(g)
                    pe.wait_ge(*at("mla_ols", NB // 2))
                    for h in range(4):
                        hb = 64 * (h % 2)
                        last = put(ps[hb:hb + 64, h // 2, 0:N], M("uv", h * 64, (h + 1) * 64), m_ol[:, h, :])
                    last.then_inc(S("mla_o"), 1)

                    pe.wait_ge(*at("ml_exp"))
                    pe.wait_ge(*at("mla_done"))
                    for i, (c0, n) in enumerate(TT):
                        turn(ps[0:n, 0, i * 8:i * 8 + 4], l_g[0:4, c0:c0 + n])
                        turn(ps[0:n, 0, i * 8 + 4:i * 8 + 8], l_rows[0:4, L_WE + c0:L_WE + c0 + n])
                    for hp in range(2):
                        sel = C("sel_p", 2 * P, 4)[:, hp * P:(hp + 1) * P]
                        put(ps[:, 1 + hp, 0:N], sel, l_rows[0:4, L_EM:L_EM + N])
                        put(ps[:, 3, hp * NS:(hp + 1) * NS], sel, l_rows[0:4, L_WI:L_WI + NS])
                        put(ps[:, 3, 64 + hp * NB:64 + (hp + 1) * NB], sel, l_rows[0:4, L_SO:L_SO + NB])
                    for i, (c0, n) in enumerate(TT):
                        for hp in range(2):
                            c = i % 2 * 256 + hp * P
                            last = turn(ps[0:n, 4 + i // 2, c:c + P], PR[:, MK + hp, c0:c0 + n])
                    last.then_inc(S("ml_turned"), 1)
                    pe.wait_ge(*at("ml_k"))
                    for h in range(4):
                        if h >= 2:
                            pe.wait_ge(*at("ml_w", h - 1))
                        bias, qk = ps[:, 4 + h % 2, :], ps[:, 6 + h % 2, :]
                        sel = C("sel_h", 4 * P, 4)[:, h * P:(h + 1) * P]
                        put(bias[:, 0:416], ident, C("bias_m", 416))
                        add(bias[:, 0:256], sel, l_nm[0:4, 0:TP])
                        add(bias[:, 256:384], sel, l_nm[0:4, P:TP])
                        add(bias[:, 384:416], sel, l_nm[0:4, TP:N])
                        r, hp = slice(64 * (h % 2), 64 * (h % 2) + 64), h // 2
                        k, q = PR[r, MK + hp, :], PR[r, MQ + hp, :]
                        put(qk[:, 0:256], k[:, 0:P], q[:, 0:TP])
                        put(qk[:, 256:384], k[:, P:TP], q[:, P:TP])
                        put(qk[0:NS, 384:416], k[:, TP:N], q[:, TP:N]).then_inc(S("ml_s"), 1)
                    pe.wait_ge(*at("ml_w", 4))
                    for h in range(4):
                        r, hp = slice(64 * (h % 2), 64 * (h % 2) + 64), h // 2
                        for out, lhs, st in (
                                (ps[r, 4 + hp, :], lambda i, n: VT[0:n, i, 256 + h * 64:256 + (h + 1) * 64],
                                 lambda b: l_c0[r, hp, b * 64:(b + 1) * 64]),
                                (ps[r, 6 + hp, :], lambda i, n: C("ones", 64, n), lambda b: l_nbc[r, hp, b, :])):
                            put(out[:, 0:P], lhs(0, P), l_w[:, h, 0:P])
                            put(out[:, P:TP], lhs(0, P), l_w[:, h, P:TP])
                            add(out[:, P:TP], lhs(1, P), l_w[:, h, 256:384])
                            put(out[:, TP:N], lhs(2, NS), l_w[0:NS, h, 384:416])
                            for b in range(NB):
                                last = add(out[:, TP + b * TS:TP + (b + 1) * TS], st(b), l_qw[r, hp, b * TS:(b + 1) * TS])
                    last.then_inc(S("ml_num"), 1)
                    pe.wait_ge(*at("ml_h"))
                    for hp in range(2):
                        last = put(ps[:, 4 + hp, 0:N], C("blk64", P), l_h[:, hp, :])
                    last.then_inc(S("ml_mean"), 1)
                    for h in range(4):
                        r, hp = slice(64 * (h % 2), 64 * (h % 2) + 64), h // 2
                        hc = slice(h * 64, (h + 1) * 64)
                        for i in range(2):
                            mm(ps[r, 3, hp * 64:(hp + 1) * 64], l_kw[:, i, hc], VT[:, i, 256 + h * 64:256 + (h + 1) * 64],
                               start=i == 0, stop=i == 1)
                        for i in range(2):
                            mm(ps[r, 3, P + hp:P + hp + 1], l_kw[:, i, hc], C("ones", 1), start=i == 0, stop=i == 1)
                        put(ps[r, 3, 136 + hp * NB:136 + (hp + 1) * NB], l_kw[0:NS, 2, hc], C("batch", NB, NS))
                        last = put(ps[r, 1 + hp, :], l_kw[0:NS, 2, hc], l_vb[0:NS, h, :])
                    last.then_inc(S("ml_ds"), 1)
                    pe.wait_ge(*at("ml_sq"))
                    for hp in range(2):
                        last = put(ps[:, 6 + hp, 0:N], C("blk64", P), SQ[:, hp, :])
                    last.then_inc(S("ml_ss"), 1)

                    pe.wait_ge(*at("rw_tw"))
                    pe.wait_ge(*at("ml_state"))
                    pe.wait_ge(*at("ml_done"))
                    for hp in range(2):
                        c = slice(hp * P, (hp + 1) * P)
                        put(ps[:, hp, 0:N], M("wa", c.start, c.stop, 0, 64), r_tw[0:64, :])
                        put(ps[:, 2 + hp, 0:N], M("wa", c.start, c.stop, 64, P), SQ[64:P, 6, :])
                        last = put(ps[:, 4 + hp, 0:N], M("g2", c.start, c.stop), r_sg[:, :])
                    last.then_inc(S("rw_lora"), 1)
                    pe.wait_ge(*at("rw_kk"))
                    for hp in range(2):
                        last = put(ps[:, 6 + hp, 0:N], C("blk64", P), r_t[:, hp, :])
                    last.then_inc(S("rw_kks"), 1)
                    pe.wait_ge(*at("rw_vec"))
                    for hp in range(2):
                        last = put(ps[:, 6 + hp, 0:N], C("blk64", P), r_bo[:, hp, :])
                    last.then_inc(S("rw_bonus"), 1)
                    halves = [(h, slice(64 * (h % 2), 64 * (h % 2) + 64), h // 2) for h in range(4)]
                    levels = 0
                    for i, (c0, n) in enumerate(TT):
                        t = slice(c0, c0 + n)
                        if i:
                            pe.wait_ge(*at("rw_st", 2 * i))
                            pe.wait_ge(*at("rw_uc", 2 * i))
                        for odd in range(2):
                            for bank, a, b in ((0, r_be, r_al), (1, r_al, r_be), (2, r_rk, r_al), (3, r_be, r_rh), (4, r_rk, r_rh)):
                                for h, r, hp in halves[odd::2]:
                                    last = put(ps[0:n, bank, h * n:(h + 1) * n], a[r, hp, t], b[r, hp, t])
                            if not odd:
                                fence(last)
                        last.then_inc(S("rw_pair"), 1)
                        for kind, src in ((0, r_al), (1, r_kk)):
                            for hp in range(2):
                                c = kind * 256 + hp * P
                                last = turn(ps[0:n, 5, c:c + P], src[:, hp, t])
                        last.then_inc(S("rw_tok"), 1)
                        pe.wait_ge(*at("rw_pairm", i + 1))
                        for kind, src in ((0, r_cs), (1, SQ[:, 4:6, :])):
                            for hp in range(2):
                                c = kind * 256 + hp * P
                                last = turn(ps[0:n, 0, c:c + P], src[:, hp, t])
                        last.then_inc(S("rw_tok"), 1)
                        for j in range(1, 6 if i < 2 else 2):
                            levels += 1
                            pe.wait_ge(*at("rw_off", levels))
                            for h, r, hp in halves:
                                last = put(ps[0:n, 1, h * n:(h + 1) * n], r_off[0:n, h, 0:n], r_tm[0:n, h, 0:n])
                            last.then_inc(S("rw_x"), 1)
                            pe.wait_ge(*at("rw_xc", levels))
                            for h, r, hp in halves:
                                put(ps[0:n, 2, h * n:(h + 1) * n], r_tt[0:n, h, 0:n], r_x[0:n, h, 0:n])
                                last = put(ps[0:n, 3, h * n:(h + 1) * n], r_x[0:n, h, 0:n], r_tt[0:n, h, 0:n])
                            last.then_inc(S("rw_y"), 1)
                        pe.wait_ge(*at("rw_tokc", 2 * i + 2))
                        pe.wait_ge(*at("rw_t", levels))
                        for h, r, hp in halves:
                            hc = slice(h * 64, (h + 1) * 64)
                            put(ps[0:n, 4, hc], r_bt[0:n, h, 0:n], r_tok[0:n, 3, hc])
                            last = put(ps[r, 5, hp * n:(hp + 1) * n], r_tok[0:n, 0, hc], r_tt[0:n, h, 0:n])
                        last.then_inc(S("rw_bg"), 1)
                        pe.wait_ge(*at("rw_bgc", i + 1))
                        if i == 0:
                            pe.wait_ge(*at("rw_bo"))
                        if i < 2:
                            for c in (2 * i, 2 * i + 1):
                                s = slice(64 * (c % 2), 64 * (c % 2) + 64)
                                cc = slice(c * CH, (c + 1) * CH)
                                if c:
                                    pe.wait_ge(*at("rw_st", c))
                                for h, r, hp in halves:
                                    hc = slice(h * 64, (h + 1) * 64)
                                    last = mm(ps[s, 0, hc], r_tt[s, h, s], r_bv[s, hc], start=h == 0, stop=c == 0,
                                              skip_group_check=True)
                                for odd in ((c % 2, 1 - c % 2) if c else ()):
                                    if odd != c % 2:
                                        fence(last)
                                    for h, r, hp in halves[odd::2]:
                                        last = add(ps[s, 0, h * 64:(h + 1) * 64], r_gt[r, hp, s], r_st[r, hp, :])
                                last.then_inc(S("rw_u"), 1)
                                pe.wait_ge(*at("rw_uc", c + 1))
                                for h, r, hp in halves:
                                    hc = slice(h * 64, (h + 1) * 64)
                                    put(ps[r, 1, hp * 64:(hp + 1) * 64], r_tok[s, 1, hc], r_u[s, hc])
                                    last = add(ps[r, 1, hp * 64:(hp + 1) * 64], r_tok[s, 2, hc], r_tok[s, 3, hc])
                                for h, r, hp in halves:
                                    hc = slice(h * 64, (h + 1) * 64)
                                    put(ps[r, 6 + hp, cc], r_u[s, hc], r_rb[s, h, s])
                                    last = add(ps[r, 6 + hp, cc], r_tok[s, 3, hc], r_rkm[s, h, s])
                                if c:
                                    fence(last)
                                    for h, r, hp in halves:
                                        last = add(ps[r, 6 + hp, cc], r_st[r, hp, :], r_rh[r, hp, cc])
                                last.then_inc(S("rw_ds"), 1)
                        else:
                            pe.wait_ge(*at("load_rw", 16))
                            for h, r, hp in halves:
                                hc = slice(h * 64, (h + 1) * 64)
                                put(ps[r, 0, hp * NS:(hp + 1) * NS], r_bv[0:NS, hc], r_tt[0:NS, h, 0:NS])
                                for b in range(NB):
                                    j = hp * NS + b * TS
                                    last = add(ps[r, 0, j:j + TS], r_s0[r, hp, b * 64:(b + 1) * 64],
                                               r_gt[r, hp, b * TS:(b + 1) * TS])
                            last.then_inc(S("rw_u"), 1)
                            pe.wait_ge(*at("rw_uc", 5))
                            for hp in range(2):
                                last = turn(ps[0:NS, 1, hp * P:(hp + 1) * P], r_x[:, hp, 0:NS])
                            last.then_inc(S("rw_ut"), 1)
                            pe.wait_ge(*at("rw_utc"))
                            for h, r, hp in halves:
                                hc = slice(h * 64, (h + 1) * 64)
                                put(ps[r, 2 + hp, :], r_tok[0:NS, 1, hc], r_ub[0:NS, h, :])
                                add(ps[r, 2 + hp, :], r_tok[0:NS, 2, hc], r_vb[0:NS, h, :])
                                put(ps[r, 6 + hp, TP:N], r_u[0:NS, hc], r_rb[0:NS, h, 0:NS])
                                add(ps[r, 6 + hp, TP:N], r_tok[0:NS, 3, hc], r_rkm[0:NS, h, 0:NS])
                                for b in range(NB):
                                    j = TP + b * TS
                                    last = add(ps[r, 6 + hp, j:j + TS], r_s0[r, hp, b * 64:(b + 1) * 64], r_rh[r, hp, j:j + TS])
                            last.then_inc(S("rw_ds"), 1)
                    pe.wait_ge(*at("rw_yc"))
                    for hp in range(2):
                        last = put(ps[:, hp, 0:N], C("blk64", P), r_a[:, hp, :])
                    last.then_inc(S("rw_mean"), 1)
                    pe.wait_ge(*at("rw_sq"))
                    for hp in range(2):
                        last = put(ps[:, 4 + hp, 0:N], C("blk64", P), r_t[:, hp, :])
                    last.then_inc(S("rw_ss"), 1)

                    pe.wait_ge(*at("rw_done"))
                    for g, t in tiles_of("gate", "up"):
                        if t[0] == "gate":
                            gemm(g, lambda k: H[:, k, :])
                        else:
                            gemm(g, lambda k: O[:, 2 * t[1][1] + k, :])
                            if t[1] == MEM_SUMS_AT:
                                sum_squares("mem", sq=c_mkt)

                    for g, t in tiles_of("mem_k"):
                        gemm(g, lambda k: c_mem[:, k, :], width=MEM, normed="mem" if t[1] == 0 else None)
                    for g, t in tiles_of("mem_v"):
                        tok = t[1][1]
                        gemm(g, None, lhs=lambda k: c_mem[:, k, tok * P:(tok + 1) * P])

                    pe.wait_ge(*at("mixed", KD))
                    projection("out", lambda k: PR[:, k, :], "post_mix")

                    sum_squares("pre_ca")
                    for g, t in tiles_of("ca_q"):
                        gemm(g, lambda k: H[:, k, :], normed="pre_ca" if t[1] == 0 else None)
                    read_done(pe, "ca_q")
                    for qt in range(2):
                        q = slice(qt * P, (qt + 1) * P)
                        for h in range(4):
                            for j in range(2):
                                last = mm(ps[:, h, 0:MEM], O[:, 2 * h + j, q], c_mkt[:, 2 * h + j, :], start=j == 0, stop=j == 1)
                        last.then_inc(S("ca_s"), 1)
                        pe.wait_ge(*at("ca_pn", qt + 1))
                        for b in range(2):
                            for h in range(4):
                                last = turn(ps[:, 4 + b, h * P:(h + 1) * P], c_p[:, h, b * P:(b + 1) * P])
                        last.then_inc(S("ca_pt"), 1)
                        pe.wait_ge(*at("ca_ptc", qt + 1))
                        for h in range(4):
                            for j in range(2):
                                d = 2 * h + j
                                for b in range(2):
                                    last = mm(ps[:, 6 + d // 4, d % 4 * P:(d % 4 + 1) * P], c_mv[:, b, d * P:(d + 1) * P],
                                              c_pt[:, b, h, :], start=b == 0, stop=b == 1)
                        last.then_inc(S("ca_o"), 1)
                    pe.wait_ge(*at("ca_oc", 2))
                    def mem_scores(g):
                        for b in (2 * g, 2 * g + 1):
                            pe.wait_ge(*at(f"ca_full{b % 4}", 16 * (b // 4 + 1)))
                            k_t = c_kv[b % 4].rearrange("p (a s) -> p a s", a=KD)
                            for h in range(4):
                                for j in range(2):
                                    last = mm(ps[32 * h:32 * h + 32, g, b % 2 * MEM:(b % 2 + 1) * MEM], O[:, 2 * h + j, TP:N],
                                              k_t[:, 2 * h + j, :], start=j == 0, stop=j == 1)
                            last.then_inc(S("ca_ss_s"), 1)

                    def mem_turns(g):
                        pe.wait_ge(*at("ca_pn_s", g + 1))
                        for b in (2 * g, 2 * g + 1):
                            for s in range(2):
                                c = b % 2 * 256 + s * P
                                last = turn(ps[:, 4 + g, c:c + P], c_ps[:, b, s * P:(s + 1) * P])
                        last.then_inc(S("ca_pt_s"), 1)

                    for g in range(NB // 2):
                        mem_scores(g)
                        if g:
                            mem_turns(g - 1)
                    mem_turns(NB // 2 - 1)
                    for b in range(NB):
                        i = NB + b
                        pe.wait_ge(*at("ca_pts", b // 2 + 1))
                        pe.wait_ge(*at(f"ca_full{i % 4}", 16 * (i // 4 + 1)))
                        v_b = c_kv[i % 4].rearrange("p (s d) -> p s d", s=2)
                        for s in range(2):
                            for h in range(4):
                                r = slice(32 * h, 32 * h + 32)
                                last = mm(ps[r, 0, 0:256], c_pts[:, b, s, r], v_b[:, s, 256 * h:256 * h + 256],
                                          start=b == 0 and s == 0, stop=b == NB - 1 and s == 1)
                        last.then_inc(S("ca_o_s"), 1)
                    pe.wait_ge(*at("ca_po"))
                    for j in range(2):
                        last = turn(ps[:, 1, j * P:(j + 1) * P], c_po[:, j * P:(j + 1) * P])
                    last.then_inc(S("ca_ot"), 1)
                    pe.wait_ge(*at("ca_oc_s"))
                    projection("ca_o", lambda k: H[:, k, :], "post_ca")

                    sum_squares("pre_ffn")
                    for g, t in tiles_of("ffn_a", "ffn_g"):
                        gemm(g, lambda k: H[:, k, :], normed="pre_ffn" if t[:2] == ("ffn_a", 0) else None)
                    read_done(pe, "ffn_g")
                    projection("down", lambda k: f_f[:, k, :], "post_ffn")

                @block.scalar
                def _(act):
                    step = Steps(act, "act_step")
                    A = nc.scalar.activation

                    def copy(out, in_, signal=None):
                        step(A(out, in_, ACT.Copy), signal)

                    def wait(name, n=1):
                        act.wait_ge(*at(name, n))

                    def tile_ready(g):
                        wait("gemm_done", g + 1)

                    def rms(name, rs=RS):
                        wait(name + "_ss")
                        step(A(rs, ps[:, 7, 0:rs.shape[1]], ACT.Sqrt, bias=eps, scale=1.0 / D), name + "_rstd")

                    def squares(name, src, gained, sq=SQ, after=None):
                        for k in range(KD):
                            if after:
                                wait(after, k + 1)
                            step(A(sq[:, k, :], src[:, k, :], ACT.Square), name + "_sq")
                            step(A(gained[:, k, :], src[:, k, :], ACT.Identity, scale=V(name, k)))

                    def into(stage, dst, name=None):
                        for g, t in tiles_of(stage):
                            tile_ready(g)
                            src = ps[:, g % GEMM_BANKS, 0:N]
                            if name:
                                step(A(SQ[:, t[1], :], src, ACT.Square), name + "_sq")
                                step(A(dst[:, t[1], :], src, ACT.Identity, scale=V(name, t[1])), "bank_read_act")
                            else:
                                copy(dst[:, t[1], :], src, "bank_read_act")

                    wait("load_vec", 16)
                    squares("pre_mix", X, H)
                    rms("pre_mix")
                    wait("halo")
                    for g, t in tiles_of("in"):
                        tile_ready(g)
                        j, src = t[1], ps[:, g % GEMM_BANKS, :]
                        if j >= RW:
                            step(A(ext_prompt(RE[:, j - RW, :]), src[:, 0:TP], ACT.Copy))
                            copy(ext_sample(RE[:, j - RW, :]), per_batch(src[:, TP:N], TS), "bank_read_act")
                        else:
                            f = ACT.Silu if j in (GR, GR + 1) else ACT.Sigmoid if j in (MO, MO + 1) else ACT.Copy
                            step(A(PR[:, j, :], src[:, 0:N], f), "bank_read_act")
                    for g, t in tiles_of("in_tok"):
                        tile_ready(g)
                        n = TT[t[1]][1]
                        copy(VT[0:n, t[1], :], ps[0:n, g % GEMM_BANKS, :], "bank_read_act")

                    wait("gla_abs")
                    step(A(g_t3, g_t2, ACT.Exp))
                    step(A(g_t3, g_t3, ACT.Ln, bias=one), "gla_log")
                    wait("gla_cum")
                    step(A(g_eb, g_cum, ACT.Exp, scale=1.0 / 16))
                    step(A(g_enb, g_cum, ACT.Exp, scale=-1.0 / 16))
                    step(A(g_ebe, g_t2, ACT.Exp, scale=1.0 / 16), "gla_exp")
                    wait("gla_o")
                    step(A(SQ[:, 0:2, :], ps[:, 6:8, 0:N], ACT.Square), "gla_sq")
                    step(A(SQ[:, 2:5, :], PR[:, CQ:CQ + 3, :], ACT.Square), "mla_sq")
                    wait("gla_ss")
                    step(A(g_ra, ps[:, 0:2, 0:N], ACT.Ln, bias=eps, scale=1.0 / 64))
                    step(A(g_ra, g_ra, ACT.Exp, scale=-0.5), "gla_r")

                    wait("mla_ss")
                    step(A(m_rr[:, 0, :], ps[:, 2, 0:N], ACT.Ln, bias=eps, scale=1.0 / 256))
                    step(A(m_rr[:, 1, :], ps[:, 3, 0:N], ACT.Ln, bias=eps, scale=1.0 / 128))
                    step(A(m_rr, m_rr, ACT.Exp, scale=-0.5), "mla_r")
                    wait("mla_ql")
                    copy(m_ql, ps[:, 0:4, 0:N], "mla_qlc")
                    for qt in range(2):
                        nk = (qt + 1) * P
                        wait("mla_max", qt + 1)
                        for h in range(4):
                            step(A(m_p[:, h, 0:nk], ps[:, h, 0:nk], ACT.Exp, bias=m_nm[:, h:h + 1], scale=SCALE_MLA,
                                   accum_out=m_sum[:, h:h + 1]), "mla_p" if h == 3 else None)
                        wait("mla_pt", qt + 1)
                        for b in range(qt + 1):
                            copy(m_pt[:, b, :, :], ps[:, 4 + b, :].rearrange("p (h t) -> p h t", h=4),
                                 "mla_ptc" if b == qt else None)
                        wait("mla_ol", qt + 1)
                        copy(m_ol[:, :, qt * P:(qt + 1) * P], ps[:, 6, :].rearrange("p (h t) -> p h t", h=4), "mla_olc")
                    def exps(g):
                        wait("mla_nm", g + 1)
                        step(A(m_ps, ps[:, g, :], ACT.Exp, bias=m_top[:, g:g + 1], scale=SCALE_MLA, accum_out=m_sums[:, 0:1]))
                        step(A(m_po, m_own[:, NS * g:NS * g + NS], ACT.Exp, bias=m_top[:, g:g + 1], scale=SCALE_MLA,
                               accum_out=m_sums[:, 1:2]), "mla_p_s")

                    for b in range(NB):
                        for j in range(5):
                            n = 5 * b + j
                            wait("pages_turned", n + 1)
                            if b:
                                wait("page_scores", 4 * (b - 1) + max(j, 1))
                            copy(m_kt[:, j - 1, :] if j else m_krt, ps[:, 4 + n % 2, :], "pages_copied")
                        if b % 2 == 0 and b:
                            exps(b // 2 - 1)
                    exps(NB // 2 - 1)
                    wait("mla_o")
                    copy(O[:, 2:4, :], ps[:, 0:2, 0:N], "mla_done")

                    wait("ml_abs")
                    step(A(l_t[0:4, :], l_t[0:4, :], ACT.Exp))
                    step(A(l_t[0:4, :], l_t[0:4, :], ACT.Ln, bias=one[0:4, :]), "ml_log")
                    wait("ml_rows")
                    step(A(l_rows[0:4, :], l_rows[0:4, :], ACT.Exp), "ml_exp")
                    wait("ml_gw")
                    for h in range(4):
                        wait("ml_s", h + 1)
                        for a, b, i, n in ((0, 256, 0, P), (256, 384, 1, P), (384, 416, 2, NS)):
                            step(A(l_w[0:n, h, a:b], ps[0:n, 4 + h % 2, a:b], ACT.Exp, bias=l_gw[0:n, i * 8 + h:i * 8 + h + 1]),
                                 "ml_e" if i == 2 else None)
                    wait("ml_c")
                    step(A(SQ[:, 0:2, :], l_h, ACT.Square), "ml_sq")
                    wait("ml_ss")
                    step(A(l_r, ps[:, 6:8, 0:N], ACT.Ln, bias=eps, scale=1.0 / 64))
                    step(A(l_r, l_r, ACT.Exp, scale=-0.5), "ml_r")

                    wait("rw_pm")
                    step(A(r_tw[0:64, :], SQ[0:64, 6, :], ACT.Tanh))
                    step(A(r_sg, SQ[:, 7, :], ACT.Sigmoid), "rw_tw")
                    wait("rw_lora")
                    for hp in range(2):
                        step(A(r_s[:, hp, :], ps[:, hp, 0:N], ACT.Sigmoid, bias=V("w0", hp)))
                        step(A(r_a[:, hp, :], ps[:, 2 + hp, 0:N], ACT.Sigmoid, bias=V("a0", hp)))
                    copy(r_g, ps[:, 4:6, 0:N], "rw_sig")
                    wait("rw_clamped")
                    step(A(r_t, r_t, ACT.Ln))
                    step(A(r_t, r_t, ACT.Exp, bias=C("kk_b"), scale=-0.5), "rw_inv")
                    wait("rw_cum")
                    step(A(r_rh, r_cs, ACT.Exp, scale=-DECAY))
                    step(A(r_cs, r_cs, ACT.Exp, scale=DECAY))
                    step(A(r_csx, r_csx, ACT.Exp, scale=-DECAY))
                    step(A(r_cse, r_cse, ACT.Exp, scale=-DECAY), "rw_exp")
                    levels = 0
                    uc = 0
                    for i, (c0, n) in enumerate(TT):
                        wait("rw_tok", 2 * i + 1)
                        copy(r_tok[0:n, 0:2, :], ps[0:n, 5, :].rearrange("p (a b) -> p a b", a=2), "rw_tokc")
                        wait("rw_tok", 2 * i + 2)
                        copy(r_tok[0:n, 2:4, :], ps[0:n, 0, :].rearrange("p (a b) -> p a b", a=2), "rw_tokc")
                        for j in range(1, 6 if i < 2 else 2):
                            levels += 1
                            wait("rw_x", levels)
                            copy(r_x[0:n, :, 0:n], ps[0:n, 1, 0:4 * n].rearrange("p (h s) -> p h s", h=4), "rw_xc")
                        wait("rw_bg", i + 1)
                        copy(r_bv[0:n, :], ps[0:n, 4, 0:256])
                        copy(r_gt[:, :, 0:n], ps[:, 5, 0:2 * n].rearrange("p (a b) -> p a b", a=2), "rw_bgc")
                        if i < 2:
                            for c in (2 * i, 2 * i + 1):
                                s = slice(64 * (c % 2), 64 * (c % 2) + 64)
                                wait("rw_u", c + 1)
                                copy(r_u[s, :], ps[s, 0, 0:256], "rw_uc")
                        else:
                            wait("rw_u", 5)
                            copy(r_x[:, 0:2, 0:NS], ps[:, 0, 0:2 * NS].rearrange("p (a b) -> p a b", a=2), "rw_uc")
                            wait("rw_ut")
                            copy(r_u[0:NS, :], ps[0:NS, 1, 0:256], "rw_utok")
                    wait("rw_ds", 5)
                    copy(r_a, ps[:, 6:8, 0:N], "rw_yc")
                    wait("rw_c")
                    step(A(r_t, r_a, ACT.Square), "rw_sq")
                    wait("rw_ss")
                    step(A(r_s, ps[:, 4:6, 0:N], ACT.Ln, bias=eps_r, scale=1.0 / 64))
                    step(A(r_s, r_s, ACT.Exp, scale=-0.5), "rw_r")

                    for g, t in tiles_of("gate"):
                        d, n = t[1]
                        if d >= 1:
                            wait("bank_read_dve", 4 * (d - 1) + n + 1)
                        tile_ready(g)
                        step(A(SQ[:, n, :], ps[:, g % GEMM_BANKS, 0:N], ACT.Sigmoid), "bank_read_act")
                        if (d, n) == MEM_SQUARES_AT:
                            wait("load_mem", 16)
                            squares("mem", c_mem, c_mem, c_mkt)
                        if (d, n) == MEM_SUMS_AT:
                            rms("mem", c_rs)

                    for g, t in tiles_of("mem_k"):
                        tile_ready(g)
                        copy(c_mkt[:, t[1], :], ps[:, g % GEMM_BANKS, 0:MEM], "bank_read_act")
                    for g, t in tiles_of("mem_v"):
                        half, tok = t[1]
                        tile_ready(g)
                        copy(c_mv[:, tok, half * 512:(half + 1) * 512], ps[:, g % GEMM_BANKS, :], "bank_read_act")

                    into("out", O, "post_mix")
                    rms("post_mix")

                    squares("pre_ca", X, H, after="post_mix_done")
                    rms("pre_ca")
                    into("ca_q", O)
                    for qt in range(2):
                        wait("ca_max", qt + 1)
                        for h in range(4):
                            step(A(c_p[:, h, :], ps[:, h, 0:MEM], ACT.Exp, bias=c_nm[:, h:h + 1], scale=SCALE_CA,
                                   accum_out=c_sum[:, h:h + 1]), "ca_p" if h == 3 else None)
                        wait("ca_pt", qt + 1)
                        copy(c_pt, ps[:, 4:6, :].rearrange("p b (h t) -> p b h t", h=4), "ca_ptc")
                        wait("ca_o", qt + 1)
                        copy(H[:, :, qt * P:(qt + 1) * P].rearrange("p (a d) t -> p a d t", a=2),
                             ps[:, 6:8, :].rearrange("p a (d t) -> p a d t", d=4), "ca_oc")
                    for g in range(NB // 2):
                        wait("ca_max_s", g + 1)
                        for b in (2 * g, 2 * g + 1):
                            step(A(c_ps[:, b, :], ps[:, g, b % 2 * MEM:(b % 2 + 1) * MEM], ACT.Exp, bias=c_nm[:, b:b + 1],
                                   scale=SCALE_CA, accum_out=c_sum[:, b:b + 1]), "ca_p_s" if b % 2 else None)
                    wait("ca_o_s", NB)
                    copy(c_po, ps[:, 0, 0:256], "ca_po")
                    wait("ca_ot")
                    copy(H[:, :, TP:N].rearrange("p (h j) t -> p j h t", j=2),
                         ps[:, 1, 0:256].rearrange("p (j h t) -> p j h t", j=2, h=4), "ca_oc_s")
                    into("ca_o", O, "post_ca")
                    rms("post_ca")

                    squares("pre_ffn", X, H, after="post_ca_done")
                    rms("pre_ffn")
                    wait("conv_halo", 2)
                    a_tiles = tiles_of("ffn_a")
                    for k in range(KF + 1):
                        if k < KF:
                            g, t = a_tiles[k]
                            tile_ready(g)
                            if k >= 2:
                                wait("conv_state", k - 1)
                            step(A(f_a[:, k % 2, 2:2 + TP], ps[:, g % GEMM_BANKS, 0:TP], ACT.Copy))
                            copy(per_batch(f_a[:, k % 2, 2 + TP:EXC], 2 + TS)[:, :, 2:2 + TS],
                                 per_batch(ps[:, g % GEMM_BANKS, TP:N], TS), "bank_read_act")
                        if k >= 1:
                            wait("conv", k)
                            step(A(f_c[:, (k - 1) % 2, :], f_c[:, (k - 1) % 2, :], ACT.Gelu), "gelu")
                    into("down", O, "post_ffn")
                    rms("post_ffn")

                @block.vector
                def _(dve):
                    step = Steps(dve, "dve_step")
                    v = nc.vector

                    def wait(name, n=1):
                        dve.wait_ge(*at(name, n))

                    def tt(out, a, b, op, signal=None):
                        step(v.tensor_tensor(out, a, b, op), signal)

                    def ts(out, a, s1, s2, op0, op1=None, signal=None):
                        if op1 is None:
                            step(v.tensor_scalar(out, a, s1, None, op0), signal)
                        else:
                            step(v.tensor_scalar(out, a, s1, s2, op0, op1), signal)

                    def stt(out, a, s, b, op0, op1, signal=None):
                        step(v.scalar_tensor_tensor(out, a, s, b, op0, op1), signal)

                    def copy(out, in_, signal=None):
                        step(v.tensor_copy(out, in_), signal)

                    def fill(out, value, signal=None):
                        step(v.memset(out, value), signal)

                    MUL, ADD, SUB, MAX, MIN = ALU.mult, ALU.add, ALU.subtract, ALU.max, ALU.min

                    def normed(name, dst, rs=RS):
                        wait(name + "_rstd")
                        step(v.reciprocal(rs, rs))
                        for k in range(KD):
                            tt(dst[:, k, :], dst[:, k, :], rs, MUL, name + "_done")

                    def residual(name):
                        wait(name + "_rstd")
                        step(v.reciprocal(RS[:, :], RS[:, :]))
                        for k in range(KD):
                            tt(O[:, k, :], O[:, k, :], RS[:, :], MUL)
                            tt(X[:, k, :], X[:, k, :], O[:, k, :], ADD, name + "_done")

                    wait("load_vec", 16)
                    wait("load_shift", 16)
                    fill(RE[:, :, 0:1], 0.0)
                    copy(RE[:, :, 1 + TP:EXT].rearrange("p a (b t) -> p a b t", t=1 + TS)[:, :, :, 0], r_hs[:, :, :], "halo")
                    normed("pre_mix", H)

                    wait("gla_z")
                    ts(g_t1, ps[:, 4, 0:N], V("gla_b"), None, ADD)
                    stt(g_t2, g_t1, -1.0, g_t1, MUL, MIN, "gla_abs")
                    wait("gla_log")
                    stt(g_t2, g_t1, 0.0, g_t3, MIN, SUB)
                    step(v.tensor_tensor_scan(g_cum, C("reset", N), g_t2, 0.0, MUL, ADD))
                    tt(chunks(g_t2), bc(chunks(g_cum)[:, :, CH - 1:CH], [P, NCH, CH]), chunks(g_cum), SUB)
                    tt(smp(g_t2), bc(smp(g_cum)[:, :, TS - 1:TS], [P, NB, TS]), smp(g_cum), SUB, "gla_cum")
                    tt(g_vb.rearrange("p h (b v) -> p h b v", b=NB)[0:NS],
                       VT[0:NS, 2, 0:256].rearrange("p (h o v) -> p h o v", h=4, o=1).broadcast_to([NS, 4, NB, 64]),
                       C("batch", NB, NS).rearrange("p (o b u) -> p o b u", o=1, u=1).broadcast_to([NS, 4, NB, 64]), MUL)
                    wait("gla_exp")
                    stt(g_q, PR[:, GQ, :], 32.0 ** -0.5, g_eb, MUL, MUL)
                    tt(g_k, PR[:, GK, :], g_enb, MUL)
                    tt(g_ke, PR[:, GK, :], g_ebe, MUL, "gla_k")
                    wait("gla_turned")
                    copy(g_ktok[:, 0:2, :], ps[:, 3, 0:2 * P].rearrange("p (a b) -> p a b", a=2))
                    copy(g_ktok[0:NS, 2, :], ps[0:NS, 3, 2 * P:3 * P], "gla_kt")
                    wait("gla_att")
                    for i, (c0, n) in enumerate(TT):
                        m = C("upper", P) if i < 2 else C("upper_s", NS, NS)
                        tt(g_att[0:n, i, 0:4 * n].rearrange("p (h t) -> p h t", h=4),
                           ps[0:n, i, 0:4 * n].rearrange("p (h t) -> p h t", h=4),
                           m.rearrange("p (o t) -> p o t", o=1).broadcast_to([n, 4, n]), MUL, "gla_attm" if i == 2 else None)
                    wait("gla_ds")
                    wait("load_gla", 16)
                    copy(g_st[:, 1, :], ps[:, 4, 0:64])
                    for c in range(1, NCH):
                        e = (c + 1) * CH - 1
                        stt(g_st[:, c + 1, :], g_st[:, c, :], g_eb[:, e:e + 1], ps[:, 4, c * 64:(c + 1) * 64], MUL, ADD)
                    tt(g_s1, g_s0, bc(smp(g_eb)[:, :, TS - 1:TS], [P, NB, 64]), MUL)
                    tt(g_s1, g_s1, ps[:, 5, :].rearrange("p (b v) -> p b v", b=NB), ADD, "gla_state")
                    wait("gla_r")
                    stt(O[:, 0:2, :], ps[:, 6:8, 0:N], V("gla_norm"), g_ra, MUL, MUL)
                    tt(O[:, 0:2, :], O[:, 0:2, :], PR[:, GR:GR + 2, :], MUL, "gla_done")

                    wait("mla_r")
                    wait("stores", 32)
                    for j in range(2):
                        stt(m_cqn[:, j, :], PR[:, CQ + j, :], V("norm_q", j), m_rr[:, 0, :], MUL, MUL)
                    stt(m_ck, PR[:, CKV, :], V("norm_kv"), m_rr[:, 1, :], MUL, MUL)
                    tt(m_ta[0:32, :], PR[64:96, MIX1, :], C("cos", N, 32, 64), MUL)
                    tt(m_tb[0:32, :], PR[96:128, MIX1, :], C("sin", N, 32, 96), MUL)
                    tt(m_kp[0:32, :], m_ta[0:32, :], m_tb[0:32, :], ADD)
                    for r in (32, 64, 96):
                        copy(m_kp[r:r + 32, :], m_kp[0:32, :], "mla_norm" if r == 96 else None)
                    wait("mla_q")
                    copy(m_qn, ps[:, 2:4, 0:N])
                    tt(m_ta, ps[:, 4, 0:N], C("cos", N), MUL)
                    tt(m_tb, ps[:, 5, 0:N], C("sin", N), MUL)
                    tt(m_qp, m_ta, m_tb, ADD)
                    copy(m_cktok[:, 0:2, :], ps[:, 6, 0:2 * P].rearrange("p (a b) -> p a b", a=2))
                    copy(m_cktok[0:NS, 2, :], ps[0:NS, 6, 2 * P:3 * P], "mla_qn")
                    qpz = m_qpz.rearrange("p (b k q) -> p b k q", b=NB, k=4)
                    fill(m_qz, 0.0)
                    fill(m_qpz, 0.0)
                    for h in range(4):
                        copy(qpz[0:32, :, 0, TS * h:TS * h + TS], smp(m_qp)[32 * h:32 * h + 32])
                    for k in range(1, 4):
                        copy(qpz[32 * k:32 * k + 32, :, k, :], qpz[0:32, :, 0, :])
                    wait("mla_qlc")
                    for h in range(4):
                        copy(m_qz[:, 0:64 * NB].rearrange("p (b z) -> p b z", b=NB)[:, :, 48 + TS * h:48 + TS * h + TS],
                             smp(m_ql[:, h, :]), "mla_qs" if h == 3 else None)
                    for qt in range(2):
                        nk = (qt + 1) * P
                        wait("mla_s", qt + 1)
                        step(v.tensor_reduce(m_mx[:, :], ps[:, 0:4, 0:nk], AX.X, MAX))
                        ts(m_nm, m_mx, -SCALE_MLA, None, MUL, signal="mla_max")
                        wait("mla_p", qt + 1)
                        step(v.reciprocal(m_rec, m_sum))
                        tt(m_p[:, :, 0:nk], m_p[:, :, 0:nk],
                           m_rec.rearrange("p (h o) -> p h o", o=1).broadcast_to([P, 4, nk]), MUL, "mla_pn")
                    def pack_rotated(b):
                        wait(f"kv_full{b % KV_SLOTS}", 16 * PAGES * (b // KV_SLOTS + 1))
                        if b >= 2:
                            wait("pages_turned", 5 * (b - 2) + 1)
                        copy(m_kr[b % 2].rearrange("p (g r) -> p g r", r=32), kv[b % KV_SLOTS][:, :, P:ROW], "rotated_packed")

                    pack_rotated(0)
                    pack_rotated(1)
                    wait("mla_own")
                    copy(m_own, ps[:, 7, 0:P])
                    step(v.tensor_reduce(m_otop, ps[:, 7, 0:P].rearrange("p (g k) -> p g k", k=NS), AX.X, MAX), "mla_own_max")
                    fill(m_os, 0.0)
                    pack_rotated(2)
                    for g in range(NB // 2):
                        wait("page_scores", 8 * g + 8)
                        step(v.tensor_reduce(m_top[:, g:g + 1], ps[:, g, :], AX.X, MAX))
                        tt(m_top[:, g:g + 1], m_top[:, g:g + 1], m_otop[:, g:g + 1], MAX, "mla_top")
                        wait("mla_topt", g + 1)
                        step(v.tensor_reduce(m_tops.rearrange("p (f q) -> p f q", f=2),
                                             ps[0:1, 7, 0:P].rearrange("p (f k q) -> p f q k", f=2, k=4), AX.X, MAX))
                        copy(m_row.rearrange("p (f k q) -> p f k q", f=2, k=4),
                             m_tops.rearrange("p (f o q) -> p f o q", f=2, o=1).broadcast_to([1, 2, 4, 16]), "mla_max_s")
                        wait("mla_maxt", g + 1)
                        ts(m_top[:, g:g + 1], ps[:, 7, P:P + 1], -SCALE_MLA, None, MUL, signal="mla_nm")
                        wait("mla_pt_s", g + 1)
                        if g:
                            wait("mla_pv", 2 * g)
                        copy(m_pot, ps[0:NS, 7, 2 * P:3 * P])
                        copy(m_pts, ps[:, 6, :].rearrange("p (i r) -> p i r", i=4), "mla_pts")
                        if 2 * g + 3 < NB:
                            pack_rotated(2 * g + 3)
                        wait("mla_pv", 2 * g + 2)
                        step(v.reciprocal(m_recs, ps[0:64, 7, 384:385]))
                        ts(m_os[0:16], ps[0:16, 7, P:2 * P], m_recs[0:16], None, MUL)
                        ts(m_os[32:48], ps[32:48, 7, P:2 * P], m_recs[32:48], None, MUL, signal="mla_os")
                        wait("mla_ot", g + 1)
                        j = TP + 2 * TS * g
                        copy(m_ol[:, :, j:j + 2 * TS].rearrange("p h (f t) -> p h f t", f=2),
                             ps[:, 7, 0:64].rearrange("p (f r) -> p f r", f=2)[:, :, 0:16].rearrange("p f (h t) -> p h f t", h=4),
                             "mla_ols")
                        if 2 * g + 4 < NB:
                            pack_rotated(2 * g + 4)

                    wait("mla_done")
                    wait("load_ml", 48)
                    ts(l_x[0:4, :], PR[0:4, MIX2, :], V("f_bias", 0, 4), None, ADD)
                    stt(l_t[0:4, :], l_x[0:4, :], -1.0, l_x[0:4, :], MUL, MIN, "ml_abs")
                    fill(l_fe[0:4, :], NEG)
                    fill(l_ie[0:4, :], 0.0)
                    ts(ext_prompt(l_ie[0:4]), PR[0:4, MIX1, 0:TP], V("i_bias", 0, 4), None, ADD)
                    ts(ext_sample(l_ie[0:4]), smp(PR[0:4, MIX1, :]), V("i_bias", 0, 4), None, ADD)
                    copy(per_batch(l_ie[0:4, 1 + TP:EXT], 1 + TS)[:, :, 0:1], l_m0[0:4, :].rearrange("p (b o) -> p b o", o=1))
                    wait("ml_log")
                    stt(l_x[0:4, :], l_x[0:4, :], 0.0, l_t[0:4, :], MIN, SUB)
                    copy(ext_prompt(l_fe[0:4]), l_x[0:4, 0:TP])
                    copy(ext_sample(l_fe[0:4]), smp(l_x[0:4]))
                    step(v.tensor_tensor_scan(l_me[0:4, :], l_fe[0:4, :], l_ie[0:4, :], 0.0, ADD, MAX))
                    step(v.tensor_tensor_scan(l_b[0:4, :], C("reset_m", N, 4), l_x[0:4, :], 0.0, MUL, ADD))
                    tt(l_nm[0:4, 0:TP], l_b[0:4, 0:TP], ext_prompt(l_me[0:4]), SUB)
                    tt(smp(l_nm[0:4]), smp(l_b[0:4]), ext_sample(l_me[0:4]), SUB)
                    tt(l_g[0:4, 0:TP], ext_prompt(l_ie[0:4]), l_b[0:4, 0:TP], SUB)
                    tt(smp(l_g[0:4]), ext_sample(l_ie[0:4]), smp(l_b[0:4]), SUB)
                    rows = l_rows[0:4]
                    tt(rows[:, L_EM:L_EM + N], l_nm[0:4, :], l_b[0:4, :], SUB)
                    m0 = l_m0[0:4, :].rearrange("p (b o) -> p b o", o=1)
                    tt(per_batch(rows[:, L_WI:L_WI + NS], TS), smp(l_nm[0:4]), bc(m0, [4, NB, TS]), ADD)
                    ts(rows[:, L_WE:L_WE + TP], l_g[0:4, 0:TP], l_nm[0:4, TP - 1:TP], None, ADD)
                    nm_end = smp(l_nm[0:4])[:, :, TS - 1:TS]
                    tt(per_batch(rows[:, L_WE + TP:L_WE + N], TS), smp(l_g[0:4]), bc(nm_end, [4, NB, TS]), ADD)
                    copy(l_mo[0:4, 0:1], l_me[0:4, TP:TP + 1])
                    copy(l_mo[0:4, 1:1 + NB].rearrange("p (b o) -> p b o", o=1), ext_sample(l_me[0:4])[:, :, TS - 1:TS])
                    tt(rows[:, L_SO:L_SO + NB].rearrange("p (b o) -> p b o", o=1), m0, nm_end, ADD, "ml_rows")
                    tt(l_vb.rearrange("p h (b v) -> p h b v", b=NB)[0:NS],
                       VT[0:NS, 2, 256:512].rearrange("p (h o v) -> p h o v", h=4, o=1).broadcast_to([NS, 4, NB, 64]),
                       C("batch", NB, NS).rearrange("p (o b u) -> p o b u", o=1, u=1).broadcast_to([NS, 4, NB, 64]), MUL)
                    copy(l_nbc, l_n0.rearrange("p a (b o) -> p a b o", o=1).broadcast_to([P, 2, NB, 64]))
                    wait("ml_turned")
                    copy(l_gw[:, 0:16], ps[:, 0, 0:16])
                    copy(l_gw[0:NS, 16:24], ps[0:NS, 0, 16:24], "ml_gw")
                    for i, (c0, n) in enumerate(TT):
                        c = i % 2 * 256
                        tt(l_kw[0:n, i, :].rearrange("p (h k) -> p h k", h=4),
                           ps[0:n, 4 + i // 2, c:c + 256].rearrange("p (h k) -> p h k", h=4),
                           l_gw[0:n, i * 8 + 4:i * 8 + 8].rearrange("p (h o) -> p h o", o=1).broadcast_to([n, 4, 64]), MUL)
                    stt(l_qw, ps[:, 3, 0:2 * NS].rearrange("p (a b) -> p a b", a=2), 0.125, PR[:, MQ:MQ + 2, TP:N], MUL, MUL)
                    copy(l_so, ps[:, 3, 64:64 + 2 * NB].rearrange("p (a b) -> p a b", a=2), "ml_k")
                    for h in range(4):
                        wait("ml_e", h + 1)
                        qk = ps[:, 6 + h % 2, :]
                        stt(l_w[:, h, 0:384], qk[:, 0:384], 0.125, l_w[:, h, 0:384], MUL, MUL)
                        stt(l_w[0:NS, h, 384:416], qk[0:NS, 384:416], 0.125, l_w[0:NS, h, 384:416], MUL, MUL, "ml_w")
                    wait("ml_num")
                    copy(l_h, ps[:, 1:3, 0:N])
                    copy(l_den, ps[:, 6:8, 0:N])
                    stt(l_den, l_den, -1.0, l_den, MUL, MAX)
                    tt(l_den, l_den, l_h, MAX)
                    step(v.reciprocal(l_den, l_den))
                    tt(l_h, ps[:, 4:6, 0:N], l_den, MUL, "ml_h")
                    wait("ml_mean")
                    stt(l_h, ps[:, 4:6, 0:N], -1.0 / 64, l_h, MUL, ADD, "ml_c")
                    wait("ml_ds")
                    for hp in range(2):
                        c0 = l_c0[:, hp, :].rearrange("p (b v) -> p b v", b=NB)
                        tt(c0, c0, l_so[:, hp, :].rearrange("p (b o) -> p b o", o=1).broadcast_to([P, NB, 64]), MUL)
                        tt(l_c0[:, hp, :], l_c0[:, hp, :], ps[:, 1 + hp, :], ADD)
                    tt(l_n0, l_n0, l_so, MUL)
                    tt(l_n0, l_n0, ps[:, 3, 136:136 + 2 * NB].rearrange("p (a b) -> p a b", a=2), ADD)
                    copy(l_cp, ps[:, 3, 0:P].rearrange("p (a b) -> p a b", a=2))
                    copy(l_np, ps[:, 3, P:P + 2], "ml_state")
                    wait("ml_r")
                    for hp in range(2):
                        stt(l_h[:, hp, :], l_h[:, hp, :], V("ml_norm", hp), l_r[:, hp, :], MUL, MUL)
                    tt(O[:, 6:8, :], l_h, PR[:, MO:MO + 2, :], MUL, "ml_done")

                    wait("stores_ml", 80)
                    tt(r_d, RE[:, :, 0:EXT - 1], RE[:, :, 1:EXT], SUB)
                    for j in range(8):
                        stt(SQ[:, j, 0:TP], r_d[:, j, 0:TP], V("mu", j), ext_prompt(RE[:, j, :]), MUL, ADD)
                        stt(smp(SQ[:, j, :]), per_batch(r_d[:, j, TP:EXT - 1], 1 + TS)[:, :, 1:1 + TS], V("mu", j), ext_sample(RE[:, j, :]), MUL, ADD,
                            "rw_pm" if j == 7 else None)
                    copy(r_sh[:, :, 0:1], RE[:, :, TP:TP + 1])
                    copy(r_sh[:, :, 1:1 + NB], RE[:, :, 1 + TP:EXT].rearrange("p a (b t) -> p a b t", t=1 + TS)[:, :, :, TS])
                    rr, rk, rv = SQ[:, 0:2, :], SQ[:, 2:4, :], SQ[:, 4:6, :]
                    for hp in range(2):
                        ts(r_kk[:, hp, :], rk[:, hp, :], V("k_k", hp), None, MUL)
                    tt(r_t, r_kk, r_kk, MUL, "rw_kk")
                    wait("rw_kks")
                    ts(r_t, ps[:, 6:8, 0:N], 1e-24, 2.0 ** 20, MAX, MUL, "rw_clamped")
                    wait("rw_sig")
                    for hp in range(2):
                        step(v.tensor_tensor_scan(r_cs[:, hp, :], C("reset", N), r_s[:, hp, :], 0.0, MUL, ADD))
                    tt(r_csx, r_cs, r_s, SUB)
                    for hp in range(2):
                        a, b = r_cse[:, hp, :], r_cs[:, hp, :]
                        tt(chunks(a), bc(chunks(b)[:, :, CH - 1:CH], [P, NCH, CH]), chunks(b), SUB)
                        tt(smp(a), bc(smp(b)[:, :, TS - 1:TS], [P, NB, TS]), smp(b), SUB, "rw_cum" if hp == 1 else None)
                    wait("rw_inv")
                    tt(r_kk, r_kk, r_t, MUL)
                    tt(r_ka, r_kk, r_a, MUL)
                    for hp in range(2):
                        ts(r_t[:, hp, :], r_a[:, hp, :], 1.0, V("k_a", hp), SUB, MUL)
                    stt(r_rk, r_t, 1.0, rk, ADD, MUL)
                    for hp in range(2):
                        stt(r_bo[:, hp, :], rr[:, hp, :], V("r_k", hp), r_rk[:, hp, :], MUL, MUL)
                    wait("rw_exp")
                    tt(r_al, r_kk, r_csx, MUL)
                    stt(r_be, r_ka, -1.0, r_cs, MUL, MUL)
                    stt(r_kk, r_ka, -1.0, r_cse, MUL, MUL)
                    tt(r_csx, r_rk, r_cs, MUL)
                    tt(r_cs, r_rk, r_cse, MUL)
                    copy(r_rk, r_csx)
                    copy(r_s, r_rh)
                    tt(r_rh, rr, r_rh, MUL, "rw_vec")
                    wait("rw_bonus")
                    tt(r_bo, ps[:, 6:8, 0:N], rv, MUL, "rw_bo")
                    levels = 0
                    for i, (c0, n) in enumerate(TT):
                        def heads(a):
                            return a.rearrange("p (h t) -> p h t", h=4)

                        def bank(j):
                            return heads(ps[0:n, j, 0:4 * n])

                        def mask(name, j=0):
                            o = CON[name] + j * P
                            return con[0:n, o:o + n].rearrange("p (o t) -> p o t", o=1).broadcast_to([n, 4, n])

                        tm, tr, ato = r_tm[0:n, :, 0:n], r_tt[0:n, :, 0:n], r_at[0:n, :, 0:n]
                        wait("rw_pair", i + 1)
                        sfx = "" if i < 2 else "_s"
                        tt(ato, bank(0), mask("strict" + sfx), MUL)
                        tt(tr, ato, mask("level"), MUL)
                        tt(tr, tr, mask("ident"), ADD)
                        tt(tm, bank(1), mask("level0"), MUL)
                        tt(tm, tm, mask("ident"), ADD)
                        tt(r_bt[0:n, :, 0:n], bank(2), mask("strict" + sfx), MUL)
                        tt(r_rb[0:n, :, 0:n], bank(3), mask("upper" + sfx), MUL)
                        tt(r_rkm[0:n, :, 0:n], bank(4), mask("upper" + sfx), MUL, "rw_pairm")
                        for j in range(1, 6 if i < 2 else 2):
                            levels += 1
                            tt(r_off[0:n, :, 0:n], ato, mask("level", j), MUL, "rw_off")
                            wait("rw_y", levels)
                            tt(tm, tm, bank(2), ADD)
                            tt(tr, tr, bank(3), ADD, "rw_t")
                        if i < 2:
                            for c in (2 * i, 2 * i + 1):
                                e = (c + 1) * CH - 1
                                wait("rw_ds", c + 1)
                                for hp in range(2):
                                    src = ps[:, 1, hp * 64:(hp + 1) * 64]
                                    sig = "rw_st" if hp else None
                                    if c:
                                        stt(r_st[:, hp, :], r_st[:, hp, :], r_s[:, hp, e:e + 1], src, MUL, ADD, sig)
                                    else:
                                        copy(r_st[:, hp, :], src, sig)
                        else:
                            def spread(out, src, signal=None):
                                tt(out.rearrange("p h (b v) -> p h b v", b=NB)[0:NS],
                                   src.rearrange("p (h o v) -> p h o v", h=4, o=1).broadcast_to([NS, 4, NB, 64]),
                                   C("batch", NB, NS).rearrange("p (o b u) -> p o b u", o=1, u=1)
                                   .broadcast_to([NS, 4, NB, 64]), MUL, signal)
                            wait("rw_tokc", 6)
                            spread(r_vb, r_tok[0:NS, 3, :])
                            wait("rw_utok")
                            spread(r_ub, r_u[0:NS, :], "rw_utc")
                            wait("rw_ds", 5)
                            for hp in range(2):
                                s0 = r_s0[:, hp, :].rearrange("p (b v) -> p b v", b=NB)
                                tt(s0, s0, bc(smp(r_s[:, hp, :])[:, :, TS - 1:TS], [P, NB, 64]), MUL)
                                tt(r_s0[:, hp, :], r_s0[:, hp, :], ps[:, 2 + hp, :], ADD, "rw_state" if hp else None)
                    wait("rw_mean")
                    stt(r_a, ps[:, 0:2, 0:N], -1.0 / 64, r_a, MUL, ADD, "rw_c")
                    wait("rw_r")
                    for hp in range(2):
                        stt(r_t[:, hp, :], r_a[:, hp, :], V("ln_w", hp), r_s[:, hp, :], MUL, MUL)
                        stt(r_t[:, hp, :], r_t[:, hp, :], V("ln_b", hp), r_bo[:, hp, :], ADD, ADD)
                    tt(O[:, 4:6, :], r_t, r_g, MUL, "rw_done")

                    for g, t in tiles_of("up"):
                        d, n = t[1]
                        wait("gemm_done", g + 1)
                        wait("bank_read_act", READ_NO[g - 1])
                        dst = PR[:, d, :] if n == 0 else RS[:, :]
                        tt(dst, ps[:, g % GEMM_BANKS, 0:N], SQ[:, n, :], MUL, "bank_read_dve")
                        if n:
                            tt(PR[:, d, :], PR[:, d, :], RS[:, :], ADD, "mixed" if n == 3 else None)
                        if (d, n) == MEM_SUMS_AT:
                            normed("mem", c_mem, c_rs)

                    residual("post_mix")
                    normed("pre_ca", H)

                    for qt in range(2):
                        wait("ca_s", qt + 1)
                        step(v.tensor_reduce(c_mx[:, 0:4], ps[:, 0:4, 0:MEM], AX.X, MAX))
                        ts(c_nm[:, 0:4], c_mx[:, 0:4], -SCALE_CA, None, MUL, signal="ca_max")
                        wait("ca_p", qt + 1)
                        step(v.reciprocal(c_rec[:, 0:4], c_sum[:, 0:4]))
                        tt(c_p, c_p, c_rec[:, 0:4].rearrange("p (h o) -> p h o", o=1).broadcast_to([P, 4, MEM]), MUL, "ca_pn")
                    for g in range(NB // 2):
                        b2 = slice(2 * g, 2 * g + 2)
                        wait("ca_ss_s", 2 * g + 2)
                        step(v.tensor_reduce(c_mx[:, b2], ps[:, g, :].rearrange("p (b s) -> p b s", b=2), AX.X, MAX))
                        ts(c_nm[:, b2], c_mx[:, b2], -SCALE_CA, None, MUL, signal="ca_max_s")
                        wait("ca_p_s", g + 1)
                        step(v.reciprocal(c_rec[:, b2], c_sum[:, b2]))
                        tt(c_rec[:, b2], c_rec[:, b2], C("mem_own", NB)[:, b2], MUL)
                        tt(c_ps[:, b2, :], c_ps[:, b2, :], c_rec[:, b2].rearrange("p (b o) -> p b o", o=1).broadcast_to([P, 2, MEM]),
                           MUL, "ca_pn_s")
                        wait("ca_pt_s", g + 1)
                        copy(c_pts[:, b2, :, :], ps[:, 4 + g, :].rearrange("p (b s r) -> p b s r", b=2, s=2), "ca_pts")
                    residual("post_ca")
                    normed("pre_ffn", H)

                    wait("load_conv", 16)
                    wait("ca_oc_s")
                    for i in range(2):
                        fill(f_a[:, i, 0:2], 0.0, "conv_halo")
                    g_tiles = tiles_of("ffn_g")
                    for k in range(KF + 1):
                        if k < KF:
                            a = f_a[:, k % 2, :]
                            copy(per_batch(a[:, 2 + TP:EXC], 2 + TS)[:, :, 0:2], per_batch(f_s[:, k, :], 2))
                            wait("bank_read_act", READ_NO[tiles_of("ffn_a")[k][0]])
                            c = f_c[:, k % 2, :]
                            w = [V("conv_w", 3 * k + j) for j in range(3)]
                            ts(c, a[:, 0:EXC - 2], w[0], V("conv_b", k), MUL, ADD)
                            stt(c, a[:, 1:EXC - 1], w[1], c, MUL, ADD)
                            stt(c, a[:, 2:EXC], w[2], c, MUL, ADD, "conv")
                            copy(f_o[:, k, 0:2], a[:, TP:TP + 2])
                            copy(per_batch(f_o[:, k, 2:2 + 2 * NB], 2), per_batch(a[:, 2 + TP:EXC], 2 + TS)[:, :, TS:TS + 2],
                                 "conv_state")
                        if k >= 1:
                            j = k - 1
                            g, t = g_tiles[j]
                            wait("gelu", k)
                            wait("gemm_done", g + 1)
                            c, src = f_c[:, j % 2, :], ps[:, g % GEMM_BANKS, :]
                            tt(f_f[:, j, 0:TP], c[:, 0:TP], src[:, 0:TP], MUL)
                            tt(smp(f_f[:, j, :]), per_batch(c[:, TP:EXC - 2], 2 + TS)[:, :, 2:2 + TS],
                               per_batch(src[:, TP:N], TS), MUL, "bank_read_dve")
                    residual("post_ffn")

            with nc.Block() as block:
                @block.gpsimd
                def _(pool):
                    pool.dma_reset()
                    for name in sorted(sems):
                        if name != "load_once":
                            pool.sem_clear(sems[name])

        with nc.Block() as block:
            @block.sync
            def _(sp):
                sp.dma_start(t_out["y"], X[:, :, :]).then_inc(S("store_y"), 16)
                sp.wait_ge(S("store_y"), 16)


OUT = {
    "y": (P, KD, N), "ckv": (L, P, N), "kpe": (L, 32, N), "mem_kt": (L, P, KD, MEM), "mem_v": (L, P, 2, D),
    "gla_p": (L, P, 64), "gla_s": (L, P, NB, 64), "rwkv_p": (L, P, 2, 64), "rwkv_s": (L, P, 2, NB * 64),
    "shift_ps": (L, P, 8, 1 + NB), "ml_c_p": (L, P, 2, 64), "ml_c_s": (L, P, 2, NB * 64), "ml_n_p": (L, P, 2),
    "ml_n_s": (L, P, 2, NB), "ml_m_ps": (L, 4, 1 + NB), "conv_ps": (L, P, KF, 2 * (1 + NB)),
}


def constants():
    c = np.zeros((P, NCON), np.float32)

    def put(name, a):
        c[:a.shape[0], CON[name]:CON[name] + a.shape[1]] = a

    i = np.arange(P)
    row, col = i[:, None], i[None, :]
    put("ident", np.eye(P))
    put("ones", np.ones((P, P)))
    put("blk64", (row // 64 == col // 64) * 1.0)
    same, r4, c4 = row // CH == col // CH, row[:NS], col[:, :NS]
    put("upper", (same & (row <= col)) * 1.0)
    put("strict", (same & (row < col)) * 1.0)
    same4 = r4 // TS == c4 // TS
    put("upper_s", (same4 & (r4 <= c4)) * 1.0)
    put("strict_s", (same4 & (r4 < c4)) * 1.0)
    for j in range(6):
        s = 1 << j
        later = (row // (2 * s) == col // (2 * s)) & (row // s % 2 == 0) & (col // s % 2 == 1)
        c[:, CON["level"] + j * P:CON["level"] + (j + 1) * P] = later
        if j == 0:
            put("level0", later.T * 1.0)
    put("bias_tok", np.where(col <= row, 0.0, NEG))
    m = np.zeros((P, 416))
    m[:, 0:128] = m[:, 256:384] = np.where(row <= col, 0.0, NEG)
    m[:NS, 384:416] = np.where(same4 & (r4 <= c4), 0.0, NEG)
    put("bias_m", m)
    half, part, tok = row // 64, row // 16 % 4, row % TS
    group, key = np.arange(P)[None, :] // NS, np.arange(P)[None, :] % NS
    put("bias_own", np.where((part == 0) & (key // TS == 2 * group + half) & (key % TS <= tok), 0.0, NEG))
    col = np.arange(64)[None, :]
    put("sum_own", ((half == col // 32) & (row % 16 == col % 16)) * 1.0)
    put("mem_own", (row % NS // TS == np.arange(NB)[None, :]) * 1.0)
    for h in range(4):
        c[h, CON["sel_h"] + h * P:CON["sel_h"] + (h + 1) * P] = 1
        at = CON["sel_p"] + h // 2 * P + h % 2 * 64
        c[h, at:at + 64] = 1
    put("batch", (np.arange(NS)[:, None] // TS == np.arange(NB)[None, :]) * 1.0)
    half = 16
    freq = (np.float32(10000.0) ** (-np.arange(half, dtype=np.float32) / np.float32(half))).astype(np.float32)
    pos = np.concatenate([np.arange(TP), PAGES * PAGE + np.arange(NS) % TS]).astype(np.float32)
    ang = (pos[None, :] * freq[:, None]).astype(np.float32).astype(np.float64)
    put("cos", np.tile(np.cos(ang), (8, 1)))
    put("sin", np.tile(np.concatenate([-np.sin(ang), np.sin(ang)]), (4, 1)))
    first = np.r_[np.arange(TP) % CH == 0, np.arange(NS) % TS == 0]
    put("reset", np.tile(1.0 - first, (P, 1)))
    first[1:TP] = False
    put("reset_m", np.tile(1.0 - first, (P, 1)))
    for name, value in (("eps", 1e-6), ("eps_r", 64e-5), ("one", 1.0), ("kk_b", 10 * np.log(2.0))):
        put(name, np.full((P, 1), value))
    return c


def col(a, n):
    return np.moveaxis(a.reshape(a.shape[:-1] + (n, P)), -2, -1)


def blocks(w, order="j"):
    k, m = w.shape
    return w.reshape(k // P, P, m // P, P).transpose(2, 0, 1, 3).reshape(-1, P, P)


def wide(w):
    k, m = w.shape
    return w.reshape(k // P, P, m // 512, 4, P).transpose(2, 0, 3, 1, 4).reshape(-1, P, P)


def stream(i, l):
    w = i["w_in"][l]
    z = lambda n: np.zeros((D, n), np.float32)
    o_mla, o_rw, o_ml, o_g = 784, 1200, 2224, 3256
    kr = w[:, o_mla + 384:o_mla + 416]
    mix1 = np.concatenate([w[:, o_ml + 768:o_ml + 772], z(28), w[:, 512:528], z(16), kr, kr[:, 16:], kr[:, :16]], 1)
    mix2 = np.concatenate([w[:, o_ml + 772:o_ml + 776], z(124)], 1)
    feat = np.concatenate([w[:, 0:256], w[:, 528:784], w[:, o_mla:o_mla + 384], mix1, mix2, w[:, o_ml:o_ml + 512],
                           w[:, o_ml + 776:o_ml + 1032], w[:, o_rw:o_rw + 1024]], 1)
    tok = np.concatenate([w[:, 256:512], w[:, o_ml + 512:o_ml + 768]], 1)
    parts = [blocks(feat)]
    parts.append(np.zeros((-len(parts[0]) % SLOT, P, P), np.float32))
    parts.append(wide(tok))
    gate = blocks(w[:, o_g:]).reshape(4, KD, KD, P, P)
    up = np.stack([blocks(i["w_branch"][l, n]).reshape(KD, 2, P, P) for n in range(4)])
    parts.append(np.concatenate([gate, up], 2).transpose(1, 0, 2, 3, 4).reshape(-1, P, P))
    parts += [blocks(i["ca_w_k"][l]), wide(i["ca_w_v"][l]), blocks(i["w_out"][l]), blocks(i["ca_w_q"][l]),
              blocks(i["ca_w_o"][l])]
    f = blocks(i["ffn_w_up"][l]).reshape(2, KF, KD, P, P)
    parts.append(f.transpose(1, 0, 2, 3, 4).reshape(-1, P, P))
    parts.append(blocks(i["ffn_w_down"][l]))
    s = np.concatenate(parts)
    assert len(s) == NBLOCK, (len(s), NBLOCK)
    s = np.concatenate([s, np.zeros((NSLOT * SLOT - NBLOCK, P, P), np.float32)])
    return s.reshape(NSLOT, SLOT, P, P).transpose(0, 2, 1, 3).reshape(NSLOT, P, SLOT * P)


def kernel(**inputs):
    import concourse.bacc as bacc
    from concourse.bass_utils import run_bass_kernel_spmd

    i = {k: np.asarray(a) for k, a in inputs.items()}
    f32 = np.float32
    a = {"const": constants()}
    x = np.concatenate([i["x_prompt"].reshape(TP, D), i["x_sample"].reshape(NS, D)])
    feat = lambda t: np.ascontiguousarray(t.T.reshape(-1, P, t.shape[0]).transpose(1, 0, 2))
    a["x"] = feat(x)
    a["mem"] = feat(i["mem_prompt"].reshape(MEM, D))
    a["pages"] = np.ascontiguousarray(i["page_table"].reshape(1, NB * PAGES).astype(np.int32))
    a["w"] = np.stack([stream(i, l) for l in range(L)])
    v = np.zeros((L, P, NVEC), f32)

    def vec(name, t):
        v[:, :t.shape[1], VEC[name]:VEC[name] + t.shape[2]] = t

    for name in ("pre_mix", "post_mix", "pre_ca", "post_ca", "pre_ffn", "post_ffn"):
        vec(name, col(i["norm_" + name], KD))
    vec("mem", col(i["ca_norm_mem"], KD))
    vec("mu", col(i["rwkv_mu"], 8))
    for name, src in (("w0", "rwkv_w0"), ("a0", "rwkv_a0"), ("k_k", "rwkv_k_k"), ("k_a", "rwkv_k_a"), ("ln_w", "rwkv_ln_w"),
                      ("ln_b", "rwkv_ln_b"), ("ml_norm", "mlstm_norm"), ("norm_q", "mla_norm_q")):
        vec(name, col(i[src], 2))
    vec("r_k", col(i["rwkv_r_k"].reshape(L, 256), 2))
    vec("gla_norm", np.tile(i["gla_norm"], (1, 2))[:, :, None])
    vec("gla_b", i["gla_b_gate"][:, :, None])
    vec("norm_kv", i["mla_norm_kv"][:, :, None])
    vec("conv_w", i["ffn_conv_w"].reshape(L, 3, KF, P).transpose(0, 3, 2, 1).reshape(L, P, 3 * KF))
    vec("conv_b", col(i["ffn_conv_b"], KF))
    vec("i_bias", i["mlstm_i_bias"][:, :, None])
    vec("f_bias", i["mlstm_f_bias"][:, :, None])
    a["vec"] = v
    m = np.zeros((L, P, NMAT), f32)

    def mat(name, t, r0=0):
        m[:, r0:r0 + t.shape[1], MAT[name]:MAT[name] + t.shape[2]] = t

    mat("gate2", i["gla_w_gate2"], GLO_AT)
    uq = i["mla_w_uq"].reshape(L, 256, 4, 96)
    rope = uq[..., 64:]
    swap = np.concatenate([rope[..., 16:], rope[..., :16]], -1)
    uq = np.concatenate([uq[..., :64].reshape(L, 256, 256), rope.reshape(L, 256, P), swap.reshape(L, 256, P)], -1)
    mat("uq", uq.reshape(L, 2, P, 512).transpose(0, 2, 1, 3).reshape(L, P, 1024))
    mat("uk", i["mla_w_uk"].transpose(0, 1, 3, 2).reshape(L, 2, P, P).transpose(0, 2, 1, 3).reshape(L, P, 256))
    mat("uv", i["mla_w_uv"].transpose(0, 2, 1, 3).reshape(L, P, 256))
    mat("wa", i["rwkv_w2"])
    mat("wa", i["rwkv_a2"], 64)
    mat("g2", i["rwkv_g2"])
    a["mat"] = m
    a["pool"] = np.concatenate([i["cache_ckv"], i["cache_kpe"]], -1)
    mk = i["cache_mem_k"].reshape(L, NB, MEM, KD, P)
    a["mem_k"] = np.ascontiguousarray(mk.transpose(0, 1, 4, 3, 2)).reshape(L, NB, P, 2 * D)
    mv = i["cache_mem_v"].reshape(L, NB, 2, P, D)
    a["mem_v"] = np.ascontiguousarray(mv.transpose(0, 1, 3, 2, 4)).reshape(L, NB, P, 2 * D)
    a["gla"] = np.ascontiguousarray(i["state_gla"].reshape(L, NB, P, 64).transpose(0, 2, 1, 3))
    two = lambda t: np.ascontiguousarray(t.reshape(L, NB, 2, P, 64).transpose(0, 3, 2, 1, 4).reshape(L, P, 2, NB * 64))
    a["rwkv"] = two(i["state_rwkv"].transpose(0, 1, 2, 4, 3))
    a["shift"] = np.ascontiguousarray(i["state_rwkv_shift"].reshape(L, NB, 8, P).transpose(0, 3, 2, 1))
    a["ml_c"] = two(i["state_mlstm_c"])
    a["ml_n"] = np.ascontiguousarray(i["state_mlstm_n"].reshape(L, NB, 2, P).transpose(0, 3, 2, 1))
    a["ml_m"] = np.ascontiguousarray(i["state_mlstm_m"].transpose(0, 2, 1))
    a["conv"] = np.ascontiguousarray(i["state_conv"].reshape(L, NB, 2, KF, P).transpose(0, 4, 3, 1, 2)
                                     .reshape(L, P, KF, 2 * NB))

    nc = bacc.Bacc("TRN2", target_bir_lowering=False, num_devices=1)
    t_in = {k: nc.dram_tensor("in_" + k, t.shape, mybir.dt.from_np(t.dtype), kind="ExternalInput").ap()
            for k, t in a.items()}
    t_out = {k: nc.dram_tensor("out_" + k, s, F32, kind="ExternalOutput").ap() for k, s in OUT.items()}
    program(nc, t_in, t_out)
    r = run_bass_kernel_spmd(nc, [{"in_" + k: t for k, t in a.items()}], core_ids=[0]).results[0]
    o = {k: r["out_" + k] for k in OUT}

    y = o["y"].transpose(2, 1, 0).reshape(N, D)
    tok = lambda t: t.transpose(0, 2, 1)
    ckv, kpe = tok(o["ckv"]), tok(o["kpe"])
    two = lambda t: t.reshape(L, 2, 64, 2, -1, 64).transpose(0, 4, 3, 1, 2, 5).reshape(L, -1, 4, 64, 64)
    shift = o["shift_ps"].transpose(0, 3, 2, 1).reshape(L, 1 + NB, D)
    rows = lambda t: t.transpose(0, 3, 2, 1).reshape(L, -1, 4, 64)
    conv = o["conv_ps"].transpose(0, 3, 2, 1).reshape(L, 1 + NB, 2, FF)
    mm = tok(o["ml_m_ps"])
    return (y[:TP].reshape(1, TP, D), y[TP:].reshape(NB, TS, D),
            ckv[:, :TP].reshape(L, 1, TP, P), kpe[:, :TP].reshape(L, 1, TP, 32),
            ckv[:, TP:].reshape(L, NB, TS, P), kpe[:, TP:].reshape(L, NB, TS, 32),
            o["mem_kt"].transpose(0, 3, 2, 1).reshape(L, 1, MEM, 4, 256),
            o["mem_v"].transpose(0, 2, 1, 3).reshape(L, 1, MEM, 4, 256),
            o["gla_p"].reshape(L, 1, 4, 32, 64), o["gla_s"].transpose(0, 2, 1, 3).reshape(L, NB, 4, 32, 64),
            two(o["rwkv_p"]).transpose(0, 1, 2, 4, 3), two(o["rwkv_s"]).transpose(0, 1, 2, 4, 3),
            shift[:, :1], shift[:, 1:],
            two(o["ml_c_p"]), two(o["ml_c_s"]),
            rows(o["ml_n_p"].reshape(L, P, 2, 1)), rows(o["ml_n_s"]),
            mm[:, :1], mm[:, 1:], conv[:, :1], conv[:, 1:])
```

```python
from contextlib import ExitStack

import numpy as np

import concourse.bass as bass
from concourse import mybir

F32 = mybir.dt.float32
I32 = mybir.dt.int32
ALU = mybir.AluOpType
ACT = mybir.ActivationFunctionType
AX = mybir.AxisListType

P = 128
D = 1024
KD = D // P
L = 2
TP, NB, TS = 256, 8, 4
NS = NB * TS
N = TP + NS
PAGES, PAGE = 16, 128
KV_SLOTS = 5
POOL = NB * PAGES * 5 // 4
KEYS = PAGES * PAGE
FF = 2816
KF = FF // P
MEM = 256
CH = 64
NCH = TP // CH
TT = [(0, 128), (128, 128), (256, NS)]
EXT = 1 + TP + NB * (1 + TS)
EXC = 2 + TP + NB * (2 + TS)
NEG = -1e30
DECAY = float(np.exp(-0.5))
SCALE_MLA = 96.0 ** -0.5
SCALE_CA = 256.0 ** -0.5

GQ, GK, GR, CQ, CKV, MIX1, MIX2, MQ, MK, MO, RW = 0, 1, 2, 4, 6, 7, 8, 9, 11, 13, 15
NF = 23
I_AT, GLO_AT, KR_AT, KRS_AT = 0, 32, 64, 96

_v, VEC = 0, {}
for _name, _n in (("pre_mix", 8), ("post_mix", 8), ("pre_ca", 8), ("post_ca", 8), ("pre_ffn", 8), ("post_ffn", 8),
                  ("mem", 8), ("mu", 8), ("w0", 2), ("a0", 2), ("k_k", 2), ("k_a", 2), ("r_k", 2), ("ln_w", 2),
                  ("ln_b", 2), ("ml_norm", 2), ("gla_norm", 1), ("gla_b", 1), ("norm_q", 2), ("norm_kv", 1),
                  ("conv_w", 3 * KF), ("conv_b", KF), ("i_bias", 1), ("f_bias", 1)):
    VEC[_name] = _v
    _v += _n
NVEC = _v
_v, MAT = 0, {}
for _name, _n in (("gate2", 128), ("uq", 2 * 512), ("uk", 2 * 128), ("uv", 4 * 64), ("wa", 256), ("g2", 256)):
    MAT[_name] = _v
    _v += _n
NMAT = _v
_v, CON = 0, {}
for _name, _n in (("ident", 128), ("ones", 128), ("blk64", 128), ("upper", 128), ("strict", 128), ("upper_s", NS),
                  ("strict_s", NS), ("level", 6 * 128), ("level0", 128), ("bias_tok", 128), ("bias_m", 416),
                  ("bias_own", 128), ("sum_own", 64), ("mem_own", NB), ("sel_h", 4 * 128), ("sel_p", 2 * 128), ("batch", NB), ("cos", N), ("sin", N),
                  ("reset", N), ("reset_m", N), ("eps", 1), ("eps_r", 1), ("one", 1), ("kk_b", 1)):
    CON[_name] = _v
    _v += _n
NCON = _v

SLOT = 16
RING = 5
ROW = 160
GEMM_BANKS = 4


MIXING = [("gate", 0, n) for n in range(4)] + [("up", 0, n) for n in (0, 1, 3)]
MIXING += [("gate", 1, 0), ("up", 1, 0), ("up", 0, 2)]
MIXING += [(stage, 1, n) for n in range(1, 4) for stage in ("gate", "up")]
MIXING += [(stage, d, n) for d in range(2, KD) for n in range(4) for stage in ("gate", "up")]


def plan():
    tiles, at = [], 0

    def add(stage, index, n, reader, hold=False):
        nonlocal at
        tiles.append((stage, index, at, n, reader))
        if not hold:
            at += n

    for j in range(NF):
        add("in", j, KD, "act")
    at += (-at) % SLOT
    for i in range(3):
        add("in_tok", i, 4 * KD, "act", hold=i < 2)
    for stage, d, n in MIXING:
        add(stage, (d, n), *((KD, "act") if stage == "gate" else (2, "dve")))
    for j in range(KD):
        add("mem_k", j, KD, "act")
    for stage in ("mem_v0", "out", "mem_v1", "ca_q", "ca_o"):
        if stage in ("mem_v0", "mem_v1"):
            add(stage, 0, 4 * KD, "act", hold=True)
            add(stage, 1, 4 * KD, "act")
        else:
            for j in range(KD):
                add(stage, j, KD, "act")
    for j in range(KF):
        add("ffn_a", j, KD, "act")
        add("ffn_g", j, KD, "dve")
    for j in range(KD):
        add("down", j, KF, "act")
    return tiles, at


MEM_SQUARES_AT, MEM_SUMS_AT = (2, 3), (3, 3)
TILES, NBLOCK = plan()
NSLOT = -(-NBLOCK // SLOT)
READER = [t[4] for t in TILES]
READ_NO = [READER[:g].count(READER[g]) + 1 for g in range(len(TILES))]


def tiles_of(*stages):
    return [(g, t) for g, t in enumerate(TILES) if t[0] in stages]


N_IN = next(t[2] for t in TILES if t[0] == "gate") // SLOT
LENT = next(s for s in range(N_IN, N_IN + RING) if s % RING + 1 < RING)


def gate_read(d, n):
    return READ_NO[next(g for g, t in tiles_of("gate") if t[1] == (d, n))]


def slot_done(s):
    end = min((s + 1) * SLOT, NBLOCK)
    return next(g + 1 for g, t in enumerate(TILES) if t[2] + t[3] >= end and
                not any(u[2] < end and u[2] + u[3] > s * SLOT for u in TILES[g + 1:]))


STAGES = {
    "norm_squares": ("mem_sq", "post_mix_sq", "pre_ca_sq", "post_ca_sq", "pre_ffn_sq", "post_ffn_sq", "next_sq"),
    "norm_sums": ("mem_ss", "post_mix_ss", "pre_ca_ss", "post_ca_ss", "pre_ffn_ss", "post_ffn_ss", "next_ss"),
    "norm_scales": ("mem_rstd", "post_mix_rstd", "pre_ca_rstd", "post_ca_rstd", "pre_ffn_rstd", "post_ffn_rstd",
                    "next_rstd"),
    "norm_applied": ("pre_mix_done", "mem_done", "post_mix_done", "pre_ca_done", "post_ca_done", "pre_ffn_done",
                     "post_ffn_done"),
    "gla_tensor": ("gla_z", "gla_turned", "gla_att", "gla_ds", "gla_o", "gla_ss"),
    "gla_scalar": ("gla_log", "gla_exp", "gla_sq", "gla_r"),
    "gla_vector": ("gla_abs", "gla_cum", "gla_k", "gla_kt", "gla_attm", "gla_state", "gla_done"),
    "mla_tensor": ("mla_ss", "mla_q", "mla_ql", "mla_own", "mla_o"),
    "ca_sample": ("ca_po", "ca_oc_s"),
    "mla_scalar": ("mla_sq", "mla_r", "mla_qlc", "mla_done"),
    "mla_vector": ("mla_cq", "mla_norm", "mla_qn", "mla_qs", "mla_own_max"),
    "mlstm_tensor": ("ml_turned", "ml_num", "ml_ds", "ml_mean", "ml_ss"),
    "mlstm_scalar": ("ml_log", "ml_exp", "ml_sq", "ml_r"),
    "mlstm_vector": ("ml_abs", "ml_rows", "ml_gw", "ml_k", "ml_em", "ml_h", "ml_c", "ml_state", "ml_done"),
    "rwkv_tensor": ("rw_lora", "rw_kks", "rw_bonus", "rw_ut", "rw_mean", "rw_ss"),
    "rwkv_scalar": ("rw_tw", "rw_sig", "rw_inv", "rw_exp", "rw_utok", "rw_yc", "rw_sq", "rw_r"),
    "rwkv_vector": ("rw_pm", "rw_kk", "rw_clamped", "rw_cum", "rw_vec", "rw_bo", "rw_utc", "rw_state", "rw_c", "rw_done"),
}
SERIES = {stage: series for series, stages in STAGES.items() for stage in stages}
TIMES = {series: KD if series in ("norm_squares", "norm_applied") else 1 for series in STAGES}
PLACE = {stage: k * TIMES[series] for series, stages in STAGES.items() for k, stage in enumerate(stages)}


def program(nc, t_in, t_out):
    with ExitStack() as ctx:
        def sb(name, shape, dt=F32):
            return ctx.enter_context(nc.sbuf_tensor(name, shape, dt))

        sems = {}

        def S(name):
            name = SERIES.get(name, name)
            if name not in sems:
                sems[name] = ctx.enter_context(nc.semaphore(name))
            return sems[name]

        def at(name, n=1):
            return S(name), n + PLACE.get(name, 0)

        ring = sb("weight_ring", [P, RING, SLOT * P])
        con = sb("constants", [P, NCON])
        mat = sb("small_matrices", [P, NMAT])
        vec = sb("vectors", [P, NVEC])
        pages = sb("pages", [1, NB * PAGES], I32)
        X = sb("x_residual", [P, KD, N])
        H = sb("h_normed", [P, KD, N])
        O = sb("o_branches", [P, KD, N])
        SQ = sb("squares", [P, KD, N])
        PR = sb("projected", [P, RW, N])
        RE = sb("rwkv_projected", [P, 8, EXT])
        VT = sb("values_by_token", [P, 3, 512])
        RS = sb("rstd", [P, N])[:, :]
        r_hs = sb("rwkv_last_rows", [P, 8, NB])
        WORK = 17500
        L_WORK = 8640
        work = sb("work", [P, WORK])
        ps = ctx.enter_context(nc.psum_tensor("banks", [P, 8, 512], F32))

        def carve(word, *shape):
            n = int(np.prod(shape))
            assert word + n <= WORK, (word, n)
            a = work[:, word:word + n]
            if len(shape) == 2:
                a = a.rearrange("p (a b) -> p a b", a=shape[0])
            elif len(shape) == 3:
                a = a.rearrange("p (a b c) -> p a b c", a=shape[0], b=shape[1])
            return a, word + n

        def C(name, n=None, rows=P, r0=0):
            n = {"ident": P, "ones": P}.get(name, 1) if n is None else n
            return con[r0:r0 + rows, CON[name]:CON[name] + n]

        def V(name, j=0, rows=P):
            return vec[0:rows, VEC[name] + j:VEC[name] + j + 1]

        def M(name, a, b, r0=0, r1=P):
            return mat[r0:r1, MAT[name] + a:MAT[name] + b]

        ident = C("ident")
        eps, eps_r, one = C("eps"), C("eps_r"), C("one")

        kv, w0 = [], 0
        for i in range(KV_SLOTS - 1):
            a, w0 = carve(w0, PAGES, ROW)
            kv.append(a)
        lent = ring[:, LENT % RING:LENT % RING + 2, :].rearrange("p a b -> p (a b)")
        kv.append(lent[:, 0:PAGES * ROW].rearrange("p (g r) -> p g r", g=PAGES))
        g0 = w0
        g_t1, w0 = carve(g0, N)
        g_t2, w0 = carve(w0, N)
        g_t3, w0 = carve(w0, N)
        g_cum, w0 = carve(w0, N)
        g_eb, w0 = carve(w0, N)
        g_enb, w0 = carve(w0, N)
        g_ebe, w0 = carve(w0, N)
        g_q, w0 = carve(w0, N)
        g_k, w0 = carve(w0, N)
        g_ke, w0 = carve(w0, N)
        g_ktok, w0 = carve(w0, 3, P)
        g_att, w0 = carve(w0, 3, 512)
        sqf = SQ[:, :, :].rearrange("p a b -> p (a b)")
        g_vb = sqf[:, 0:4 * NB * 64].rearrange("p (h n) -> p h n", h=4)
        g_st, w0 = carve(w0, NCH + 1, 64)
        g_ra, w0 = carve(w0, 2, N)
        g_s0, w0 = carve(w0, NB, 64)
        g_s1, _ = carve(g0, NB, 64)
        m_cqn, w0 = carve(g0, 2, N)
        m_qn, w0 = carve(w0, 2, N)
        m_rr, w0 = carve(w0, 2, N)
        m_ta, w0 = carve(w0, N)
        m_tb, w0 = carve(w0, N)
        m_kt, _ = carve(g0, 4, 512)
        m_ck, w0 = carve(w0, N)
        m_cktok, w0 = carve(w0, 3, P)
        m_kp, w0 = carve(w0, N)
        m_qp, w0 = carve(w0, N)
        m_ql, w0 = carve(w0, 4, N)
        m_qz, w0 = carve(w0, 64 * NB + 48)
        m_qpz, w0 = carve(w0, 64 * NB)
        m_ol, w0 = carve(w0, 4, N)
        m_top, w0 = carve(w0, NB // 2)
        m_otop, m_end = carve(w0, NB // 2)
        m_p = [sqf[:, i * 1024:(i + 1) * 1024].rearrange("p (h s) -> p h s", h=4) for i in range(2)]
        m_pt, _ = carve(g0, 2, 4, P)
        m_mx, m_nm, m_sum, m_rec = ([sqf[:, 2048 + 8 * k + 4 * i:2052 + 8 * k + 4 * i] for i in range(2)] for k in range(4))
        m_ps = sqf[:, 0:512]
        m_pts = sqf[:, 512:1024].rearrange("p (i r) -> p i r", i=4)
        m_own = sqf[:, 1024:1024 + P]
        m_po = sqf[:, 1152:1152 + NS]
        m_pot = sqf[0:NS, 1280:1280 + P]
        m_os = sqf[0:64, 1408:1408 + P]
        m_row = sqf[0:1, 1536:1536 + P]
        m_tops = sqf[0:1, 1664:1664 + NS]
        m_sums = sqf[:, 1700:1702]
        m_recs = sqf[0:64, 1702:1703]
        m_krt = sqf[:, 1792:2304]
        m_kr = [O[:, :, :].rearrange("p a b -> p (a b)")[:, 4 * N + i * 512:4 * N + (i + 1) * 512] for i in range(2)]
        prf = PR[:, :, :].rearrange("p a b -> p (a b)")
        l_x, l_t = O[:, 2, :], O[:, 3, :]
        l_fe, l_ie, l_me = (prf[:, k * EXT:(k + 1) * EXT] for k in range(3))
        l_nm = l_fe[:, 0:N]
        l_b = prf[:, 3 * EXT:3 * EXT + N]
        L_WE, L_EM, L_WI, L_SO = 0, N, 2 * N, 2 * N + NS
        l_rows = prf[:, 3 * EXT + N:3 * EXT + N + 2 * N + NS + NB]
        assert 3 * EXT + 3 * N + NS + NB <= MIX1 * N
        l_g, w0 = carve(m_end, N)
        l_mo, w0 = carve(w0, 1 + NB)
        l_m0, w0 = carve(w0, NB)
        assert L_WORK + 8500 <= m_end
        w0 = L_WORK
        l_gw, w0 = carve(w0, 24)
        l_kw, w0 = carve(w0, 3, 256)
        l_w, w0 = carve(w0, 4, 416)
        l_vb, w0 = carve(w0, 4, NB * 64)
        l_c0, w0 = carve(w0, 2, NB * 64)
        l_n0, w0 = carve(w0, 2, NB)
        l_nbc, w0 = carve(w0, 2, NB, 64)
        l_so, w0 = carve(w0, 2, NB)
        l_qw, w0 = carve(w0, 2, NS)
        l_den, w0 = carve(w0, 2, N)
        l_h, w0 = carve(w0, 2, N)
        l_r, w0 = carve(w0, 2, N)
        l_cp, w0 = carve(w0, 2, 64)
        l_np, w0 = carve(w0, 2)
        r_tw, w0 = carve(0, N)
        r_sg, w0 = carve(w0, N)
        r_s, w0 = carve(w0, 2, N)
        r_a, w0 = carve(w0, 2, N)
        r_g, w0 = carve(w0, 2, N)
        r_kk, w0 = carve(w0, 2, N)
        r_t, w0 = carve(w0, 2, N)
        r_cs, w0 = carve(w0, 2, N)
        r_csx, w0 = carve(w0, 2, N)
        r_cse, w0 = carve(w0, 2, N)
        r_rk, w0 = carve(w0, 2, N)
        r_al, w0 = carve(w0, 2, N)
        r_be, w0 = carve(w0, 2, N)
        r_ka, w0 = carve(w0, 2, N)
        r_rh, w0 = carve(w0, 2, N)
        r_bo, w0 = carve(w0, 2, N)
        r_d = work[:, w0 - 5 * 2 * N:w0 - 5 * 2 * N + 8 * (EXT - 1)].rearrange("p (a b) -> p a b", a=8)
        r_tok, w0 = carve(w0, 4, 256)
        r_at, w0 = carve(w0, 4, P)
        r_tm, w0 = carve(w0, 4, P)
        r_tt, w0 = carve(w0, 4, P)
        r_x, w0 = carve(w0, 4, P)
        r_off, w0 = carve(w0, 4, P)
        r_bt, w0 = carve(w0, 4, P)
        r_rb, w0 = carve(w0, 4, P)
        r_rkm, w0 = carve(w0, 4, P)
        r_bv, w0 = carve(w0, 256)
        r_gt, w0 = carve(w0, 2, P)
        r_u, w0 = carve(w0, 256)
        r_st, w0 = carve(w0, 2, 64)
        r_s0, w0 = carve(w0, 2, NB * 64)
        r_ub = prf[:, 0:2048].rearrange("p (h n) -> p h n", h=4)
        r_vb = prf[:, 2048:4096].rearrange("p (h n) -> p h n", h=4)
        r_sh, w0 = carve(w0, 8, 1 + NB)
        r_tok2, w0 = carve(w0, 4, 256)
        r_bv2, w0 = carve(w0, 256)
        r_gt2, w0 = carve(w0, 2, P)
        r_2 = [prf[:, i * 512:(i + 1) * 512].rearrange("p (h t) -> p h t", h=4) for i in range(8)]
        r_at, r_tm, r_tt, r_x = (r_at, r_2[0], r_at), (r_tm, r_2[1], r_tm), (r_tt, r_2[2], r_tt), (r_x, r_2[3], r_x)
        r_off, r_bt, r_rb, r_rkm = (r_off, r_2[4], r_off), (r_bt, r_2[5], r_bt), (r_rb, r_2[6], r_rb), (r_rkm, r_2[7], r_rkm)
        r_tok, r_bv, r_gt = (r_tok, r_tok2, r_tok), (r_bv, r_bv2, r_bv), (r_gt, r_gt2, r_gt)
        RW_BANKS = ((1, 2, 3), (0, 4, 5), (1, 2, 3))
        RW_BG = ((4, 5), (2, 3), (4, 5))
        RW_LEVELS = [(j, i) for j in range(1, 6) for i in range(2)] + [(1, 2)]
        first_gates = VT[:, :, :].rearrange("p a b -> p (a b)")[:, 0:4 * N].rearrange("p (n t) -> p n t", n=4)
        c_mem, w0 = carve(0, KD, MEM)
        c_mkt, w0 = carve(w0, KD, MEM)
        c_mv, w0 = carve(w0, 2, D)
        c_rs = c_mv[:, 0, 0:MEM]
        c_kv = []
        for i in range(4):
            a, w0 = carve(w0, 2 * D)
            c_kv.append(a)
        c_pts, w0 = carve(w0, NB, 2, P)
        c_mx, w0 = carve(w0, 8)
        c_nm, w0 = carve(w0, 8)
        c_sum, w0 = carve(w0, 8)
        c_rec, w0 = carve(w0, 8)
        c_p = [sqf[:, i * 1024:(i + 1) * 1024].rearrange("p (h s) -> p h s", h=4) for i in range(2)]
        c_pt = c_pts[:, 0:4, :, :].rearrange("p (b g) s r -> p b (g s) r", b=2)
        c_ps = sqf[:, 0:NB * MEM].rearrange("p (b s) -> p b s", b=NB)
        c_po = sqf[:, NB * MEM:NB * MEM + 256]
        f_f, w0 = carve(0, KF, N)
        f_a, w0 = carve(w0, 2, EXC)
        f_c, w0 = carve(w0, 2, EXC - 2)
        f_s, w0 = carve(w0, KF, 2 * NB)
        f_o, w0 = carve(w0, KF, 2 * (1 + NB))

        def per_batch(ap, n):
            return ap.rearrange("p (b t) -> p b t", t=n)

        def smp(ap):
            return per_batch(ap[:, TP:N], TS)

        def ext_prompt(ap):
            return ap[:, 1:1 + TP]

        def ext_sample(ap):
            return per_batch(ap[:, 1 + TP:EXT], 1 + TS)[:, :, 1:1 + TS]

        def chunks(ap):
            return ap[:, 0:TP].rearrange("p (c t) -> p c t", t=CH)

        def bc(ap, shape):
            return ap.broadcast_to(shape)

        def read_done(eng, stage):
            g = tiles_of(stage)[-1][0]
            eng.wait_ge(*at("bank_read_" + READER[g], READ_NO[g]))

        class Steps:

            def __init__(self, eng, chain):
                self.eng, self.chain, self.n = eng, chain, {}

            def __call__(self, ins, signal=None):
                name = SERIES.get(signal or self.chain, signal or self.chain)
                self.n[name] = self.n.get(name, 0) + 1
                assert signal not in PLACE or 0 < self.n[name] - PLACE[signal] <= TIMES[name], signal
                ins.then_inc(S(name), 1)
                self.eng.wait_ge(S(name), self.n[name])

        dq = {}

        def dma(eng, name, dst, src):
            dq[name] = dq.get(name, 0) + 16
            eng.dma_start(dst, src).then_inc(S(name), 16)

        with nc.Block() as block:
            @block.sync
            def _(sp):
                sp.dma_start(con[:, :], t_in["const"]).then_inc(S("load_once"), 16)
                sp.dma_start(X[:, :, :], t_in["x"]).then_inc(S("load_once"), 16)
                sp.dma_start(pages[:, :], t_in["pages"]).then_inc(S("load_once"), 16)
                sp.wait_ge(*at("load_once", 48))

            @block.scalar
            def _(act):
                act.wait_ge(S("load_once"), 48)
                for k in range(KD):
                    nc.scalar.activation(SQ[:, k, :], X[:, k, :], ACT.Square).then_inc(S("first_sq"), 1)
                act.wait_ge(S("first_ss"), 1)
                nc.scalar.activation(RS, ps[:, 7, 0:N], ACT.Sqrt, bias=eps, scale=1.0 / D).then_inc(S("first_rms"), 1)
                act.wait_ge(S("first_rms"), 1)

            @block.tensor
            def _(pe):
                pe.wait_ge(S("load_once"), 48)
                for k in range(KD):
                    pe.wait_ge(S("first_sq"), k + 1)
                    last = nc.tensor.matmul(ps[:, 7, 0:N], C("ones"), SQ[:, k, :], start=k == 0, stop=k == KD - 1)
                last.then_inc(S("first_ss"), 1)
                pe.wait_ge(S("first_ss"), 1)

        with nc.Fori(0, L) as layer:
            def dram(name, group=t_in):
                a = group[name][bass.ds(layer, 1)]
                k = len(a.shape)
                if k == 3:
                    return a.rearrange("o p a -> (o p) a")
                if k == 4:
                    return a.rearrange("o p a b -> (o p) a b")
                return a.rearrange("o p a b c -> (o p) a b c")

            def dram_out(name):
                return dram(name, t_out)

            with nc.Block() as block:
                @block.sync
                def _(sp):
                    def slot(s):
                        if s >= RING:
                            sp.wait_ge(*at("gemm_done", slot_done(s - RING)))
                        src = t_in["w"][bass.ds(layer, 1), s].rearrange("o p a -> (o p) a")
                        sp.dma_start(ring[:, s % RING, :], src).then_inc(S(f"slot_full{s % RING}"), 16)

                    def cache(b):
                        at_b = [sp.value_load(pages[0:1, b * PAGES + p:b * PAGES + p + 1], min_val=0, max_val=POOL - 1)
                                for p in range(PAGES)]
                        if b >= KV_SLOTS:
                            sp.wait_ge(*at("mla_pv", b - KV_SLOTS + 1))
                        for p, page in enumerate(at_b):
                            src = t_in["pool"][bass.ds(layer, 1), bass.ds(page, 1)].rearrange("o g p a -> (o g p) a")
                            sp.dma_start(kv[b % KV_SLOTS][:, p, :], src).then_inc(S(f"kv_full{b % KV_SLOTS}"), 16)

                    for s in range(N_IN):
                        slot(s)
                    for b in range(KV_SLOTS - 1):
                        cache(b)
                    for s in range(N_IN, LENT):
                        slot(s)
                    sp.wait_ge(*at("gemm_done", slot_done(LENT + 1 - RING)))
                    for b in range(KV_SLOTS - 1, NB):
                        cache(b)
                    sp.wait_ge(*at("mla_pv", KV_SLOTS))
                    for s in range(LENT, NSLOT):
                        slot(s)

                @block.gpsimd
                def _(pool):
                    dma(pool, "load_vec", vec[:, :], dram("vec"))
                    dma(pool, "load_shift", r_hs[:, :, :], dram("shift"))
                    dma(pool, "load_mat", mat[:, :], dram("mat"))
                    dma(pool, "load_gla", g_s0[:, :, :], dram("gla"))
                    dma(pool, "load_m0", l_m0[0:4, :], dram("ml_m"))
                    pool.wait_ge(*at("gla_state"))
                    dma(pool, "stores", dram_out("gla_p"), g_st[:, NCH, :])
                    dma(pool, "stores", dram_out("gla_s"), g_s1[:, :, :])
                    pool.wait_ge(*at("mla_norm"))
                    dma(pool, "stores", dram_out("ckv"), m_ck[:, :])
                    dma(pool, "stores", dram_out("kpe"), m_kp[0:32, :])
                    pool.wait_ge(*at("mla_done"))
                    pool.wait_ge(*at("stores", 64))
                    dma(pool, "load_ml", l_c0[:, :, :], dram("ml_c"))
                    dma(pool, "load_ml", l_n0[:, :, :], dram("ml_n"))
                    pool.wait_ge(*at("ml_state"))
                    dma(pool, "stores_ml", dram_out("ml_c_s"), l_c0[:, :, :])
                    dma(pool, "stores_ml", dram_out("ml_n_s"), l_n0[:, :, :])
                    dma(pool, "stores_ml", dram_out("ml_c_p"), l_cp[:, :, :])
                    dma(pool, "stores_ml", dram_out("ml_n_p"), l_np[:, :])
                    dma(pool, "stores_ml", dram_out("ml_m_ps"), l_mo[0:4, :])
                    pool.wait_ge(*at("stores_ml", 80))
                    pool.wait_ge(*at("ml_done"))
                    dma(pool, "load_rw", r_s0[:, :, :], dram("rwkv"))
                    pool.wait_ge(*at("rw_state"))
                    dma(pool, "stores_rw", dram_out("rwkv_s"), r_s0[:, :, :])
                    dma(pool, "stores_rw", dram_out("rwkv_p"), r_st[:, :, :])
                    dma(pool, "stores_rw", dram_out("shift_ps"), r_sh[:, :, :])
                    pool.wait_ge(*at("rw_done"))
                    pool.wait_ge(*at("stores_rw", 48))
                    dma(pool, "load_mem", c_mem[:, :, :], t_in["mem"])
                    for i in range(2 * NB):
                        if i >= 4:
                            pool.wait_ge(*at("ca_ss_s", i - 3) if i < 4 + NB else at("ca_o_s", i - 3 - NB))
                        src = t_in["mem_k" if i < NB else "mem_v"][bass.ds(layer, 1), i % NB].rearrange("o p a -> (o p) a")
                        dma(pool, f"ca_full{i % 4}", c_kv[i % 4][:, :], src)
                        if i == 3:
                            read_done(pool, "mem_v1")
                            dma(pool, "stores_mem", dram_out("mem_kt"), c_mkt[:, :, :])
                            dma(pool, "stores_mem", dram_out("mem_v"), c_mv[:, :, :])
                    pool.wait_ge(*at("ca_oc_s"))
                    pool.wait_ge(*at("stores_mem", 32))
                    dma(pool, "load_conv", f_s[:, :, :], dram("conv"))
                    pool.wait_ge(*at("conv_state", KF))
                    dma(pool, "stores_conv", dram_out("conv_ps"), f_o[:, :, :])
                    pool.wait_ge(*at("stores_conv", 16))

                @block.tensor
                def _(pe):
                    mm = nc.tensor.matmul

                    def add(out, lhs, rhs):
                        return mm(out, lhs, rhs, start=False, stop=True, skip_group_check=True)

                    def put(out, lhs, rhs):
                        return mm(out, lhs, rhs, start=True, stop=True, skip_group_check=True)

                    def turn(out, in_):
                        k = in_.shape[0]
                        return nc.tensor.transpose(out, in_, ident[0:k, 0:k])

                    fences = [0]

                    def fence(ins):
                        fences[0] += 1
                        ins.then_inc(S("rows_free"), 1)
                        pe.wait_ge(*at("rows_free", fences[0]))

                    def block_of(i):
                        return ring[:, i // SLOT % RING, i % SLOT * P:(i % SLOT + 1) * P]

                    arrived = [0]

                    def gemm(g, rhs, lhs=None, width=N, normed=None):
                        stage, _, first, n, _ = TILES[g]
                        if g >= GEMM_BANKS:
                            h = g - GEMM_BANKS
                            pe.wait_ge(*at("bank_read_" + READER[h], READ_NO[h]))
                        bank = g % GEMM_BANKS
                        if lhs is None:
                            for k in range(n):
                                slot_here(first + k)
                                if normed:
                                    pe.wait_ge(*at(normed + "_done", k + 1))
                                last = mm(ps[:, bank, 0:width], block_of(first + k), rhs(k), start=k == 0, stop=k == n - 1)
                        else:
                            for k in range(n // 4):
                                slot_here(first + 4 * k)
                                i = first + 4 * k
                                four = ring[:, i // SLOT % RING, i % SLOT * P:(i % SLOT + 4) * P]
                                a = lhs(k)
                                last = mm(ps[0:a.shape[1], bank, :], a, four, start=k == 0, stop=k == n // 4 - 1)
                        last.then_inc(S("gemm_done"), 1)

                    def slot_here(i):
                        s = i // SLOT
                        if s >= arrived[0]:
                            pe.wait_ge(*at(f"slot_full{s % RING}", 16 * (s // RING + 1)))
                            arrived[0] = s + 1

                    def sum_squares(name, ks=range(KD), sq=SQ):
                        for k in ks:
                            pe.wait_ge(*at(name + "_sq", k + 1))
                            last = mm(ps[:, 7, 0:sq.shape[2]], C("ones"), sq[:, k, :], start=k == 0, stop=k == KD - 1)
                            if k == KD - 1:
                                last.then_inc(S(name + "_ss"), 1)

                    def projection(stage, rhs, norm):
                        for g, t in tiles_of(stage):
                            gemm(g, rhs)
                            if t[1]:
                                sum_squares(norm, [t[1] - 1])
                        sum_squares(norm, [KD - 1])

                    for g, t in tiles_of("in"):
                        gemm(g, lambda k: H[:, k, :], normed="pre_mix" if t[1] == 0 else None)
                    read_done(pe, "in")
                    pe.wait_ge(*at("load_mat", 16))
                    put(ps[:, 4, 0:N], M("gate2", 0, P, GLO_AT, GLO_AT + 16), PR[GLO_AT:GLO_AT + 16, MIX1, :])\
                        .then_inc(S("gla_z"), 1)
                    for g, t in tiles_of("in_tok"):
                        c0, n = TT[t[1]]
                        gemm(g, None, lhs=lambda k: H[:, k, c0:c0 + n])

                    read_done(pe, "in_tok")
                    pe.wait_ge(*at("gla_k"))
                    for i, (c0, n) in enumerate(TT):
                        last = turn(ps[0:n, 3, i * P:(i + 1) * P], g_ke[:, c0:c0 + n])
                    last.then_inc(S("gla_turned"), 1)
                    for h in range(4):
                        r = slice(32 * h, 32 * h + 32)
                        if h:
                            fence(last)
                        for i, (c0, n) in enumerate(TT):
                            last = put(ps[0:n, i, h * n:(h + 1) * n], g_k[r, c0:c0 + n], g_q[r, c0:c0 + n])
                    last.then_inc(S("gla_att"), 1)
                    pe.wait_ge(*at("gla_kt"))
                    for odd in range(2):
                        b0 = 64 * odd
                        for h in range(4):
                            r = slice(32 * h, 32 * h + 32)
                            for c in range(odd, NCH, 2):
                                last = put(ps[r, 4, c * 64:(c + 1) * 64], g_ktok[b0:b0 + 64, c // 2, r],
                                           VT[b0:b0 + 64, c // 2, h * 64:(h + 1) * 64])
                        if not odd:
                            fence(last)
                    for h in range(4):
                        r = slice(32 * h, 32 * h + 32)
                        last = put(ps[r, 5, :], g_ktok[0:NS, 2, r], g_vb[0:NS, h, :])
                    last.then_inc(S("gla_ds"), 1)
                    pe.wait_ge(*at("gla_attm"))
                    pe.wait_ge(*at("gla_state"))
                    o_heads = [(h, slice(32 * h, 32 * h + 32), ps[64 * (h % 2):64 * (h % 2) + 64, 6 + h // 2, :]) for h in range(4)]
                    for h, r, out in o_heads:
                        for i, (c0, n) in enumerate(TT[:2]):
                            last = put(out[:, c0:c0 + n], VT[0:n, i, h * 64:(h + 1) * 64], g_att[0:n, i, h * n:(h + 1) * n])
                            for c in (2 * i, 2 * i + 1):
                                if c:
                                    last = add(out[:, c * CH:(c + 1) * CH], g_st[r, c, :], g_q[r, c * CH:(c + 1) * CH])
                    fence(last)
                    for h, r, out in o_heads:
                        last = put(out[:, TP:N], VT[0:NS, 2, h * 64:(h + 1) * 64], g_att[0:NS, 2, h * NS:(h + 1) * NS])
                    fence(last)
                    for h, r, out in o_heads:
                        for b in range(NB):
                            j = TP + b * TS
                            last = add(out[:, j:j + TS], g_s0[r, b, :], g_q[r, j:j + TS])
                    last.then_inc(S("gla_o"), 1)
                    pe.wait_ge(*at("gla_sq"))
                    for j in range(2):
                        last = put(ps[:, j, 0:N], C("blk64", P), SQ[:, j, :])
                    last.then_inc(S("gla_ss"), 1)

                    pe.wait_ge(*at("mla_sq"))
                    mm(ps[:, 2, 0:N], C("ones"), O[:, 5, :], start=True, stop=False)
                    mm(ps[:, 2, 0:N], C("ones"), O[:, 6, :], start=False, stop=True)
                    put(ps[:, 3, 0:N], C("ones"), O[:, 7, :]).then_inc(S("mla_ss"), 1)
                    pe.wait_ge(*at("mla_cq"))
                    for j in range(4):
                        for k in range(2):
                            last = mm(ps[:, 2 + j, 0:N], M("uq", k * 512 + j * P, k * 512 + (j + 1) * P), m_cqn[:, k, :],
                                      start=k == 0, stop=k == 1)
                    pe.wait_ge(*at("gla_done"))
                    pe.wait_ge(*at("mla_norm"))
                    for i, (c0, n) in enumerate(TT):
                        last = turn(ps[0:n, 6, i * P:(i + 1) * P], m_ck[:, c0:c0 + n])
                    last.then_inc(S("mla_q"), 1)
                    pe.wait_ge(*at("mla_qn"))
                    for h in range(4):
                        hb, hp = 64 * (h % 2), h // 2
                        last = put(ps[:, h, 0:N], M("uk", hp * P, (hp + 1) * P, hb, hb + 64), m_qn[hb:hb + 64, hp, :])
                    last.then_inc(S("mla_ql"), 1)
                    pe.wait_ge(*at("mla_qlc"))
                    for qt in range(2):
                        nk = (qt + 1) * P
                        q = slice(qt * P, (qt + 1) * P)
                        for h in (0, 2, 1, 3):
                            if h == 1:
                                fence(last)
                            r = slice(32 * h, 32 * h + 32)
                            out = ps[:, 2 * qt + h // 2, h % 2 * 256:h % 2 * 256 + nk]
                            put(out, m_ql[:, h, q], m_ck[:, 0:nk])
                            add(out, m_qp[r, q], m_kp[r, 0:nk])
                            last = add(out[:, q], ident, C("bias_tok", P))
                        last.then_inc(S("mla_s"), 1)
                    for qt in range(2):
                        pe.wait_ge(*at("mla_pn", qt + 1))
                        for b in range(qt + 1):
                            for h in range(4):
                                last = turn(ps[:, 4 + b, h * P:(h + 1) * P], m_p[qt][:, h, b * P:(b + 1) * P])
                        last.then_inc(S("mla_pt"), 1)
                        pe.wait_ge(*at("mla_ptc", qt + 1))
                        if qt:
                            pe.wait_ge(*at("mla_olc"))
                        for h in range(4):
                            for b in range(qt + 1):
                                last = mm(ps[:, 6, h * P:(h + 1) * P], m_cktok[:, b, :], m_pt[:, b, h, :],
                                          start=b == 0, stop=b == qt)
                        last.then_inc(S("mla_ol"), 1)
                    pe.wait_ge(*at("mla_qs"))
                    def q_rows(b, k):
                        c = 64 * b + 48 - 16 * k
                        return m_qz[:, c:c + 64]

                    for b in range(NB):
                        out = ps[64 * (b % 2):64 * (b % 2) + 64, 7, NS * (b // 2):NS * (b // 2) + NS]
                        mm(out, q_rows(b, 0), m_ck[:, TP:N], start=b < 2, stop=False, skip_group_check=True)
                        add(out, m_qpz[0:32, 64 * b:64 * b + 64], m_kp[0:32, TP:N])
                    add(ps[:, 7, 0:P], ident, C("bias_own", P)).then_inc(S("mla_own"), 1)

                    def turns(b, j):
                        n = 5 * b + j
                        if j == 0:
                            pe.wait_ge(*at("rotated_packed", b + 1))
                        if n >= 2:
                            pe.wait_ge(*at("pages_copied", n - 1))
                        for i in range(4):
                            src = kv[b % KV_SLOTS][:, 4 * i + j - 1, 0:P] if j else m_kr[b % 2][:, i * P:(i + 1) * P]
                            last = turn(ps[:, 4 + n % 2, i * P:(i + 1) * P], src)
                        last.then_inc(S("pages_turned"), 1)

                    def scores(b, j):
                        out = ps[64 * (b % 2):64 * (b % 2) + 64, b // 2, :]
                        if j == 0:
                            pe.wait_ge(*at("pages_copied", 5 * b + 1))
                            mm(out, m_qpz[:, 64 * b:64 * b + 64], m_krt, start=True, stop=False)
                        pe.wait_ge(*at("pages_copied", 5 * b + j + 2))
                        last = mm(out, q_rows(b, j), m_kt[:, j, :], start=False, stop=j == 3)
                        last.then_inc(S("page_scores"), 1)

                    def maxima(g):
                        pe.wait_ge(*at("mla_top", g + 1))
                        turn(ps[0:1, 7, 0:P], m_top[:, g:g + 1]).then_inc(S("mla_topt"), 1)

                    def maxima_back(g):
                        pe.wait_ge(*at("mla_max_s", g + 1))
                        turn(ps[:, 7, P:P + 1], m_row).then_inc(S("mla_maxt"), 1)

                    def attend(g):
                        pe.wait_ge(*at("mla_p_s", g + 1))
                        for i in range(4):
                            turn(ps[:, 6, i * P:(i + 1) * P], m_ps[:, i * P:(i + 1) * P])
                        turn(ps[0:NS, 7, 2 * P:3 * P], m_po).then_inc(S("mla_pt_s"), 1)
                        pe.wait_ge(*at("mla_pts", g + 1))
                        put(ps[0:64, 7, 384:385], C("sum_own", 64), m_sums[:, 0:1])
                        add(ps[0:64, 7, 384:385], C("sum_own", 64), m_sums[:, 1:2])
                        for b in (2 * g, 2 * g + 1):
                            f = b % 2
                            out = ps[32 * f:32 * f + 16, 7, P:2 * P]
                            for p in range(PAGES):
                                r = 64 * f + 16 * (p % 4)
                                mm(out, m_pts[:, p // 4, r:r + 16], kv[b % KV_SLOTS][:, p, 0:P], start=p == 0, stop=False)
                            last = mm(out, m_pot[:, 64 * f:64 * f + 16], m_cktok[0:NS, 2, :], start=False, stop=True)
                            last.then_inc(S("mla_pv"), 1)

                    def outputs(g):
                        pe.wait_ge(*at("mla_os", g + 1))
                        turn(ps[:, 7, 0:64], m_os).then_inc(S("mla_ot"), 1)

                    for b in range(NB):
                        g = b // 2 - 1
                        turns(b, 0)
                        turns(b, 1)
                        for j in range(4):
                            if j < 3:
                                turns(b, j + 2)
                            scores(b, j)
                            if b % 2 == 0 and g >= 0:
                                if j == 0:
                                    maxima(g)
                                if j == 1:
                                    maxima_back(g)
                            elif b % 2 and g >= 0 and j == 0:
                                outputs(g)
                        if b % 2 == 0 and g >= 0:
                            attend(g)
                    g = NB // 2 - 1
                    maxima(g)
                    maxima_back(g)
                    attend(g)
                    outputs(g)
                    pe.wait_ge(*at("mla_ols", NB // 2))
                    for h in range(4):
                        hb = 64 * (h % 2)
                        last = put(ps[hb:hb + 64, h // 2, 0:N], M("uv", h * 64, (h + 1) * 64), m_ol[:, h, :])
                    last.then_inc(S("mla_o"), 1)

                    pe.wait_ge(*at("ml_exp"))
                    pe.wait_ge(*at("mla_done"))
                    for i, (c0, n) in enumerate(TT):
                        turn(ps[0:n, 0, i * 8:i * 8 + 4], l_g[0:4, c0:c0 + n])
                        turn(ps[0:n, 0, i * 8 + 4:i * 8 + 8], l_rows[0:4, L_WE + c0:L_WE + c0 + n])
                    for hp in range(2):
                        sel = C("sel_p", 2 * P, 4)[:, hp * P:(hp + 1) * P]
                        put(ps[:, 1 + hp, 0:N], sel, l_rows[0:4, L_EM:L_EM + N])
                        put(ps[:, 3, hp * NS:(hp + 1) * NS], sel, l_rows[0:4, L_WI:L_WI + NS])
                        put(ps[:, 3, 64 + hp * NB:64 + (hp + 1) * NB], sel, l_rows[0:4, L_SO:L_SO + NB])
                    for i, (c0, n) in enumerate(TT):
                        for hp in range(2):
                            c = i % 2 * 256 + hp * P
                            last = turn(ps[0:n, 4 + i // 2, c:c + P], PR[:, MK + hp, c0:c0 + n])
                    last.then_inc(S("ml_turned"), 1)
                    pe.wait_ge(*at("ml_k"))
                    for h in range(4):
                        if h >= 2:
                            pe.wait_ge(*at("ml_w", h - 1))
                        bias, qk = ps[:, 4 + h % 2, :], ps[:, 6 + h % 2, :]
                        sel = C("sel_h", 4 * P, 4)[:, h * P:(h + 1) * P]
                        put(bias[:, 0:416], ident, C("bias_m", 416))
                        add(bias[:, 0:256], sel, l_nm[0:4, 0:TP])
                        add(bias[:, 256:384], sel, l_nm[0:4, P:TP])
                        add(bias[:, 384:416], sel, l_nm[0:4, TP:N])
                        r, hp = slice(64 * (h % 2), 64 * (h % 2) + 64), h // 2
                        k, q = PR[r, MK + hp, :], PR[r, MQ + hp, :]
                        put(qk[:, 0:256], k[:, 0:P], q[:, 0:TP])
                        put(qk[:, 256:384], k[:, P:TP], q[:, P:TP])
                        put(qk[0:NS, 384:416], k[:, TP:N], q[:, TP:N]).then_inc(S("ml_s"), 1)
                    pe.wait_ge(*at("ml_w", 4))
                    for h in range(4):
                        r, hp = slice(64 * (h % 2), 64 * (h % 2) + 64), h // 2
                        for out, lhs, st in (
                                (ps[r, 4 + hp, :], lambda i, n: VT[0:n, i, 256 + h * 64:256 + (h + 1) * 64],
                                 lambda b: l_c0[r, hp, b * 64:(b + 1) * 64]),
                                (ps[r, 6 + hp, :], lambda i, n: C("ones", 64, n), lambda b: l_nbc[r, hp, b, :])):
                            put(out[:, 0:P], lhs(0, P), l_w[:, h, 0:P])
                            put(out[:, P:TP], lhs(0, P), l_w[:, h, P:TP])
                            add(out[:, P:TP], lhs(1, P), l_w[:, h, 256:384])
                            put(out[:, TP:N], lhs(2, NS), l_w[0:NS, h, 384:416])
                            for b in range(NB):
                                last = add(out[:, TP + b * TS:TP + (b + 1) * TS], st(b), l_qw[r, hp, b * TS:(b + 1) * TS])
                    last.then_inc(S("ml_num"), 1)
                    pe.wait_ge(*at("ml_em"))
                    for h in range(4):
                        r, hp = slice(64 * (h % 2), 64 * (h % 2) + 64), h // 2
                        hc = slice(h * 64, (h + 1) * 64)
                        for i in range(2):
                            mm(ps[r, 3, hp * 64:(hp + 1) * 64], l_kw[:, i, hc], VT[:, i, 256 + h * 64:256 + (h + 1) * 64],
                               start=i == 0, stop=i == 1)
                        for i in range(2):
                            mm(ps[r, 3, P + hp:P + hp + 1], l_kw[:, i, hc], C("ones", 1), start=i == 0, stop=i == 1)
                        put(ps[r, 3, 136 + hp * NB:136 + (hp + 1) * NB], l_kw[0:NS, 2, hc], C("batch", NB, NS))
                        last = put(ps[r, 1 + hp, :], l_kw[0:NS, 2, hc], l_vb[0:NS, h, :])
                    last.then_inc(S("ml_ds"), 1)
                    pe.wait_ge(*at("ml_h"))
                    for hp in range(2):
                        last = put(ps[:, 4 + hp, 0:N], C("blk64", P), l_h[:, hp, :])
                    last.then_inc(S("ml_mean"), 1)
                    pe.wait_ge(*at("ml_sq"))
                    for hp in range(2):
                        last = put(ps[:, 6 + hp, 0:N], C("blk64", P), l_den[:, hp, :])
                    last.then_inc(S("ml_ss"), 1)

                    pe.wait_ge(*at("rw_tw"))
                    pe.wait_ge(*at("ml_state"))
                    for hp in range(2):
                        c = slice(hp * P, (hp + 1) * P)
                        put(ps[:, hp, 0:N], M("wa", c.start, c.stop, 0, 64), r_tw[0:64, :])
                        put(ps[:, 2 + hp, 0:N], M("wa", c.start, c.stop, 64, P), SQ[64:P, 6, :])
                        last = put(ps[:, 4 + hp, 0:N], M("g2", c.start, c.stop), r_sg[:, :])
                    last.then_inc(S("rw_lora"), 1)
                    pe.wait_ge(*at("rw_kk"))
                    pe.wait_ge(*at("ml_r"))
                    for hp in range(2):
                        last = put(ps[:, 6 + hp, 0:N], C("blk64", P), r_t[:, hp, :])
                    last.then_inc(S("rw_kks"), 1)
                    pe.wait_ge(*at("rw_sig"))
                    gates = tiles_of("gate", "up")
                    for g, t in gates[0:4]:
                        gemm(g, lambda k: H[:, k, :])
                    pe.wait_ge(*at("rw_vec"))
                    for hp in range(2):
                        last = put(ps[:, 6 + hp, 0:N], C("blk64", P), r_bo[:, hp, :])
                    last.then_inc(S("rw_bonus"), 1)
                    halves = [(h, slice(64 * (h % 2), 64 * (h % 2) + 64), h // 2) for h in range(4)]
                    def rw_pairs(i):
                        c0, n = TT[i]
                        t = slice(c0, c0 + n)
                        if i == 1:
                            pe.wait_ge(*at("rw_tokc", 2))
                        if i == 2:
                            pe.wait_ge(*at("rw_st", 4))
                            pe.wait_ge(*at("rw_uc", 4))
                        for odd in range(2):
                            for bank, a, b in ((0, r_be, r_al), (1, r_al, r_be), (2, r_rk, r_al), (3, r_be, r_rh), (4, r_rk, r_rh)):
                                for h, r, hp in halves[odd::2]:
                                    last = put(ps[0:n, bank, h * n:(h + 1) * n], a[r, hp, t], b[r, hp, t])
                            if not odd:
                                fence(last)
                        last.then_inc(S("rw_pair"), 1)
                        for kind, src in ((0, r_al), (1, r_kk)):
                            for hp in range(2):
                                c = kind * 256 + hp * P
                                last = turn(ps[0:n, 5, c:c + P], src[:, hp, t])
                        last.then_inc(S("rw_tok"), 1)
                        pe.wait_ge(*at("rw_pairm", i + 1))
                        for kind, src in ((0, r_cs), (1, SQ[:, 4:6, :])):
                            for hp in range(2):
                                c = kind * 256 + hp * P
                                last = turn(ps[0:n, 0, c:c + P], src[:, hp, t])
                        last.then_inc(S("rw_tok"), 1)

                    def rw_x(level):
                        j, i = RW_LEVELS[level]
                        n, bank = TT[i][1], RW_BANKS[i][0]
                        pe.wait_ge(*at("rw_off", level + 1))
                        for h, r, hp in halves:
                            last = put(ps[0:n, bank, h * n:(h + 1) * n], r_off[i][0:n, h, 0:n], r_tm[i][0:n, h, 0:n])
                        last.then_inc(S("rw_x"), 1)

                    def rw_y(level):
                        j, i = RW_LEVELS[level]
                        n, (_, y, z) = TT[i][1], RW_BANKS[i]
                        pe.wait_ge(*at("rw_xc", level + 1))
                        for h, r, hp in halves:
                            put(ps[0:n, y, h * n:(h + 1) * n], r_tt[i][0:n, h, 0:n], r_x[i][0:n, h, 0:n])
                            last = put(ps[0:n, z, h * n:(h + 1) * n], r_x[i][0:n, h, 0:n], r_tt[i][0:n, h, 0:n])
                        last.then_inc(S("rw_y"), 1)

                    def rw_bg(i):
                        n, (bv, gt) = TT[i][1], RW_BG[i]
                        for h, r, hp in halves:
                            hc = slice(h * 64, (h + 1) * 64)
                            put(ps[0:n, bv, hc], r_bt[i][0:n, h, 0:n], r_tok[i][0:n, 3, hc])
                            last = put(ps[r, gt, hp * n:(hp + 1) * n], r_tok[i][0:n, 0, hc], r_tt[i][0:n, h, 0:n])
                        last.then_inc(S("rw_bg"), 1)

                    pe.wait_ge(*at("bank_read_act", gate_read(0, 3)))
                    rw_pairs(0)
                    rw_pairs(1)
                    pe.wait_ge(*at("rw_tokc", 4))
                    for level in range(0, 10, 2):
                        rw_x(level)
                        rw_x(level + 1)
                        rw_y(level)
                        rw_y(level + 1)
                    pe.wait_ge(*at("rw_t", 10))
                    rw_bg(0)
                    rw_bg(1)
                    pe.wait_ge(*at("rw_bo"))
                    for c in range(NCH):
                        i = c // 2
                        s = slice(64 * (c % 2), 64 * (c % 2) + 64)
                        cc = slice(c * CH, (c + 1) * CH)
                        pe.wait_ge(*at("rw_bgc", i + 1))
                        if c:
                            pe.wait_ge(*at("rw_st", c))
                        for h, r, hp in halves:
                            hc = slice(h * 64, (h + 1) * 64)
                            last = mm(ps[s, 0, hc], r_tt[i][s, h, s], r_bv[i][s, hc], start=h == 0, stop=c == 0,
                                      skip_group_check=True)
                        for odd in ((c % 2, 1 - c % 2) if c else ()):
                            if odd != c % 2:
                                fence(last)
                            for h, r, hp in halves[odd::2]:
                                last = add(ps[s, 0, h * 64:(h + 1) * 64], r_gt[i][r, hp, s], r_st[r, hp, :])
                        last.then_inc(S("rw_u"), 1)
                        pe.wait_ge(*at("rw_uc", c + 1))
                        tok = r_tok[i]
                        for h, r, hp in halves:
                            hc = slice(h * 64, (h + 1) * 64)
                            put(ps[r, 1, hp * 64:(hp + 1) * 64], tok[s, 1, hc], r_u[s, hc])
                            last = add(ps[r, 1, hp * 64:(hp + 1) * 64], tok[s, 2, hc], tok[s, 3, hc])
                        for h, r, hp in halves:
                            hc = slice(h * 64, (h + 1) * 64)
                            put(ps[r, 6 + hp, cc], r_u[s, hc], r_rb[i][s, h, s])
                            last = add(ps[r, 6 + hp, cc], tok[s, 3, hc], r_rkm[i][s, h, s])
                        if c:
                            fence(last)
                            for h, r, hp in halves:
                                last = add(ps[r, 6 + hp, cc], r_st[r, hp, :], r_rh[r, hp, cc])
                        last.then_inc(S("rw_ds"), 1)
                    rw_pairs(2)
                    rw_x(10)
                    rw_y(10)
                    pe.wait_ge(*at("rw_tokc", 6))
                    pe.wait_ge(*at("rw_t", 11))
                    rw_bg(2)
                    pe.wait_ge(*at("rw_bgc", 3))
                    pe.wait_ge(*at("load_rw", 16))
                    for h, r, hp in halves:
                        hc = slice(h * 64, (h + 1) * 64)
                        put(ps[r, 0, hp * NS:(hp + 1) * NS], r_bv[2][0:NS, hc], r_tt[2][0:NS, h, 0:NS])
                        for b in range(NB):
                            j = hp * NS + b * TS
                            last = add(ps[r, 0, j:j + TS], r_s0[r, hp, b * 64:(b + 1) * 64],
                                       r_gt[2][r, hp, b * TS:(b + 1) * TS])
                    last.then_inc(S("rw_u"), 1)
                    pe.wait_ge(*at("rw_uc", 5))
                    for hp in range(2):
                        last = turn(ps[0:NS, 1, hp * P:(hp + 1) * P], r_x[2][:, hp, 0:NS])
                    last.then_inc(S("rw_ut"), 1)
                    pe.wait_ge(*at("rw_utc"))
                    for h, r, hp in halves:
                        hc = slice(h * 64, (h + 1) * 64)
                        put(ps[r, 2 + hp, :], r_tok[2][0:NS, 1, hc], r_ub[0:NS, h, :])
                        add(ps[r, 2 + hp, :], r_tok[2][0:NS, 2, hc], r_vb[0:NS, h, :])
                        put(ps[r, 6 + hp, TP:N], r_u[0:NS, hc], r_rb[2][0:NS, h, 0:NS])
                        add(ps[r, 6 + hp, TP:N], r_tok[2][0:NS, 3, hc], r_rkm[2][0:NS, h, 0:NS])
                        for b in range(NB):
                            j = TP + b * TS
                            last = add(ps[r, 6 + hp, j:j + TS], r_s0[r, hp, b * 64:(b + 1) * 64], r_rh[r, hp, j:j + TS])
                    last.then_inc(S("rw_ds"), 1)
                    pe.wait_ge(*at("rw_yc"))
                    for hp in range(2):
                        last = put(ps[:, hp, 0:N], C("blk64", P), r_a[:, hp, :])
                    last.then_inc(S("rw_mean"), 1)
                    pe.wait_ge(*at("rw_c"))
                    for g, t in gates[4:6]:
                        gemm(g, lambda k: O[:, 2 * t[1][1] + k, :])
                    pe.wait_ge(*at("rw_sq"))
                    for hp in range(2):
                        last = put(ps[:, 4 + hp, 0:N], C("blk64", P), r_t[:, hp, :])
                    last.then_inc(S("rw_ss"), 1)

                    for g, t in gates[6:]:
                        if t == ("up", (0, 2)) + t[2:]:
                            pe.wait_ge(*at("rw_done"))
                        if t[0] == "gate":
                            gemm(g, lambda k: H[:, k, :])
                        else:
                            gemm(g, lambda k: O[:, 2 * t[1][1] + k, :])
                            if t[1] == MEM_SUMS_AT:
                                sum_squares("mem", sq=c_mkt)

                    for g, t in tiles_of("mem_k"):
                        gemm(g, lambda k: c_mem[:, k, :], width=MEM, normed="mem" if t[1] == 0 else None)

                    def mem_values(half, tok):
                        gemm(tiles_of(f"mem_v{half}")[tok][0], None, lhs=lambda k: c_mem[:, k, tok * P:(tok + 1) * P])

                    mem_values(0, 0)
                    mem_values(0, 1)

                    pe.wait_ge(*at("mixed", KD))
                    projection("out", lambda k: PR[:, k, :], "post_mix")

                    mem_values(1, 0)
                    sum_squares("pre_ca")
                    mem_values(1, 1)
                    for g, t in tiles_of("ca_q"):
                        gemm(g, lambda k: H[:, k, :], normed="pre_ca" if t[1] == 0 else None)
                    read_done(pe, "ca_q")
                    for qt in range(2):
                        q = slice(qt * P, (qt + 1) * P)
                        for h in range(4):
                            for j in range(2):
                                last = mm(ps[:, 2 * qt + h // 2, h % 2 * MEM:(h % 2 + 1) * MEM], O[:, 2 * h + j, q],
                                          c_mkt[:, 2 * h + j, :], start=j == 0, stop=j == 1)
                        last.then_inc(S("ca_s"), 1)
                    for qt in range(2):
                        pe.wait_ge(*at("ca_pn", qt + 1))
                        for b in range(2):
                            for h in range(4):
                                last = turn(ps[:, 4 + b, h * P:(h + 1) * P], c_p[qt][:, h, b * P:(b + 1) * P])
                        last.then_inc(S("ca_pt"), 1)
                        pe.wait_ge(*at("ca_ptc", qt + 1))
                        if qt:
                            pe.wait_ge(*at("ca_oc"))
                        for h in range(4):
                            for j in range(2):
                                d = 2 * h + j
                                for b in range(2):
                                    last = mm(ps[:, 6 + d // 4, d % 4 * P:(d % 4 + 1) * P], c_mv[:, b, d * P:(d + 1) * P],
                                              c_pt[:, b, h, :], start=b == 0, stop=b == 1)
                        last.then_inc(S("ca_o"), 1)
                    pe.wait_ge(*at("ca_oc", 2))
                    def mem_scores(g):
                        for b in (2 * g, 2 * g + 1):
                            pe.wait_ge(*at(f"ca_full{b % 4}", 16 * (b // 4 + 1)))
                            k_t = c_kv[b % 4].rearrange("p (a s) -> p a s", a=KD)
                            for h in range(4):
                                for j in range(2):
                                    last = mm(ps[32 * h:32 * h + 32, g, b % 2 * MEM:(b % 2 + 1) * MEM], O[:, 2 * h + j, TP:N],
                                              k_t[:, 2 * h + j, :], start=j == 0, stop=j == 1)
                            last.then_inc(S("ca_ss_s"), 1)

                    def mem_turns(g):
                        pe.wait_ge(*at("ca_pn_s", g + 1))
                        for b in (2 * g, 2 * g + 1):
                            for s in range(2):
                                c = b % 2 * 256 + s * P
                                last = turn(ps[:, 4 + g, c:c + P], c_ps[:, b, s * P:(s + 1) * P])
                        last.then_inc(S("ca_pt_s"), 1)

                    for g in range(NB // 2):
                        mem_scores(g)
                        if g:
                            mem_turns(g - 1)
                    mem_turns(NB // 2 - 1)
                    for b in range(NB):
                        i = NB + b
                        pe.wait_ge(*at("ca_pts", b // 2 + 1))
                        pe.wait_ge(*at(f"ca_full{i % 4}", 16 * (i // 4 + 1)))
                        v_b = c_kv[i % 4].rearrange("p (s d) -> p s d", s=2)
                        for s in range(2):
                            for h in range(4):
                                r = slice(32 * h, 32 * h + 32)
                                last = mm(ps[r, 0, 0:256], c_pts[:, b, s, r], v_b[:, s, 256 * h:256 * h + 256],
                                          start=b == 0 and s == 0, stop=b == NB - 1 and s == 1)
                        last.then_inc(S("ca_o_s"), 1)
                    pe.wait_ge(*at("ca_po"))
                    for j in range(2):
                        last = turn(ps[:, 1, j * P:(j + 1) * P], c_po[:, j * P:(j + 1) * P])
                    last.then_inc(S("ca_ot"), 1)
                    pe.wait_ge(*at("ca_oc_s"))
                    projection("ca_o", lambda k: H[:, k, :], "post_ca")

                    sum_squares("pre_ffn")
                    for g, t in tiles_of("ffn_a", "ffn_g"):
                        gemm(g, lambda k: H[:, k, :], normed="pre_ffn" if t[:2] == ("ffn_a", 0) else None)
                    read_done(pe, "ffn_g")
                    projection("down", lambda k: f_f[:, k, :], "post_ffn")
                    sum_squares("next")

                @block.scalar
                def _(act):
                    step = Steps(act, "act_step")
                    A = nc.scalar.activation

                    def copy(out, in_, signal=None):
                        step(A(out, in_, ACT.Copy), signal)

                    def wait(name, n=1):
                        act.wait_ge(*at(name, n))

                    def tile_ready(g):
                        wait("gemm_done", g + 1)

                    def rms(name, rs=RS):
                        wait(name + "_ss")
                        step(A(rs, ps[:, 7, 0:rs.shape[1]], ACT.Sqrt, bias=eps, scale=1.0 / D), name + "_rstd")

                    def squares(name, src, gained, sq=SQ, after=None):
                        for k in range(KD):
                            if after:
                                wait(after, k + 1)
                            step(A(sq[:, k, :], src[:, k, :], ACT.Square), name + "_sq")
                            step(A(gained[:, k, :], src[:, k, :], ACT.Identity, scale=V(name, k)))

                    def into(stage, dst, name=None):
                        for g, t in tiles_of(stage):
                            tile_ready(g)
                            src = ps[:, g % GEMM_BANKS, 0:N]
                            if name:
                                step(A(SQ[:, t[1], :], src, ACT.Square), name + "_sq")
                                step(A(dst[:, t[1], :], src, ACT.Identity, scale=V(name, t[1])), "bank_read_act")
                            else:
                                copy(dst[:, t[1], :], src, "bank_read_act")

                    wait("load_vec", 16)
                    for k in range(KD):
                        step(A(H[:, k, :], X[:, k, :], ACT.Identity, scale=V("pre_mix", k)), "pre_mix_gained")
                    for g, t in tiles_of("in"):
                        tile_ready(g)
                        j, src = t[1], ps[:, g % GEMM_BANKS, :]
                        if j >= RW:
                            if j == RW:
                                wait("halo")
                            step(A(ext_prompt(RE[:, j - RW, :]), src[:, 0:TP], ACT.Copy))
                            copy(ext_sample(RE[:, j - RW, :]), per_batch(src[:, TP:N], TS), "bank_read_act")
                        else:
                            f = ACT.Silu if j in (GR, GR + 1) else ACT.Sigmoid if j in (MO, MO + 1) else ACT.Copy
                            step(A(PR[:, j, :], src[:, 0:N], f), "bank_read_act")
                    wait("gla_abs")
                    step(A(g_t3, g_t2, ACT.Exp))
                    step(A(g_t3, g_t3, ACT.Ln, bias=one), "gla_log")
                    for g, t in tiles_of("in_tok"):
                        if t[1] == 1:
                            wait("gla_cum")
                            step(A(g_eb, g_cum, ACT.Exp, scale=1.0 / 16))
                            step(A(g_enb, g_cum, ACT.Exp, scale=-1.0 / 16))
                            step(A(g_ebe, g_t2, ACT.Exp, scale=1.0 / 16), "gla_exp")
                        tile_ready(g)
                        n = TT[t[1]][1]
                        copy(VT[0:n, t[1], :], ps[0:n, g % GEMM_BANKS, :], "bank_read_act")

                    step(A(O[:, 5:8, :], PR[:, CQ:CQ + 3, :], ACT.Square), "mla_sq")
                    wait("gla_o")
                    step(A(SQ[:, 0:2, :], ps[:, 6:8, 0:N], ACT.Square), "gla_sq")
                    wait("gla_ss")
                    step(A(g_ra, ps[:, 0:2, 0:N], ACT.Ln, bias=eps, scale=1.0 / 64))
                    step(A(g_ra, g_ra, ACT.Exp, scale=-0.5), "gla_r")

                    wait("mla_ss")
                    step(A(m_rr[:, 0, :], ps[:, 2, 0:N], ACT.Ln, bias=eps, scale=1.0 / 256))
                    step(A(m_rr[:, 1, :], ps[:, 3, 0:N], ACT.Ln, bias=eps, scale=1.0 / 128))
                    step(A(m_rr, m_rr, ACT.Exp, scale=-0.5), "mla_r")
                    wait("mla_ql")
                    copy(m_ql, ps[:, 0:4, 0:N], "mla_qlc")
                    for qt in range(2):
                        nk = (qt + 1) * P
                        wait("mla_max", qt + 1)
                        for h in range(4):
                            c = h % 2 * 256
                            step(A(m_p[qt][:, h, 0:nk], ps[:, 2 * qt + h // 2, c:c + nk], ACT.Exp, bias=m_nm[qt][:, h:h + 1],
                                   scale=SCALE_MLA, accum_out=m_sum[qt][:, h:h + 1]), "mla_p" if h == 3 else None)
                    for qt in range(2):
                        wait("mla_pt", qt + 1)
                        for b in range(qt + 1):
                            copy(m_pt[:, b, :, :], ps[:, 4 + b, :].rearrange("p (h t) -> p h t", h=4),
                                 "mla_ptc" if b == qt else None)
                        wait("mla_ol", qt + 1)
                        copy(m_ol[:, :, qt * P:(qt + 1) * P], ps[:, 6, :].rearrange("p (h t) -> p h t", h=4), "mla_olc")
                    def exps(g):
                        wait("mla_nm", g + 1)
                        step(A(m_ps, ps[:, g, :], ACT.Exp, bias=m_top[:, g:g + 1], scale=SCALE_MLA, accum_out=m_sums[:, 0:1]))
                        step(A(m_po, m_own[:, NS * g:NS * g + NS], ACT.Exp, bias=m_top[:, g:g + 1], scale=SCALE_MLA,
                               accum_out=m_sums[:, 1:2]), "mla_p_s")

                    wait("ml_abs")
                    step(A(l_t[0:4, :], l_t[0:4, :], ACT.Exp))
                    step(A(l_t[0:4, :], l_t[0:4, :], ACT.Ln, bias=one[0:4, :]), "ml_log")
                    for b in range(NB):
                        if b == 3:
                            wait("ml_rows")
                            step(A(l_rows[0:4, :], l_rows[0:4, :], ACT.Exp), "ml_exp")
                        for j in range(5):
                            n = 5 * b + j
                            wait("pages_turned", n + 1)
                            if b:
                                wait("page_scores", 4 * (b - 1) + max(j, 1))
                            copy(m_kt[:, j - 1, :] if j else m_krt, ps[:, 4 + n % 2, :], "pages_copied")
                        if b % 2 == 0 and b:
                            exps(b // 2 - 1)
                    exps(NB // 2 - 1)
                    wait("mla_o")
                    copy(O[:, 2:4, :], ps[:, 0:2, 0:N], "mla_done")

                    wait("ml_gw")
                    for h in range(4):
                        wait("ml_s", h + 1)
                        for a, b, i, n in ((0, 256, 0, P), (256, 384, 1, P), (384, 416, 2, NS)):
                            step(A(l_w[0:n, h, a:b], ps[0:n, 4 + h % 2, a:b], ACT.Exp, bias=l_gw[0:n, i * 8 + h:i * 8 + h + 1]),
                                 "ml_e" if i == 2 else None)
                    wait("rw_pm")
                    step(A(r_tw[0:64, :], SQ[0:64, 6, :], ACT.Tanh))
                    step(A(r_sg, SQ[:, 7, :], ACT.Sigmoid), "rw_tw")
                    wait("ml_c")
                    step(A(l_den, l_h, ACT.Square), "ml_sq")
                    wait("ml_ss")
                    step(A(l_r, ps[:, 6:8, 0:N], ACT.Ln, bias=eps, scale=1.0 / 64))
                    step(A(l_r, l_r, ACT.Exp, scale=-0.5), "ml_r")

                    wait("rw_lora")
                    for hp in range(2):
                        step(A(r_s[:, hp, :], ps[:, hp, 0:N], ACT.Sigmoid, bias=V("w0", hp)))
                        step(A(r_a[:, hp, :], ps[:, 2 + hp, 0:N], ACT.Sigmoid, bias=V("a0", hp)))
                    copy(r_g, ps[:, 4:6, 0:N], "rw_sig")
                    wait("rw_clamped")
                    step(A(r_t, r_t, ACT.Ln))
                    step(A(r_t, r_t, ACT.Exp, bias=C("kk_b"), scale=-0.5), "rw_inv")
                    wait("rw_cum")
                    step(A(r_rh, r_cs, ACT.Exp, scale=-DECAY))
                    step(A(r_cs, r_cs, ACT.Exp, scale=DECAY))
                    step(A(r_csx, r_csx, ACT.Exp, scale=-DECAY))
                    step(A(r_cse, r_cse, ACT.Exp, scale=-DECAY), "rw_exp")
                    for n in range(4):
                        g, t = tiles_of("gate")[n]
                        tile_ready(g)
                        step(A(first_gates[:, n, :], ps[:, g % GEMM_BANKS, 0:N], ACT.Sigmoid), "bank_read_act")

                    def rw_tokens(i):
                        n = TT[i][1]
                        wait("rw_tok", 2 * i + 1)
                        copy(r_tok[i][0:n, 0:2, :], ps[0:n, 5, :].rearrange("p (a b) -> p a b", a=2), "rw_tokc")
                        wait("rw_tok", 2 * i + 2)
                        copy(r_tok[i][0:n, 2:4, :], ps[0:n, 0, :].rearrange("p (a b) -> p a b", a=2), "rw_tokc")

                    def rw_level(level):
                        j, i = RW_LEVELS[level]
                        n = TT[i][1]
                        wait("rw_x", level + 1)
                        copy(r_x[i][0:n, :, 0:n], ps[0:n, RW_BANKS[i][0], 0:4 * n].rearrange("p (h s) -> p h s", h=4), "rw_xc")

                    def rw_bv_gt(i):
                        n, (bv, gt) = TT[i][1], RW_BG[i]
                        wait("rw_bg", i + 1)
                        copy(r_bv[i][0:n, :], ps[0:n, bv, 0:256])
                        copy(r_gt[i][:, :, 0:n], ps[:, gt, 0:2 * n].rearrange("p (a b) -> p a b", a=2), "rw_bgc")

                    rw_tokens(0)
                    rw_tokens(1)
                    for level in range(10):
                        rw_level(level)
                    rw_bv_gt(0)
                    rw_bv_gt(1)
                    for c in range(NCH):
                        s = slice(64 * (c % 2), 64 * (c % 2) + 64)
                        wait("rw_u", c + 1)
                        copy(r_u[s, :], ps[s, 0, 0:256], "rw_uc")
                    rw_tokens(2)
                    rw_level(10)
                    rw_bv_gt(2)
                    wait("rw_u", 5)
                    copy(r_x[2][:, 0:2, 0:NS], ps[:, 0, 0:2 * NS].rearrange("p (a b) -> p a b", a=2), "rw_uc")
                    wait("rw_ut")
                    copy(r_u[0:NS, :], ps[0:NS, 1, 0:256], "rw_utok")
                    wait("rw_ds", 5)
                    copy(r_a, ps[:, 6:8, 0:N], "rw_yc")
                    wait("rw_c")
                    step(A(r_t, r_a, ACT.Square), "rw_sq")
                    wait("rw_ss")
                    step(A(r_s, ps[:, 4:6, 0:N], ACT.Ln, bias=eps_r, scale=1.0 / 64))
                    step(A(r_s, r_s, ACT.Exp, scale=-0.5), "rw_r")

                    for g, t in tiles_of("gate")[4:]:
                        d, n = t[1]
                        if d >= 2:
                            wait("bank_read_dve", 4 * (d - 1) + n + 1)
                        tile_ready(g)
                        step(A(SQ[:, n, :], ps[:, g % GEMM_BANKS, 0:N], ACT.Sigmoid), "bank_read_act")
                        if (d, n) == MEM_SQUARES_AT:
                            wait("load_mem", 16)
                            squares("mem", c_mem, c_mem, c_mkt)
                        if (d, n) == MEM_SUMS_AT:
                            rms("mem", c_rs)

                    for g, t in tiles_of("mem_k"):
                        tile_ready(g)
                        copy(c_mkt[:, t[1], :], ps[:, g % GEMM_BANKS, 0:MEM], "bank_read_act")

                    def mem_values(half, tok):
                        g, t = tiles_of(f"mem_v{half}")[tok]
                        tile_ready(g)
                        copy(c_mv[:, tok, half * 512:(half + 1) * 512], ps[:, g % GEMM_BANKS, :], "bank_read_act")

                    mem_values(0, 0)
                    mem_values(0, 1)

                    into("out", O, "post_mix")
                    rms("post_mix")

                    squares("pre_ca", X, H, after="post_mix_done")
                    mem_values(1, 0)
                    rms("pre_ca")
                    mem_values(1, 1)
                    into("ca_q", O)
                    for qt in range(2):
                        wait("ca_max", qt + 1)
                        for h in range(4):
                            c, k = h % 2 * MEM, 4 * qt + h
                            step(A(c_p[qt][:, h, :], ps[:, 2 * qt + h // 2, c:c + MEM], ACT.Exp, bias=c_nm[:, k:k + 1],
                                   scale=SCALE_CA, accum_out=c_sum[:, k:k + 1]), "ca_p" if h == 3 else None)
                    for qt in range(2):
                        wait("ca_pt", qt + 1)
                        copy(c_pt, ps[:, 4:6, :].rearrange("p b (h t) -> p b h t", h=4), "ca_ptc")
                        wait("ca_o", qt + 1)
                        copy(H[:, :, qt * P:(qt + 1) * P].rearrange("p (a d) t -> p a d t", a=2),
                             ps[:, 6:8, :].rearrange("p a (d t) -> p a d t", d=4), "ca_oc")
                    for g in range(NB // 2):
                        wait("ca_max_s", g + 1)
                        for b in (2 * g, 2 * g + 1):
                            step(A(c_ps[:, b, :], ps[:, g, b % 2 * MEM:(b % 2 + 1) * MEM], ACT.Exp, bias=c_nm[:, b:b + 1],
                                   scale=SCALE_CA, accum_out=c_sum[:, b:b + 1]), "ca_p_s" if b % 2 else None)
                    wait("ca_o_s", NB)
                    copy(c_po, ps[:, 0, 0:256], "ca_po")
                    wait("ca_ot")
                    copy(H[:, :, TP:N].rearrange("p (h j) t -> p j h t", j=2),
                         ps[:, 1, 0:256].rearrange("p (j h t) -> p j h t", j=2, h=4), "ca_oc_s")
                    into("ca_o", O, "post_ca")
                    rms("post_ca")

                    squares("pre_ffn", X, H, after="post_ca_done")
                    rms("pre_ffn")
                    wait("conv_halo", 2)
                    a_tiles = tiles_of("ffn_a")
                    for k in range(KF + 1):
                        if k < KF:
                            g, t = a_tiles[k]
                            tile_ready(g)
                            if k >= 2:
                                wait("conv_state", k - 1)
                            step(A(f_a[:, k % 2, 2:2 + TP], ps[:, g % GEMM_BANKS, 0:TP], ACT.Copy))
                            copy(per_batch(f_a[:, k % 2, 2 + TP:EXC], 2 + TS)[:, :, 2:2 + TS],
                                 per_batch(ps[:, g % GEMM_BANKS, TP:N], TS), "bank_read_act")
                        if k >= 1:
                            wait("conv", k)
                            step(A(f_c[:, (k - 1) % 2, :], f_c[:, (k - 1) % 2, :], ACT.Gelu), "gelu")
                    into("down", O, "post_ffn")
                    rms("post_ffn")
                    for k in range(KD):
                        wait("post_ffn_done", k + 1)
                        step(A(SQ[:, k, :], X[:, k, :], ACT.Square), "next_sq")
                    rms("next")

                @block.vector
                def _(dve):
                    step = Steps(dve, "dve_step")
                    v = nc.vector

                    def wait(name, n=1):
                        dve.wait_ge(*at(name, n))

                    def tt(out, a, b, op, signal=None):
                        step(v.tensor_tensor(out, a, b, op), signal)

                    def ts(out, a, s1, s2, op0, op1=None, signal=None):
                        if op1 is None:
                            step(v.tensor_scalar(out, a, s1, None, op0), signal)
                        else:
                            step(v.tensor_scalar(out, a, s1, s2, op0, op1), signal)

                    def stt(out, a, s, b, op0, op1, signal=None):
                        step(v.scalar_tensor_tensor(out, a, s, b, op0, op1), signal)

                    def copy(out, in_, signal=None):
                        step(v.tensor_copy(out, in_), signal)

                    def fill(out, value, signal=None):
                        step(v.memset(out, value), signal)

                    MUL, ADD, SUB, MAX, MIN = ALU.mult, ALU.add, ALU.subtract, ALU.max, ALU.min

                    def normed(name, dst, rs=RS):
                        wait(name + "_rstd")
                        step(v.reciprocal(rs, rs))
                        for k in range(KD):
                            tt(dst[:, k, :], dst[:, k, :], rs, MUL, name + "_done")

                    def residual(name):
                        wait(name + "_rstd")
                        step(v.reciprocal(RS[:, :], RS[:, :]))
                        for k in range(KD):
                            tt(O[:, k, :], O[:, k, :], RS[:, :], MUL)
                            tt(X[:, k, :], X[:, k, :], O[:, k, :], ADD, name + "_done")

                    wait("load_vec", 16)
                    step(v.reciprocal(RS, RS))
                    for k in range(KD):
                        wait("pre_mix_gained", k + 1)
                        tt(H[:, k, :], H[:, k, :], RS, MUL, "pre_mix_done")
                    wait("load_shift", 16)
                    fill(RE[:, :, 0:1], 0.0)
                    copy(RE[:, :, 1 + TP:EXT].rearrange("p a (b t) -> p a b t", t=1 + TS)[:, :, :, 0], r_hs[:, :, :], "halo")

                    wait("gla_z")
                    ts(g_t1, ps[:, 4, 0:N], V("gla_b"), None, ADD)
                    stt(g_t2, g_t1, -1.0, g_t1, MUL, MIN, "gla_abs")
                    wait("gla_log")
                    stt(g_t2, g_t1, 0.0, g_t3, MIN, SUB)
                    step(v.tensor_tensor_scan(g_cum, C("reset", N), g_t2, 0.0, MUL, ADD))
                    tt(chunks(g_t2), bc(chunks(g_cum)[:, :, CH - 1:CH], [P, NCH, CH]), chunks(g_cum), SUB)
                    tt(smp(g_t2), bc(smp(g_cum)[:, :, TS - 1:TS], [P, NB, TS]), smp(g_cum), SUB, "gla_cum")
                    wait("gla_exp")
                    stt(g_q, PR[:, GQ, :], 32.0 ** -0.5, g_eb, MUL, MUL)
                    tt(g_k, PR[:, GK, :], g_enb, MUL)
                    tt(g_ke, PR[:, GK, :], g_ebe, MUL, "gla_k")
                    read_done(dve, "in_tok")
                    tt(g_vb.rearrange("p h (b v) -> p h b v", b=NB)[0:NS],
                       VT[0:NS, 2, 0:256].rearrange("p (h o v) -> p h o v", h=4, o=1).broadcast_to([NS, 4, NB, 64]),
                       C("batch", NB, NS).rearrange("p (o b u) -> p o b u", o=1, u=1).broadcast_to([NS, 4, NB, 64]), MUL)
                    wait("gla_turned")
                    copy(g_ktok[:, 0:2, :], ps[:, 3, 0:2 * P].rearrange("p (a b) -> p a b", a=2))
                    copy(g_ktok[0:NS, 2, :], ps[0:NS, 3, 2 * P:3 * P], "gla_kt")
                    wait("gla_att")
                    for i, (c0, n) in enumerate(TT):
                        m = C("upper", P) if i < 2 else C("upper_s", NS, NS)
                        tt(g_att[0:n, i, 0:4 * n].rearrange("p (h t) -> p h t", h=4),
                           ps[0:n, i, 0:4 * n].rearrange("p (h t) -> p h t", h=4),
                           m.rearrange("p (o t) -> p o t", o=1).broadcast_to([n, 4, n]), MUL, "gla_attm" if i == 2 else None)
                    wait("gla_ds")
                    wait("load_gla", 16)
                    copy(g_st[:, 1, :], ps[:, 4, 0:64])
                    for c in range(1, NCH):
                        e = (c + 1) * CH - 1
                        stt(g_st[:, c + 1, :], g_st[:, c, :], g_eb[:, e:e + 1], ps[:, 4, c * 64:(c + 1) * 64], MUL, ADD)
                    tt(g_s1, g_s0, bc(smp(g_eb)[:, :, TS - 1:TS], [P, NB, 64]), MUL)
                    tt(g_s1, g_s1, ps[:, 5, :].rearrange("p (b v) -> p b v", b=NB), ADD, "gla_state")
                    wait("gla_r")
                    stt(O[:, 0:2, :], ps[:, 6:8, 0:N], V("gla_norm"), g_ra, MUL, MUL)
                    tt(O[:, 0:2, :], O[:, 0:2, :], PR[:, GR:GR + 2, :], MUL, "gla_done")

                    wait("mla_r")
                    wait("stores", 32)
                    for j in range(2):
                        stt(m_cqn[:, j, :], PR[:, CQ + j, :], V("norm_q", j), m_rr[:, 0, :], MUL, MUL, "mla_cq" if j else None)
                    stt(m_ck, PR[:, CKV, :], V("norm_kv"), m_rr[:, 1, :], MUL, MUL)
                    tt(m_ta[0:32, :], PR[64:96, MIX1, :], C("cos", N, 32, 64), MUL)
                    tt(m_tb[0:32, :], PR[96:128, MIX1, :], C("sin", N, 32, 96), MUL)
                    tt(m_kp[0:32, :], m_ta[0:32, :], m_tb[0:32, :], ADD)
                    for r in (32, 64, 96):
                        copy(m_kp[r:r + 32, :], m_kp[0:32, :], "mla_norm" if r == 96 else None)
                    wait("mla_q")
                    copy(m_qn, ps[:, 2:4, 0:N])
                    tt(m_ta, ps[:, 4, 0:N], C("cos", N), MUL)
                    tt(m_tb, ps[:, 5, 0:N], C("sin", N), MUL)
                    tt(m_qp, m_ta, m_tb, ADD)
                    copy(m_cktok[:, 0:2, :], ps[:, 6, 0:2 * P].rearrange("p (a b) -> p a b", a=2))
                    copy(m_cktok[0:NS, 2, :], ps[0:NS, 6, 2 * P:3 * P], "mla_qn")
                    qpz = m_qpz.rearrange("p (b k q) -> p b k q", b=NB, k=4)
                    fill(m_qz, 0.0)
                    fill(m_qpz, 0.0)
                    for h in range(4):
                        copy(qpz[0:32, :, 0, TS * h:TS * h + TS], smp(m_qp)[32 * h:32 * h + 32])
                    for k in range(1, 4):
                        copy(qpz[32 * k:32 * k + 32, :, k, :], qpz[0:32, :, 0, :])
                    wait("mla_qlc")
                    for h in range(4):
                        copy(m_qz[:, 0:64 * NB].rearrange("p (b z) -> p b z", b=NB)[:, :, 48 + TS * h:48 + TS * h + TS],
                             smp(m_ql[:, h, :]), "mla_qs" if h == 3 else None)
                    for qt in range(2):
                        nk = (qt + 1) * P
                        wait("mla_s", qt + 1)
                        step(v.tensor_reduce(m_mx[qt].rearrange("p (a b) -> p a b", a=2),
                                             ps[:, 2 * qt:2 * qt + 2, :].rearrange("p a (b s) -> p a b s", b=2)[:, :, :, 0:nk],
                                             AX.X, MAX))
                        ts(m_nm[qt], m_mx[qt], -SCALE_MLA, None, MUL, signal="mla_max")
                    for qt in range(2):
                        nk = (qt + 1) * P
                        wait("mla_p", qt + 1)
                        step(v.reciprocal(m_rec[qt], m_sum[qt]))
                        p = m_p[qt][:, :, 0:nk]
                        tt(p, p, m_rec[qt].rearrange("p (h o) -> p h o", o=1).broadcast_to([P, 4, nk]), MUL, "mla_pn")
                    def pack_rotated(b):
                        wait(f"kv_full{b % KV_SLOTS}", 16 * PAGES * (b // KV_SLOTS + 1))
                        if b >= 2:
                            wait("pages_turned", 5 * (b - 2) + 1)
                        copy(m_kr[b % 2].rearrange("p (g r) -> p g r", r=32), kv[b % KV_SLOTS][:, :, P:ROW], "rotated_packed")

                    pack_rotated(0)
                    pack_rotated(1)
                    ts(l_x[0:4, :], PR[0:4, MIX2, :], V("f_bias", 0, 4), None, ADD)
                    stt(l_t[0:4, :], l_x[0:4, :], -1.0, l_x[0:4, :], MUL, MIN, "ml_abs")
                    wait("mla_own")
                    copy(m_own, ps[:, 7, 0:P])
                    step(v.tensor_reduce(m_otop, ps[:, 7, 0:P].rearrange("p (g k) -> p g k", k=NS), AX.X, MAX), "mla_own_max")
                    fill(m_os, 0.0)
                    pack_rotated(2)
                    fill(l_fe[0:4, :], NEG)
                    fill(l_ie[0:4, :], 0.0)
                    ts(ext_prompt(l_ie[0:4]), PR[0:4, MIX1, 0:TP], V("i_bias", 0, 4), None, ADD)
                    ts(ext_sample(l_ie[0:4]), smp(PR[0:4, MIX1, :]), V("i_bias", 0, 4), None, ADD)
                    wait("load_m0", 16)
                    copy(per_batch(l_ie[0:4, 1 + TP:EXT], 1 + TS)[:, :, 0:1], l_m0[0:4, :].rearrange("p (b o) -> p b o", o=1))
                    wait("ml_log")
                    stt(l_x[0:4, :], l_x[0:4, :], 0.0, l_t[0:4, :], MIN, SUB)
                    copy(ext_prompt(l_fe[0:4]), l_x[0:4, 0:TP])
                    copy(ext_sample(l_fe[0:4]), smp(l_x[0:4]))
                    step(v.tensor_tensor_scan(l_me[0:4, :], l_fe[0:4, :], l_ie[0:4, :], 0.0, ADD, MAX))
                    step(v.tensor_tensor_scan(l_b[0:4, :], C("reset_m", N, 4), l_x[0:4, :], 0.0, MUL, ADD))
                    tt(l_nm[0:4, 0:TP], l_b[0:4, 0:TP], ext_prompt(l_me[0:4]), SUB)
                    tt(smp(l_nm[0:4]), smp(l_b[0:4]), ext_sample(l_me[0:4]), SUB)
                    tt(l_g[0:4, 0:TP], ext_prompt(l_ie[0:4]), l_b[0:4, 0:TP], SUB)
                    tt(smp(l_g[0:4]), ext_sample(l_ie[0:4]), smp(l_b[0:4]), SUB)
                    rows = l_rows[0:4]
                    tt(rows[:, L_EM:L_EM + N], l_nm[0:4, :], l_b[0:4, :], SUB)
                    m0 = l_m0[0:4, :].rearrange("p (b o) -> p b o", o=1)
                    tt(per_batch(rows[:, L_WI:L_WI + NS], TS), smp(l_nm[0:4]), bc(m0, [4, NB, TS]), ADD)
                    ts(rows[:, L_WE:L_WE + TP], l_g[0:4, 0:TP], l_nm[0:4, TP - 1:TP], None, ADD)
                    nm_end = smp(l_nm[0:4])[:, :, TS - 1:TS]
                    tt(per_batch(rows[:, L_WE + TP:L_WE + N], TS), smp(l_g[0:4]), bc(nm_end, [4, NB, TS]), ADD)
                    copy(l_mo[0:4, 0:1], l_me[0:4, TP:TP + 1])
                    copy(l_mo[0:4, 1:1 + NB].rearrange("p (b o) -> p b o", o=1), ext_sample(l_me[0:4])[:, :, TS - 1:TS])
                    tt(rows[:, L_SO:L_SO + NB].rearrange("p (b o) -> p b o", o=1), m0, nm_end, ADD, "ml_rows")
                    for g in range(NB // 2):
                        wait("page_scores", 8 * g + 8)
                        step(v.tensor_reduce(m_top[:, g:g + 1], ps[:, g, :], AX.X, MAX))
                        tt(m_top[:, g:g + 1], m_top[:, g:g + 1], m_otop[:, g:g + 1], MAX, "mla_top")
                        wait("mla_topt", g + 1)
                        step(v.tensor_reduce(m_tops.rearrange("p (f q) -> p f q", f=2),
                                             ps[0:1, 7, 0:P].rearrange("p (f k q) -> p f q k", f=2, k=4), AX.X, MAX))
                        copy(m_row.rearrange("p (f k q) -> p f k q", f=2, k=4),
                             m_tops.rearrange("p (f o q) -> p f o q", f=2, o=1).broadcast_to([1, 2, 4, 16]), "mla_max_s")
                        wait("mla_maxt", g + 1)
                        ts(m_top[:, g:g + 1], ps[:, 7, P:P + 1], -SCALE_MLA, None, MUL, signal="mla_nm")
                        wait("mla_pt_s", g + 1)
                        if g:
                            wait("mla_pv", 2 * g)
                        copy(m_pot, ps[0:NS, 7, 2 * P:3 * P])
                        copy(m_pts, ps[:, 6, :].rearrange("p (i r) -> p i r", i=4), "mla_pts")
                        if 2 * g + 3 < NB:
                            pack_rotated(2 * g + 3)
                        wait("mla_pv", 2 * g + 2)
                        step(v.reciprocal(m_recs, ps[0:64, 7, 384:385]))
                        ts(m_os[0:16], ps[0:16, 7, P:2 * P], m_recs[0:16], None, MUL)
                        ts(m_os[32:48], ps[32:48, 7, P:2 * P], m_recs[32:48], None, MUL, signal="mla_os")
                        wait("mla_ot", g + 1)
                        j = TP + 2 * TS * g
                        copy(m_ol[:, :, j:j + 2 * TS].rearrange("p h (f t) -> p h f t", f=2),
                             ps[:, 7, 0:64].rearrange("p (f r) -> p f r", f=2)[:, :, 0:16].rearrange("p f (h t) -> p h f t", h=4),
                             "mla_ols")
                        if 2 * g + 4 < NB:
                            pack_rotated(2 * g + 4)

                    wait("mla_done")
                    wait("ml_turned")
                    copy(l_gw[:, 0:16], ps[:, 0, 0:16])
                    copy(l_gw[0:NS, 16:24], ps[0:NS, 0, 16:24], "ml_gw")
                    for i, (c0, n) in enumerate(TT):
                        c = i % 2 * 256
                        tt(l_kw[0:n, i, :].rearrange("p (h k) -> p h k", h=4),
                           ps[0:n, 4 + i // 2, c:c + 256].rearrange("p (h k) -> p h k", h=4),
                           l_gw[0:n, i * 8 + 4:i * 8 + 8].rearrange("p (h o) -> p h o", o=1).broadcast_to([n, 4, 64]), MUL)
                    stt(l_qw, ps[:, 3, 0:2 * NS].rearrange("p (a b) -> p a b", a=2), 0.125, PR[:, MQ:MQ + 2, TP:N], MUL, MUL)
                    copy(l_so, ps[:, 3, 64:64 + 2 * NB].rearrange("p (a b) -> p a b", a=2), "ml_k")
                    wait("load_ml", 32)
                    tt(l_vb.rearrange("p h (b v) -> p h b v", b=NB)[0:NS],
                       VT[0:NS, 2, 256:512].rearrange("p (h o v) -> p h o v", h=4, o=1).broadcast_to([NS, 4, NB, 64]),
                       C("batch", NB, NS).rearrange("p (o b u) -> p o b u", o=1, u=1).broadcast_to([NS, 4, NB, 64]), MUL)
                    copy(l_nbc, l_n0.rearrange("p a (b o) -> p a b o", o=1).broadcast_to([P, 2, NB, 64]))
                    tt(r_d, RE[:, :, 0:EXT - 1], RE[:, :, 1:EXT], SUB)
                    for h in range(4):
                        wait("ml_e", h + 1)
                        qk = ps[:, 6 + h % 2, :]
                        stt(l_w[:, h, 0:384], qk[:, 0:384], 0.125, l_w[:, h, 0:384], MUL, MUL)
                        stt(l_w[0:NS, h, 384:416], qk[0:NS, 384:416], 0.125, l_w[0:NS, h, 384:416], MUL, MUL, "ml_w")
                        for j in (2 * h, 2 * h + 1):
                            stt(SQ[:, j, 0:TP], r_d[:, j, 0:TP], V("mu", j), ext_prompt(RE[:, j, :]), MUL, ADD)
                            stt(smp(SQ[:, j, :]), per_batch(r_d[:, j, TP:EXT - 1], 1 + TS)[:, :, 1:1 + TS], V("mu", j),
                                ext_sample(RE[:, j, :]), MUL, ADD, "rw_pm" if j == 7 else None)
                    copy(l_h, ps[:, 1:3, 0:N], "ml_em")
                    wait("ml_num")
                    copy(l_den, ps[:, 6:8, 0:N])
                    stt(l_den, l_den, -1.0, l_den, MUL, MAX)
                    tt(l_den, l_den, l_h, MAX)
                    step(v.reciprocal(l_den, l_den))
                    tt(l_h, ps[:, 4:6, 0:N], l_den, MUL, "ml_h")
                    wait("ml_mean")
                    stt(l_h, ps[:, 4:6, 0:N], -1.0 / 64, l_h, MUL, ADD, "ml_c")
                    wait("ml_ds")
                    for hp in range(2):
                        c0 = l_c0[:, hp, :].rearrange("p (b v) -> p b v", b=NB)
                        tt(c0, c0, l_so[:, hp, :].rearrange("p (b o) -> p b o", o=1).broadcast_to([P, NB, 64]), MUL)
                        tt(l_c0[:, hp, :], l_c0[:, hp, :], ps[:, 1 + hp, :], ADD)
                    tt(l_n0, l_n0, l_so, MUL)
                    tt(l_n0, l_n0, ps[:, 3, 136:136 + 2 * NB].rearrange("p (a b) -> p a b", a=2), ADD)
                    copy(l_cp, ps[:, 3, 0:P].rearrange("p (a b) -> p a b", a=2))
                    copy(l_np, ps[:, 3, P:P + 2], "ml_state")
                    rr, rk, rv = SQ[:, 0:2, :], SQ[:, 2:4, :], SQ[:, 4:6, :]
                    for hp in range(2):
                        ts(r_kk[:, hp, :], rk[:, hp, :], V("k_k", hp), None, MUL)
                    tt(r_t, r_kk, r_kk, MUL, "rw_kk")
                    wait("ml_r")
                    for hp in range(2):
                        stt(l_h[:, hp, :], l_h[:, hp, :], V("ml_norm", hp), l_r[:, hp, :], MUL, MUL)
                    tt(O[:, 6:8, :], l_h, PR[:, MO:MO + 2, :], MUL, "ml_done")

                    wait("rw_kks")
                    ts(r_t, ps[:, 6:8, 0:N], 1e-24, 2.0 ** 20, MAX, MUL, "rw_clamped")
                    wait("rw_sig")
                    for hp in range(2):
                        step(v.tensor_tensor_scan(r_cs[:, hp, :], C("reset", N), r_s[:, hp, :], 0.0, MUL, ADD))
                    tt(r_csx, r_cs, r_s, SUB)
                    for hp in range(2):
                        a, b = r_cse[:, hp, :], r_cs[:, hp, :]
                        tt(chunks(a), bc(chunks(b)[:, :, CH - 1:CH], [P, NCH, CH]), chunks(b), SUB)
                        tt(smp(a), bc(smp(b)[:, :, TS - 1:TS], [P, NB, TS]), smp(b), SUB, "rw_cum" if hp == 1 else None)
                    wait("rw_inv")
                    tt(r_kk, r_kk, r_t, MUL)
                    tt(r_ka, r_kk, r_a, MUL)
                    for hp in range(2):
                        ts(r_t[:, hp, :], r_a[:, hp, :], 1.0, V("k_a", hp), SUB, MUL)
                    stt(r_rk, r_t, 1.0, rk, ADD, MUL)
                    for hp in range(2):
                        stt(r_bo[:, hp, :], rr[:, hp, :], V("r_k", hp), r_rk[:, hp, :], MUL, MUL)
                    wait("rw_exp")
                    tt(r_al, r_kk, r_csx, MUL)
                    stt(r_be, r_ka, -1.0, r_cs, MUL, MUL)
                    stt(r_kk, r_ka, -1.0, r_cse, MUL, MUL)
                    tt(r_csx, r_rk, r_cs, MUL)
                    tt(r_cs, r_rk, r_cse, MUL)
                    copy(r_rk, r_csx)
                    copy(r_s, r_rh)
                    wait("stores_ml", 80)
                    copy(r_sh[:, :, 0:1], RE[:, :, TP:TP + 1])
                    copy(r_sh[:, :, 1:1 + NB], RE[:, :, 1 + TP:EXT].rearrange("p a (b t) -> p a b t", t=1 + TS)[:, :, :, TS])
                    tt(r_rh, rr, r_rh, MUL, "rw_vec")
                    wait("rw_bonus")
                    tt(r_bo, ps[:, 6:8, 0:N], rv, MUL, "rw_bo")
                    def bank(i, j):
                        n = TT[i][1]
                        return ps[0:n, j, 0:4 * n].rearrange("p (h t) -> p h t", h=4)

                    def mask(i, name, j=0):
                        n, o = TT[i][1], CON[name] + j * P
                        return con[0:n, o:o + n].rearrange("p (o t) -> p o t", o=1).broadcast_to([n, 4, n])

                    def tile_of(a, i):
                        n = TT[i][1]
                        return a[i][0:n, :, 0:n]

                    def rw_masks(i):
                        tm, tr, ato = tile_of(r_tm, i), tile_of(r_tt, i), tile_of(r_at, i)
                        wait("rw_pair", i + 1)
                        sfx = "" if i < 2 else "_s"
                        tt(ato, bank(i, 0), mask(i, "strict" + sfx), MUL)
                        tt(tm, bank(i, 1), mask(i, "level0"), MUL)
                        tt(tile_of(r_bt, i), bank(i, 2), mask(i, "strict" + sfx), MUL)
                        tt(tile_of(r_rb, i), bank(i, 3), mask(i, "upper" + sfx), MUL)
                        tt(tile_of(r_rkm, i), bank(i, 4), mask(i, "upper" + sfx), MUL, "rw_pairm")
                        tt(tm, tm, mask(i, "ident"), ADD)
                        tt(tr, ato, mask(i, "level"), MUL)
                        tt(tr, tr, mask(i, "ident"), ADD)

                    def rw_offs(level):
                        j, i = RW_LEVELS[level]
                        tt(tile_of(r_off, i), tile_of(r_at, i), mask(i, "level", j), MUL, "rw_off")

                    def rw_adds(level):
                        j, i = RW_LEVELS[level]
                        wait("rw_y", level + 1)
                        tt(tile_of(r_tm, i), tile_of(r_tm, i), bank(i, RW_BANKS[i][1]), ADD)
                        tt(tile_of(r_tt, i), tile_of(r_tt, i), bank(i, RW_BANKS[i][2]), ADD, "rw_t")

                    rw_masks(0)
                    rw_masks(1)
                    rw_offs(0)
                    rw_offs(1)
                    for level in range(10):
                        rw_adds(level)
                        if level < 8:
                            rw_offs(level + 2)
                    for c in range(NCH):
                        e = (c + 1) * CH - 1
                        wait("rw_ds", c + 1)
                        for hp in range(2):
                            src = ps[:, 1, hp * 64:(hp + 1) * 64]
                            sig = "rw_st" if hp else None
                            if c:
                                stt(r_st[:, hp, :], r_st[:, hp, :], r_s[:, hp, e:e + 1], src, MUL, ADD, sig)
                            else:
                                copy(r_st[:, hp, :], src, sig)
                    rw_masks(2)
                    rw_offs(10)
                    rw_adds(10)

                    def spread(out, src, signal=None):
                        tt(out.rearrange("p h (b v) -> p h b v", b=NB)[0:NS],
                           src.rearrange("p (h o v) -> p h o v", h=4, o=1).broadcast_to([NS, 4, NB, 64]),
                           C("batch", NB, NS).rearrange("p (o b u) -> p o b u", o=1, u=1)
                           .broadcast_to([NS, 4, NB, 64]), MUL, signal)

                    wait("rw_tokc", 6)
                    spread(r_vb, r_tok[2][0:NS, 3, :])
                    wait("rw_utok")
                    spread(r_ub, r_u[0:NS, :], "rw_utc")
                    wait("rw_ds", 5)
                    for hp in range(2):
                        s0 = r_s0[:, hp, :].rearrange("p (b v) -> p b v", b=NB)
                        tt(s0, s0, bc(smp(r_s[:, hp, :])[:, :, TS - 1:TS], [P, NB, 64]), MUL)
                        tt(r_s0[:, hp, :], r_s0[:, hp, :], ps[:, 2 + hp, :], ADD, "rw_state" if hp else None)
                    wait("rw_mean")
                    stt(r_a, ps[:, 0:2, 0:N], -1.0 / 64, r_a, MUL, ADD, "rw_c")
                    wait("rw_r")
                    for hp in range(2):
                        stt(r_t[:, hp, :], r_a[:, hp, :], V("ln_w", hp), r_s[:, hp, :], MUL, MUL)
                        stt(r_t[:, hp, :], r_t[:, hp, :], V("ln_b", hp), r_bo[:, hp, :], ADD, ADD)
                    tt(O[:, 4:6, :], r_t, r_g, MUL, "rw_done")

                    for g, t in tiles_of("up"):
                        d, n = t[1]
                        wait("gemm_done", g + 1)
                        wait("bank_read_act", gate_read(d, n))
                        dst = PR[:, d, :] if n == 0 else RS[:, :]
                        gate = SQ[:, n, :] if d else first_gates[:, n, :]
                        tt(dst, ps[:, g % GEMM_BANKS, 0:N], gate, MUL, "bank_read_dve")
                        if n:
                            tt(PR[:, d, :], PR[:, d, :], RS[:, :], ADD, "mixed" if n == 3 else None)
                        if (d, n) == MEM_SUMS_AT:
                            normed("mem", c_mem, c_rs)

                    residual("post_mix")
                    normed("pre_ca", H)

                    for qt in range(2):
                        wait("ca_s", qt + 1)
                        q = slice(4 * qt, 4 * qt + 4)
                        step(v.tensor_reduce(c_mx[:, q], ps[:, 2 * qt:2 * qt + 2, :].rearrange("p a (b s) -> p (a b) s", b=2), AX.X, MAX))
                        ts(c_nm[:, q], c_mx[:, q], -SCALE_CA, None, MUL, signal="ca_max")
                    for qt in range(2):
                        wait("ca_p", qt + 1)
                        q = slice(4 * qt, 4 * qt + 4)
                        step(v.reciprocal(c_rec[:, q], c_sum[:, q]))
                        tt(c_p[qt], c_p[qt], c_rec[:, q].rearrange("p (h o) -> p h o", o=1).broadcast_to([P, 4, MEM]), MUL, "ca_pn")
                    for g in range(NB // 2):
                        b2 = slice(2 * g, 2 * g + 2)
                        wait("ca_ss_s", 2 * g + 2)
                        step(v.tensor_reduce(c_mx[:, b2], ps[:, g, :].rearrange("p (b s) -> p b s", b=2), AX.X, MAX))
                        ts(c_nm[:, b2], c_mx[:, b2], -SCALE_CA, None, MUL, signal="ca_max_s")
                        wait("ca_p_s", g + 1)
                        step(v.reciprocal(c_rec[:, b2], c_sum[:, b2]))
                        tt(c_rec[:, b2], c_rec[:, b2], C("mem_own", NB)[:, b2], MUL)
                        tt(c_ps[:, b2, :], c_ps[:, b2, :], c_rec[:, b2].rearrange("p (b o) -> p b o", o=1).broadcast_to([P, 2, MEM]),
                           MUL, "ca_pn_s")
                        wait("ca_pt_s", g + 1)
                        copy(c_pts[:, b2, :, :], ps[:, 4 + g, :].rearrange("p (b s r) -> p b s r", b=2, s=2), "ca_pts")
                    residual("post_ca")
                    normed("pre_ffn", H)

                    wait("load_conv", 16)
                    wait("ca_oc_s")
                    for i in range(2):
                        fill(f_a[:, i, 0:2], 0.0, "conv_halo")
                    g_tiles = tiles_of("ffn_g")
                    for k in range(KF + 1):
                        if k < KF:
                            a = f_a[:, k % 2, :]
                            copy(per_batch(a[:, 2 + TP:EXC], 2 + TS)[:, :, 0:2], per_batch(f_s[:, k, :], 2))
                            wait("bank_read_act", READ_NO[tiles_of("ffn_a")[k][0]])
                            c = f_c[:, k % 2, :]
                            w = [V("conv_w", 3 * k + j) for j in range(3)]
                            ts(c, a[:, 0:EXC - 2], w[0], V("conv_b", k), MUL, ADD)
                            stt(c, a[:, 1:EXC - 1], w[1], c, MUL, ADD)
                            stt(c, a[:, 2:EXC], w[2], c, MUL, ADD, "conv")
                            copy(f_o[:, k, 0:2], a[:, TP:TP + 2])
                            copy(per_batch(f_o[:, k, 2:2 + 2 * NB], 2), per_batch(a[:, 2 + TP:EXC], 2 + TS)[:, :, TS:TS + 2],
                                 "conv_state")
                        if k >= 1:
                            j = k - 1
                            g, t = g_tiles[j]
                            wait("gelu", k)
                            wait("gemm_done", g + 1)
                            c, src = f_c[:, j % 2, :], ps[:, g % GEMM_BANKS, :]
                            tt(f_f[:, j, 0:TP], c[:, 0:TP], src[:, 0:TP], MUL)
                            tt(smp(f_f[:, j, :]), per_batch(c[:, TP:EXC - 2], 2 + TS)[:, :, 2:2 + TS],
                               per_batch(src[:, TP:N], TS), MUL, "bank_read_dve")
                    residual("post_ffn")

            with nc.Block() as block:
                @block.gpsimd
                def _(pool):
                    pool.dma_reset()
                    for name in sorted(sems):
                        if name != "load_once":
                            pool.sem_clear(sems[name])

        with nc.Block() as block:
            @block.sync
            def _(sp):
                sp.dma_start(t_out["y"], X[:, :, :]).then_inc(S("store_y"), 16)
                sp.wait_ge(S("store_y"), 16)


OUT = {
    "y": (P, KD, N), "ckv": (L, P, N), "kpe": (L, 32, N), "mem_kt": (L, P, KD, MEM), "mem_v": (L, P, 2, D),
    "gla_p": (L, P, 64), "gla_s": (L, P, NB, 64), "rwkv_p": (L, P, 2, 64), "rwkv_s": (L, P, 2, NB * 64),
    "shift_ps": (L, P, 8, 1 + NB), "ml_c_p": (L, P, 2, 64), "ml_c_s": (L, P, 2, NB * 64), "ml_n_p": (L, P, 2),
    "ml_n_s": (L, P, 2, NB), "ml_m_ps": (L, 4, 1 + NB), "conv_ps": (L, P, KF, 2 * (1 + NB)),
}


def constants():
    c = np.zeros((P, NCON), np.float32)

    def put(name, a):
        c[:a.shape[0], CON[name]:CON[name] + a.shape[1]] = a

    i = np.arange(P)
    row, col = i[:, None], i[None, :]
    put("ident", np.eye(P))
    put("ones", np.ones((P, P)))
    put("blk64", (row // 64 == col // 64) * 1.0)
    same, r4, c4 = row // CH == col // CH, row[:NS], col[:, :NS]
    put("upper", (same & (row <= col)) * 1.0)
    put("strict", (same & (row < col)) * 1.0)
    same4 = r4 // TS == c4 // TS
    put("upper_s", (same4 & (r4 <= c4)) * 1.0)
    put("strict_s", (same4 & (r4 < c4)) * 1.0)
    for j in range(6):
        s = 1 << j
        later = (row // (2 * s) == col // (2 * s)) & (row // s % 2 == 0) & (col // s % 2 == 1)
        c[:, CON["level"] + j * P:CON["level"] + (j + 1) * P] = later
        if j == 0:
            put("level0", later.T * 1.0)
    put("bias_tok", np.where(col <= row, 0.0, NEG))
    m = np.zeros((P, 416))
    m[:, 0:128] = m[:, 256:384] = np.where(row <= col, 0.0, NEG)
    m[:NS, 384:416] = np.where(same4 & (r4 <= c4), 0.0, NEG)
    put("bias_m", m)
    half, part, tok = row // 64, row // 16 % 4, row % TS
    group, key = np.arange(P)[None, :] // NS, np.arange(P)[None, :] % NS
    put("bias_own", np.where((part == 0) & (key // TS == 2 * group + half) & (key % TS <= tok), 0.0, NEG))
    col = np.arange(64)[None, :]
    put("sum_own", ((half == col // 32) & (row % 16 == col % 16)) * 1.0)
    put("mem_own", (row % NS // TS == np.arange(NB)[None, :]) * 1.0)
    for h in range(4):
        c[h, CON["sel_h"] + h * P:CON["sel_h"] + (h + 1) * P] = 1
        at = CON["sel_p"] + h // 2 * P + h % 2 * 64
        c[h, at:at + 64] = 1
    put("batch", (np.arange(NS)[:, None] // TS == np.arange(NB)[None, :]) * 1.0)
    half = 16
    freq = (np.float32(10000.0) ** (-np.arange(half, dtype=np.float32) / np.float32(half))).astype(np.float32)
    pos = np.concatenate([np.arange(TP), PAGES * PAGE + np.arange(NS) % TS]).astype(np.float32)
    ang = (pos[None, :] * freq[:, None]).astype(np.float32).astype(np.float64)
    put("cos", np.tile(np.cos(ang), (8, 1)))
    put("sin", np.tile(np.concatenate([-np.sin(ang), np.sin(ang)]), (4, 1)))
    first = np.r_[np.arange(TP) % CH == 0, np.arange(NS) % TS == 0]
    put("reset", np.tile(1.0 - first, (P, 1)))
    first[1:TP] = False
    put("reset_m", np.tile(1.0 - first, (P, 1)))
    for name, value in (("eps", 1e-6), ("eps_r", 64e-5), ("one", 1.0), ("kk_b", 10 * np.log(2.0))):
        put(name, np.full((P, 1), value))
    return c


def col(a, n):
    return np.moveaxis(a.reshape(a.shape[:-1] + (n, P)), -2, -1)


def blocks(w, order="j"):
    k, m = w.shape
    return w.reshape(k // P, P, m // P, P).transpose(2, 0, 1, 3).reshape(-1, P, P)


def wide(w):
    k, m = w.shape
    return w.reshape(k // P, P, m // 512, 4, P).transpose(2, 0, 3, 1, 4).reshape(-1, P, P)


def stream(i, l):
    w = i["w_in"][l]
    z = lambda n: np.zeros((D, n), np.float32)
    o_mla, o_rw, o_ml, o_g = 784, 1200, 2224, 3256
    kr = w[:, o_mla + 384:o_mla + 416]
    mix1 = np.concatenate([w[:, o_ml + 768:o_ml + 772], z(28), w[:, 512:528], z(16), kr, kr[:, 16:], kr[:, :16]], 1)
    mix2 = np.concatenate([w[:, o_ml + 772:o_ml + 776], z(124)], 1)
    feat = np.concatenate([w[:, 0:256], w[:, 528:784], w[:, o_mla:o_mla + 384], mix1, mix2, w[:, o_ml:o_ml + 512],
                           w[:, o_ml + 776:o_ml + 1032], w[:, o_rw:o_rw + 1024]], 1)
    tok = np.concatenate([w[:, 256:512], w[:, o_ml + 512:o_ml + 768]], 1)
    parts = [blocks(feat)]
    parts.append(np.zeros((-len(parts[0]) % SLOT, P, P), np.float32))
    parts.append(wide(tok))
    gate = blocks(w[:, o_g:]).reshape(4, KD, KD, P, P)
    up = np.stack([blocks(i["w_branch"][l, n]).reshape(KD, 2, P, P) for n in range(4)])
    parts += [(gate if stage == "gate" else up)[n, d] for stage, d, n in MIXING]
    mem_v = wide(i["ca_w_v"][l])
    parts += [blocks(i["ca_w_k"][l]), mem_v[:4 * KD], blocks(i["w_out"][l]), mem_v[4 * KD:], blocks(i["ca_w_q"][l]),
              blocks(i["ca_w_o"][l])]
    f = blocks(i["ffn_w_up"][l]).reshape(2, KF, KD, P, P)
    parts.append(f.transpose(1, 0, 2, 3, 4).reshape(-1, P, P))
    parts.append(blocks(i["ffn_w_down"][l]))
    s = np.concatenate(parts)
    assert len(s) == NBLOCK, (len(s), NBLOCK)
    s = np.concatenate([s, np.zeros((NSLOT * SLOT - NBLOCK, P, P), np.float32)])
    return s.reshape(NSLOT, SLOT, P, P).transpose(0, 2, 1, 3).reshape(NSLOT, P, SLOT * P)


def kernel(**inputs):
    import concourse.bacc as bacc
    from concourse.bass_utils import run_bass_kernel_spmd

    i = {k: np.asarray(a) for k, a in inputs.items()}
    f32 = np.float32
    a = {"const": constants()}
    x = np.concatenate([i["x_prompt"].reshape(TP, D), i["x_sample"].reshape(NS, D)])
    feat = lambda t: np.ascontiguousarray(t.T.reshape(-1, P, t.shape[0]).transpose(1, 0, 2))
    a["x"] = feat(x)
    a["mem"] = feat(i["mem_prompt"].reshape(MEM, D))
    a["pages"] = np.ascontiguousarray(i["page_table"].reshape(1, NB * PAGES).astype(np.int32))
    a["w"] = np.stack([stream(i, l) for l in range(L)])
    v = np.zeros((L, P, NVEC), f32)

    def vec(name, t):
        v[:, :t.shape[1], VEC[name]:VEC[name] + t.shape[2]] = t

    for name in ("pre_mix", "post_mix", "pre_ca", "post_ca", "pre_ffn", "post_ffn"):
        vec(name, col(i["norm_" + name], KD))
    vec("mem", col(i["ca_norm_mem"], KD))
    vec("mu", col(i["rwkv_mu"], 8))
    for name, src in (("w0", "rwkv_w0"), ("a0", "rwkv_a0"), ("k_k", "rwkv_k_k"), ("k_a", "rwkv_k_a"), ("ln_w", "rwkv_ln_w"),
                      ("ln_b", "rwkv_ln_b"), ("ml_norm", "mlstm_norm"), ("norm_q", "mla_norm_q")):
        vec(name, col(i[src], 2))
    vec("r_k", col(i["rwkv_r_k"].reshape(L, 256), 2))
    vec("gla_norm", np.tile(i["gla_norm"], (1, 2))[:, :, None])
    vec("gla_b", i["gla_b_gate"][:, :, None])
    vec("norm_kv", i["mla_norm_kv"][:, :, None])
    vec("conv_w", i["ffn_conv_w"].reshape(L, 3, KF, P).transpose(0, 3, 2, 1).reshape(L, P, 3 * KF))
    vec("conv_b", col(i["ffn_conv_b"], KF))
    vec("i_bias", i["mlstm_i_bias"][:, :, None])
    vec("f_bias", i["mlstm_f_bias"][:, :, None])
    a["vec"] = v
    m = np.zeros((L, P, NMAT), f32)

    def mat(name, t, r0=0):
        m[:, r0:r0 + t.shape[1], MAT[name]:MAT[name] + t.shape[2]] = t

    mat("gate2", i["gla_w_gate2"], GLO_AT)
    uq = i["mla_w_uq"].reshape(L, 256, 4, 96)
    rope = uq[..., 64:]
    swap = np.concatenate([rope[..., 16:], rope[..., :16]], -1)
    uq = np.concatenate([uq[..., :64].reshape(L, 256, 256), rope.reshape(L, 256, P), swap.reshape(L, 256, P)], -1)
    mat("uq", uq.reshape(L, 2, P, 512).transpose(0, 2, 1, 3).reshape(L, P, 1024))
    mat("uk", i["mla_w_uk"].transpose(0, 1, 3, 2).reshape(L, 2, P, P).transpose(0, 2, 1, 3).reshape(L, P, 256))
    mat("uv", i["mla_w_uv"].transpose(0, 2, 1, 3).reshape(L, P, 256))
    mat("wa", i["rwkv_w2"])
    mat("wa", i["rwkv_a2"], 64)
    mat("g2", i["rwkv_g2"])
    a["mat"] = m
    a["pool"] = np.concatenate([i["cache_ckv"], i["cache_kpe"]], -1)
    mk = i["cache_mem_k"].reshape(L, NB, MEM, KD, P)
    a["mem_k"] = np.ascontiguousarray(mk.transpose(0, 1, 4, 3, 2)).reshape(L, NB, P, 2 * D)
    mv = i["cache_mem_v"].reshape(L, NB, 2, P, D)
    a["mem_v"] = np.ascontiguousarray(mv.transpose(0, 1, 3, 2, 4)).reshape(L, NB, P, 2 * D)
    a["gla"] = np.ascontiguousarray(i["state_gla"].reshape(L, NB, P, 64).transpose(0, 2, 1, 3))
    two = lambda t: np.ascontiguousarray(t.reshape(L, NB, 2, P, 64).transpose(0, 3, 2, 1, 4).reshape(L, P, 2, NB * 64))
    a["rwkv"] = two(i["state_rwkv"].transpose(0, 1, 2, 4, 3))
    a["shift"] = np.ascontiguousarray(i["state_rwkv_shift"].reshape(L, NB, 8, P).transpose(0, 3, 2, 1))
    a["ml_c"] = two(i["state_mlstm_c"])
    a["ml_n"] = np.ascontiguousarray(i["state_mlstm_n"].reshape(L, NB, 2, P).transpose(0, 3, 2, 1))
    a["ml_m"] = np.ascontiguousarray(i["state_mlstm_m"].transpose(0, 2, 1))
    a["conv"] = np.ascontiguousarray(i["state_conv"].reshape(L, NB, 2, KF, P).transpose(0, 4, 3, 1, 2)
                                     .reshape(L, P, KF, 2 * NB))

    nc = bacc.Bacc("TRN2", target_bir_lowering=False, num_devices=1)
    t_in = {k: nc.dram_tensor("in_" + k, t.shape, mybir.dt.from_np(t.dtype), kind="ExternalInput").ap()
            for k, t in a.items()}
    t_out = {k: nc.dram_tensor("out_" + k, s, F32, kind="ExternalOutput").ap() for k, s in OUT.items()}
    program(nc, t_in, t_out)
    r = run_bass_kernel_spmd(nc, [{"in_" + k: t for k, t in a.items()}], core_ids=[0]).results[0]
    o = {k: r["out_" + k] for k in OUT}

    y = o["y"].transpose(2, 1, 0).reshape(N, D)
    tok = lambda t: t.transpose(0, 2, 1)
    ckv, kpe = tok(o["ckv"]), tok(o["kpe"])
    two = lambda t: t.reshape(L, 2, 64, 2, -1, 64).transpose(0, 4, 3, 1, 2, 5).reshape(L, -1, 4, 64, 64)
    shift = o["shift_ps"].transpose(0, 3, 2, 1).reshape(L, 1 + NB, D)
    rows = lambda t: t.transpose(0, 3, 2, 1).reshape(L, -1, 4, 64)
    conv = o["conv_ps"].transpose(0, 3, 2, 1).reshape(L, 1 + NB, 2, FF)
    mm = tok(o["ml_m_ps"])
    return (y[:TP].reshape(1, TP, D), y[TP:].reshape(NB, TS, D),
            ckv[:, :TP].reshape(L, 1, TP, P), kpe[:, :TP].reshape(L, 1, TP, 32),
            ckv[:, TP:].reshape(L, NB, TS, P), kpe[:, TP:].reshape(L, NB, TS, 32),
            o["mem_kt"].transpose(0, 3, 2, 1).reshape(L, 1, MEM, 4, 256),
            o["mem_v"].transpose(0, 2, 1, 3).reshape(L, 1, MEM, 4, 256),
            o["gla_p"].reshape(L, 1, 4, 32, 64), o["gla_s"].transpose(0, 2, 1, 3).reshape(L, NB, 4, 32, 64),
            two(o["rwkv_p"]).transpose(0, 1, 2, 4, 3), two(o["rwkv_s"]).transpose(0, 1, 2, 4, 3),
            shift[:, :1], shift[:, 1:],
            two(o["ml_c_p"]), two(o["ml_c_s"]),
            rows(o["ml_n_p"].reshape(L, P, 2, 1)), rows(o["ml_n_s"]),
            mm[:, :1], mm[:, 1:], conv[:, :1], conv[:, 1:])
```
